# Optimizing a Trainium2 kernel written in Bass

```python
import math, functools
import jax, jax.numpy as jnp
from jax import lax
import numpy as np

D_MODEL = 1024
BATCH = 1
SEQ = 512
DEPTH = 1
DEC_BATCH = 8
DEC_SEQ = 8
PAST_LEN = 2048
PAGE_SIZE = 128

MIX_WIDTH = D_MODEL
HEAD_DIM = 64
NSA_HEADS = 8
NSA_KV_HEADS = 2
NSA_GROUP = NSA_HEADS // NSA_KV_HEADS
NSA_WIDTH = NSA_HEADS * HEAD_DIM
KV_WIDTH = NSA_KV_HEADS * HEAD_DIM
CMP_BLOCK = 32
CMP_HIDDEN = 2 * HEAD_DIM
SEL_BLOCK = 64
TOP_N = 16
WINDOW = 512
Q_BLOCK = 128
N_BRANCH = 3
ATTN_SCALE = HEAD_DIM ** -0.5
MLSTM_HEADS = 4
MLSTM_WIDTH = MIX_WIDTH - NSA_WIDTH
MLSTM_DH = MLSTM_WIDTH // MLSTM_HEADS
MLSTM_CONV = 4
MLSTM_CHUNK = 64
D_FF = ((8 * D_MODEL // 3 + 127) // 128) * 128
FFN_CONV = 3
EPS = 1e-6
NEG_INF = -1e30
SEL_PRIORITY = 1e4
IN_SPLITS = (NSA_WIDTH, 2 * KV_WIDTH, 2 * KV_WIDTH, 2 * KV_WIDTH, NSA_HEADS * N_BRANCH,
             MLSTM_WIDTH, MLSTM_WIDTH, MLSTM_WIDTH, MLSTM_HEADS, MLSTM_HEADS)
N_IN = sum(IN_SPLITS)

kernel_name = 'hymba_mlstm_nsa_convffn_step'

def rmsnorm(x, g):
    xf = x.astype(jnp.float32)
    y = xf * lax.rsqrt(jnp.mean(xf * xf, axis=-1, keepdims=True) + EPS)
    return (y * g.astype(jnp.float32)).astype(x.dtype)

def causal_dwconv(x, buf, w):
    width, s = w.shape[0], x.shape[1]
    xx = jnp.concatenate([buf.astype(x.dtype), x], axis=1)
    y = xx[:, :s] * w[0]
    for j in range(1, width):
        y = y + xx[:, j:j + s] * w[j]
    return y, xx[:, s:]

def softmax_masked(scores, mask):
    return jax.nn.softmax(jnp.where(mask, scores.astype(jnp.float32), NEG_INF), axis=-1)

def mlstm_chunk_scan(q, k, v, ig, fg, C0, n0, m0):
    b, s, h, d = q.shape
    L = math.gcd(s, MLSTM_CHUNK)
    nc = s // L
    f32 = jnp.float32

    def chunks(a):
        a = a.astype(f32).reshape((b, nc, L) + a.shape[2:])
        return jnp.moveaxis(a, 1, 0)

    logf = jax.nn.log_sigmoid(fg.astype(f32))
    xs = (chunks(q), chunks(k.astype(f32) * d ** -0.5), chunks(v), chunks(ig), chunks(logf))
    tril = jnp.tril(jnp.ones((L, L), bool))[None, :, :, None]

    def step(carry, inp):
        C, n, m = carry
        qc, kc, vc, ic, lf = inp
        cum = jnp.cumsum(lf, axis=1)
        dmat = cum[:, :, None] - cum[:, None, :] + ic[:, None]
        dmat = jnp.where(tril, dmat, -jnp.inf)
        inter = cum + m[:, None]
        m_t = jnp.maximum(inter, jnp.max(dmat, axis=2))
        w = jnp.exp(dmat - m_t[:, :, None])
        sc = jnp.exp(inter - m_t)
        qk = jnp.einsum('bthd,bshd->btsh', qc, kc) * w
        num = jnp.einsum('btsh,bshe->bthe', qk, vc) + sc[..., None] * jnp.einsum('bhed,bthd->bthe', C, qc)
        den = jnp.sum(qk, axis=2) + sc * jnp.einsum('bhd,bthd->bth', n, qc)
        hc = num / jnp.maximum(jnp.abs(den), jnp.exp(-m_t))[..., None]
        m_new = m_t[:, -1]
        wl = jnp.exp(cum[:, -1:] - cum + ic - m_new[:, None])
        sl = jnp.exp(cum[:, -1] + m - m_new)
        C_new = sl[..., None, None] * C + jnp.einsum('bsh,bshe,bshd->bhed', wl, vc, kc)
        n_new = sl[..., None] * n + jnp.einsum('bsh,bshd->bhd', wl, kc)
        return (C_new, n_new, m_new), hc

    (C, n, m), hs = lax.scan(step, (C0.astype(f32), n0.astype(f32), m0.astype(f32)), xs)
    hs = jnp.moveaxis(hs, 0, 1).reshape(b, s, h, d)
    return hs, C, n, m

def mlstm_mixer(u, v, o, ig, fg, conv_buf, C0, n0, m0,
                w_conv, b_conv, w_q, w_k, b_ig, b_fg, g_head, skip):
    b, s, _ = u.shape
    uc, conv_new = causal_dwconv(u, conv_buf, w_conv)
    uc = jax.nn.silu(uc + b_conv)
    uh = uc.reshape(b, s, MLSTM_HEADS, MLSTM_DH)
    q = jnp.einsum('bshd,hde->bshe', uh, w_q)
    k = jnp.einsum('bshd,hde->bshe', uh, w_k)
    vh = v.reshape(b, s, MLSTM_HEADS, MLSTM_DH)
    hs, C, n, m = mlstm_chunk_scan(q, k, vh, ig + b_ig, fg + b_fg, C0, n0, m0)
    hn = rmsnorm(hs, g_head).reshape(b, s, MLSTM_WIDTH).astype(u.dtype)
    out = (hn + skip * uc) * jax.nn.sigmoid(o)
    return out, conv_new, C, n, m

def compress_blocks(rows, pe, w1, w2):
    b, l, h, d = rows.shape
    nb = l // CMP_BLOCK
    blk = rows[:, :nb * CMP_BLOCK].reshape(b, nb, CMP_BLOCK, h, d) + pe[:, None, :]
    blk = jnp.moveaxis(blk, 3, 2).reshape(b, nb, h, CMP_BLOCK * d)
    return jax.nn.silu(blk @ w1) @ w2

def cmp_branch(q, kc, vc, q_pos):
    nb = kc.shape[1]
    blk_end = (jnp.arange(nb) + 1) * CMP_BLOCK - 1
    avail = blk_end[None, :] <= q_pos[:, None]
    sc = jnp.einsum('btkgd,bnkd->btkgn', q, kc) * ATTN_SCALE
    p = softmax_masked(sc, avail[None, :, None, None, :])
    p = p * jnp.any(avail, axis=-1)[None, :, None, None, None]
    o = jnp.einsum('btkgn,bnkd->btkgd', p.astype(vc.dtype), vc)
    return o, jnp.sum(p, axis=3)

def select_blocks(imp, q_pos, n_sel):
    r = SEL_BLOCK // CMP_BLOCK
    imp = jnp.pad(imp, ((0, 0), (0, 0), (0, 0), (0, n_sel * r - imp.shape[-1])))
    score = imp.reshape(imp.shape[:3] + (n_sel, r)).sum(-1)
    j = jnp.arange(n_sel)[None, None, None, :]
    cur = (q_pos // SEL_BLOCK)[None, :, None, None]
    valid = j <= cur
    forced = (j == 0) | (j == cur) | (j == cur - 1)
    pri = jnp.where(valid, jnp.where(forced, SEL_PRIORITY, score), -SEL_PRIORITY)
    return lax.top_k(pri, min(TOP_N, n_sel))[1]

def sel_branch(q, kg, vg, idx, q_pos):
    b, t, h, kk, sb, d = kg.shape
    kpos = idx[..., None] * SEL_BLOCK + jnp.arange(SEL_BLOCK)
    mask = (kpos <= q_pos[None, :, None, None, None]).reshape(b, t, h, 1, kk * sb)
    sc = jnp.einsum('btkgd,btknsd->btkgns', q, kg) * ATTN_SCALE
    p = softmax_masked(sc.reshape(b, t, h, NSA_GROUP, kk * sb), mask)
    return jnp.einsum('btkgm,btkmd->btkgd', p.astype(vg.dtype), vg.reshape(b, t, h, kk * sb, d))

def win_branch(q, kw, vw, q_pos, k_pos):
    diff = q_pos[:, None] - k_pos[None, :]
    mask = (diff >= 0) & (diff < WINDOW) & (k_pos[None, :] >= 0)
    sc = jnp.einsum('btkgd,bnkd->btkgn', q, kw) * ATTN_SCALE
    p = softmax_masked(sc, mask[None, :, None, None, :])
    return jnp.einsum('btkgn,bnkd->btkgd', p.astype(vw.dtype), vw)

def nsa_prompt(q, kv_cmp, kv_sel, kv_win, pe, w1, w2):
    b, s = q.shape[:2]
    pos = jnp.arange(s)
    kc = compress_blocks(kv_cmp[:, :, 0], pe[0], w1[0], w2[0])
    vc = compress_blocks(kv_cmp[:, :, 1], pe[1], w1[1], w2[1])
    o_cmp, imp = cmp_branch(q, kc, vc, pos)
    n_sel = -(-s // SEL_BLOCK)
    idx = select_blocks(imp, pos, n_sel)
    sel_blk = jnp.pad(kv_sel, ((0, 0), (0, n_sel * SEL_BLOCK - s), (0, 0), (0, 0), (0, 0)))
    sel_blk = sel_blk.reshape(b, n_sel, SEL_BLOCK, 2, NSA_KV_HEADS, HEAD_DIM)
    win_pad = jnp.pad(kv_win, ((0, 0), (WINDOW, 0), (0, 0), (0, 0), (0, 0)))
    bi = jnp.arange(b)[:, None, None, None]
    hi = jnp.arange(NSA_KV_HEADS)[None, None, :, None]

    def q_block(start):
        qb = lax.dynamic_slice_in_dim(q, start, Q_BLOCK, axis=1)
        ib = lax.dynamic_slice_in_dim(idx, start, Q_BLOCK, axis=1)
        pb = start + jnp.arange(Q_BLOCK)
        g = sel_blk[bi, ib, :, :, hi]
        o_s = sel_branch(qb, g[..., 0, :], g[..., 1, :], ib, pb)
        wb = lax.dynamic_slice_in_dim(win_pad, start, WINDOW + Q_BLOCK, axis=1)
        kp = start - WINDOW + jnp.arange(WINDOW + Q_BLOCK)
        o_w = win_branch(qb, wb[:, :, 0], wb[:, :, 1], pb, kp)
        return o_s, o_w

    o_sel, o_win = lax.map(q_block, jnp.arange(0, s, Q_BLOCK))
    o_sel = jnp.moveaxis(o_sel, 0, 1).reshape(q.shape)
    o_win = jnp.moveaxis(o_win, 0, 1).reshape(q.shape)
    return o_cmp, o_sel, o_win, kv_cmp, kv_sel, kv_win[:, s - min(WINDOW, s):]

def nsa_sample(q, kv_cmp, kv_sel, kv_win, pool_cmp, pool_sel, win_buf, page_table, pe, w1, w2):
    b, s = q.shape[:2]
    past = page_table.shape[1] * PAGE_SIZE
    pos = past + jnp.arange(s)
    past_cmp = pool_cmp[page_table].reshape(b, past, 2, NSA_KV_HEADS, HEAD_DIM)
    kc = jnp.concatenate([compress_blocks(past_cmp[:, :, 0], pe[0], w1[0], w2[0]),
                          compress_blocks(kv_cmp[:, :, 0], pe[0], w1[0], w2[0])], axis=1)
    vc = jnp.concatenate([compress_blocks(past_cmp[:, :, 1], pe[1], w1[1], w2[1]),
                          compress_blocks(kv_cmp[:, :, 1], pe[1], w1[1], w2[1])], axis=1)
    o_cmp, imp = cmp_branch(q, kc, vc, pos)
    n_sel = -(-(past + s) // SEL_BLOCK)
    n_past_blk = past // SEL_BLOCK
    n_new_blk = n_sel - n_past_blk
    idx = select_blocks(imp, pos, n_sel)
    bi = jnp.arange(b)[:, None, None, None]
    hi = jnp.arange(NSA_KV_HEADS)[None, None, :, None]
    r2 = PAGE_SIZE // SEL_BLOCK
    pool_blk = pool_sel.reshape((-1, SEL_BLOCK) + pool_sel.shape[2:])
    jp = jnp.minimum(idx, n_past_blk - 1)
    phys = page_table[bi, jp // r2] * r2 + jp % r2
    g_past = pool_blk[phys, :, :, hi]
    new_blk = jnp.pad(kv_sel, ((0, 0), (0, n_new_blk * SEL_BLOCK - s), (0, 0), (0, 0), (0, 0)))
    new_blk = new_blk.reshape(b, n_new_blk, SEL_BLOCK, 2, NSA_KV_HEADS, HEAD_DIM)
    jn = jnp.clip(idx - n_past_blk, 0, n_new_blk - 1)
    g_new = new_blk[bi, jn, :, :, hi]
    g = jnp.where((idx < n_past_blk)[..., None, None, None], g_past.astype(g_new.dtype), g_new)
    o_sel = sel_branch(q, g[..., 0, :], g[..., 1, :], idx, pos)
    nb = win_buf.shape[1]
    w_rows = jnp.concatenate([win_buf.astype(kv_win.dtype), kv_win], axis=1)
    kp = past - nb + jnp.arange(nb + s)
    o_win = win_branch(q, w_rows[:, :, 0], w_rows[:, :, 1], pos, kp)
    return o_cmp, o_sel, o_win, kv_cmp, kv_sel, w_rows[:, s:]

def decoder_layer(x, nsa_fn, m_conv_buf, m_C, m_n, m_m, f_buf,
                  g_mix, w_in, w_out, w_mconv, b_mconv, w_mq, w_mk, b_ig, b_fg,
                  g_mhead, m_skip, g_nsa, g_ffn, w_up, w_fconv, w_down):
    b, s, _ = x.shape
    xn = rmsnorm(x, g_mix)
    q, kvc, kvs, kvw, gt, mu, mv, mo, mi, mf = jnp.split(
        xn @ w_in, np.cumsum(IN_SPLITS)[:-1].tolist(), axis=-1)
    kv_shape = (b, s, 2, NSA_KV_HEADS, HEAD_DIM)
    qh = q.reshape(b, s, NSA_KV_HEADS, NSA_GROUP, HEAD_DIM)
    o_cmp, o_sel, o_win, new_cmp, new_sel, new_win = nsa_fn(
        qh, kvc.reshape(kv_shape), kvs.reshape(kv_shape), kvw.reshape(kv_shape))
    gates = jax.nn.sigmoid(gt).reshape(b, s, NSA_KV_HEADS, NSA_GROUP, N_BRANCH, 1)
    o_nsa = gates[..., 0, :] * o_cmp + gates[..., 1, :] * o_sel + gates[..., 2, :] * o_win
    o_nsa = rmsnorm(o_nsa.reshape(b, s, NSA_WIDTH), g_nsa).astype(x.dtype)
    o_m, m_conv_new, C, n, m = mlstm_mixer(mu, mv, mo, mi, mf, m_conv_buf, m_C, m_n, m_m,
                                           w_mconv, b_mconv, w_mq, w_mk, b_ig, b_fg, g_mhead, m_skip)
    h = x + jnp.concatenate([o_m, o_nsa], axis=-1) @ w_out
    up, f_new = causal_dwconv(rmsnorm(h, g_ffn) @ w_up, f_buf, w_fconv)
    a, g = jnp.split(up, 2, axis=-1)
    y = h + (jax.nn.silu(g) * a) @ w_down
    return y, new_cmp, new_sel, new_win, m_conv_new, C, n, m, f_new

def setup_inputs(seed: int = 0) -> dict:
    key = jax.random.key(seed)
    keys = iter(jax.random.split(key, 40))
    f32 = jnp.float32

    def nrm(shape, scale):
        return jax.random.normal(next(keys), shape, f32) * scale

    def gain(shape):
        return 1.0 + nrm(shape, 0.05)

    n_pages = PAST_LEN // PAGE_SIZE
    used = DEC_BATCH * n_pages
    n_pool = used + max(1, used // 4)
    win_buf = min(WINDOW, PAST_LEN)
    page_table = jax.random.permutation(next(keys), n_pool)[:used].reshape(DEC_BATCH, n_pages).astype(jnp.int32)
    kv_row = (2, NSA_KV_HEADS, HEAD_DIM)
    return {
        'x_prompt': nrm((BATCH, SEQ, D_MODEL), 1.0),
        'x_sample': nrm((DEC_BATCH, DEC_SEQ, D_MODEL), 1.0),
        'cache_cmp': nrm((DEPTH, n_pool, PAGE_SIZE) + kv_row, 1.0),
        'cache_sel': nrm((DEPTH, n_pool, PAGE_SIZE) + kv_row, 1.0),
        'state_win': nrm((DEPTH, DEC_BATCH, win_buf) + kv_row, 1.0),
        'state_mlstm_C': nrm((DEPTH, DEC_BATCH, MLSTM_HEADS, MLSTM_DH, MLSTM_DH), 0.1),
        'state_mlstm_n': nrm((DEPTH, DEC_BATCH, MLSTM_HEADS, MLSTM_DH), 0.3),
        'state_mlstm_m': nrm((DEPTH, DEC_BATCH, MLSTM_HEADS), 0.5),
        'state_mlstm_conv': nrm((DEPTH, DEC_BATCH, MLSTM_CONV - 1, MLSTM_WIDTH), 1.0),
        'state_ffn_conv': nrm((DEPTH, DEC_BATCH, FFN_CONV - 1, 2 * D_FF), 1.0),
        'page_table': page_table,
        'g_mix': gain((DEPTH, D_MODEL)),
        'w_in': nrm((DEPTH, D_MODEL, N_IN), D_MODEL ** -0.5),
        'w_out': nrm((DEPTH, MIX_WIDTH, D_MODEL), MIX_WIDTH ** -0.5),
        'w_mconv': nrm((DEPTH, MLSTM_CONV, MLSTM_WIDTH), MLSTM_CONV ** -0.5),
        'b_mconv': nrm((DEPTH, MLSTM_WIDTH), 0.02),
        'w_mq': nrm((DEPTH, MLSTM_HEADS, MLSTM_DH, MLSTM_DH), MLSTM_DH ** -0.5),
        'w_mk': nrm((DEPTH, MLSTM_HEADS, MLSTM_DH, MLSTM_DH), MLSTM_DH ** -0.5),
        'b_ig': nrm((DEPTH, MLSTM_HEADS), 0.1),
        'b_fg': jnp.linspace(3.0, 6.0, MLSTM_HEADS, dtype=f32) + nrm((DEPTH, MLSTM_HEADS), 0.1),
        'g_mhead': gain((DEPTH, MLSTM_HEADS, MLSTM_DH)),
        'm_skip': gain((DEPTH, MLSTM_WIDTH)),
        'pe_cmp': nrm((DEPTH, 2, CMP_BLOCK, HEAD_DIM), 0.1),
        'w_cmp1': nrm((DEPTH, 2, CMP_BLOCK * HEAD_DIM, CMP_HIDDEN), (CMP_BLOCK * HEAD_DIM) ** -0.5),
        'w_cmp2': nrm((DEPTH, 2, CMP_HIDDEN, HEAD_DIM), CMP_HIDDEN ** -0.5),
        'g_nsa': gain((DEPTH, NSA_WIDTH)),
        'g_ffn': gain((DEPTH, D_MODEL)),
        'w_up': nrm((DEPTH, D_MODEL, 2 * D_FF), D_MODEL ** -0.5),
        'w_fconv': nrm((DEPTH, FFN_CONV, 2 * D_FF), FFN_CONV ** -0.5),
        'w_down': nrm((DEPTH, D_FF, D_MODEL), D_FF ** -0.5),
        'g_final': gain((D_MODEL,)),
    }

def reference(x_prompt, x_sample, cache_cmp, cache_sel, state_win, state_mlstm_C, state_mlstm_n,
              state_mlstm_m, state_mlstm_conv, state_ffn_conv, page_table,
              g_mix, w_in, w_out, w_mconv, b_mconv, w_mq, w_mk, b_ig, b_fg, g_mhead, m_skip,
              pe_cmp, w_cmp1, w_cmp2, g_nsa, g_ffn, w_up, w_fconv, w_down, g_final):
    yp, ys = x_prompt, x_sample
    bp, dt = x_prompt.shape[0], x_prompt.dtype
    per_p, per_s = [], []
    for l in range(DEPTH):
        wl = (g_mix[l], w_in[l], w_out[l], w_mconv[l], b_mconv[l], w_mq[l], w_mk[l], b_ig[l], b_fg[l],
              g_mhead[l], m_skip[l], g_nsa[l], g_ffn[l], w_up[l], w_fconv[l], w_down[l])
        nsa_p = functools.partial(nsa_prompt, pe=pe_cmp[l], w1=w_cmp1[l], w2=w_cmp2[l])
        nsa_s = functools.partial(nsa_sample, pool_cmp=cache_cmp[l], pool_sel=cache_sel[l],
                                  win_buf=state_win[l], page_table=page_table,
                                  pe=pe_cmp[l], w1=w_cmp1[l], w2=w_cmp2[l])
        yp, *st_p = decoder_layer(
            yp, nsa_p,
            jnp.zeros((bp, MLSTM_CONV - 1, MLSTM_WIDTH), dt),
            jnp.zeros((bp, MLSTM_HEADS, MLSTM_DH, MLSTM_DH), jnp.float32),
            jnp.zeros((bp, MLSTM_HEADS, MLSTM_DH), jnp.float32),
            jnp.zeros((bp, MLSTM_HEADS), jnp.float32),
            jnp.zeros((bp, FFN_CONV - 1, 2 * D_FF), dt), *wl)
        ys, *st_s = decoder_layer(
            ys, nsa_s, state_mlstm_conv[l], state_mlstm_C[l], state_mlstm_n[l], state_mlstm_m[l],
            state_ffn_conv[l], *wl)
        per_p.append(st_p)
        per_s.append(st_s)
    y_prompt = rmsnorm(yp, g_final)
    y_sample = rmsnorm(ys, g_final)
    cmp_p, sel_p, win_p, mconv_p, C_p, n_p, m_p, fconv_p = [jnp.stack(a) for a in zip(*per_p)]
    cmp_s, sel_s, win_s, mconv_s, C_s, n_s, m_s, fconv_s = [jnp.stack(a) for a in zip(*per_s)]
    return (y_prompt, y_sample, cmp_p, cmp_s, sel_p, sel_s, win_p, win_s,
            C_p, C_s, n_p, n_s, m_p, m_s, mconv_p, mconv_s, fconv_p, fconv_s)


_drawn_inputs = setup_inputs


def setup_inputs(seed=0):
    import zlib

    import numpy as np

    out = dict(_drawn_inputs(seed))
    spreads = {}
    factors = {'g_mhead': 10.075, 'm_skip': 15.856, 'g_nsa': 3.591}
    for name, (base, spread) in spreads.items():
        noise = np.random.default_rng([zlib.crc32(name.encode()), seed]).standard_normal(out[name].shape)
        drawn = base * np.exp(spread * noise) if base else spread * noise
        out[name] = __import__('jax').numpy.asarray(drawn.astype(out[name].dtype))
    for name, factor in factors.items():
        out[name] = (out[name] * factor).astype(out[name].dtype)
    return out
```

```python
import concourse.bass as bass
from concourse import mybir
from contextlib import ExitStack

F32 = mybir.dt.float32
I32 = mybir.dt.int32
ALU = mybir.AluOpType
ACT = mybir.ActivationFunctionType
AX = mybir.AxisListType

P = 128
D = 1024
KD = D // P
SEQ = 512
NB, TS = 8, 8
NSMP = NB * TS
T = SEQ + NSMP
NTILE = 5
TROWS = [P] * 4 + [NSMP]
PAST, PAGE = 2048, 128
HD, KVH, GRP = 64, 2, 4
HEADS = KVH * GRP
MH = 4
DFF = 2816
NFF = DFF // P
WIN = 512
NIN = 2848
EPS = 1e-6
NEG = -1e30
SCALE = HD ** -0.5
KSCALE = P ** -0.5
NSEL = PAST // 64
PRIORITY = 1e4
ROWF = 4096
UPW = 3 + SEQ + NB * (3 + TS)
CVW = UPW - 3
FPW = 2 + SEQ + NB * (2 + TS)
FVW = FPW - 2

V_GMIX, V_GFFN, V_GNSA, V_SKIP, V_GHEAD, V_BCONV, V_WCONV, V_PE, V_GFIN = 0, 8, 16, 20, 24, 28, 32, 48, 80
V_ROWS = 88
V_MCS = 88
V_N = V_MCS + 4 * 24
V_COLS = V_N + NB * MH


def hybrid_decoder_layer(nc, A, O):
    ctx = ExitStack()
    with ctx:
        def sb(name, shape, dt=F32):
            return ctx.enter_context(nc.sbuf_tensor(name, shape, dt))

        made = {}

        def S(name):
            if name not in made:
                made[name] = ctx.enter_context(nc.semaphore(name))
            return made[name]

        banks = ctx.enter_context(nc.psum_tensor("banks", [P, 8, 512], F32))
        ps = [banks[:, i, :] for i in range(8)]

        def carve(region, sizes):
            at, out = 0, {}
            for name, n in sizes:
                out[name] = region[:, at:at + n]
                at += n
            assert at <= region.shape[1], (at, region.shape)
            return out

        ident = sb("ident", [P, P])
        ones = sb("ones", [P, P])
        causal = sb("causal", [P, P])
        causalT = sb("causalT", [P, P])
        smask = sb("smask", [P, NSMP])
        winmask = sb("winmask", [P, WIN])
        newmask = sb("newmask", [P, TS])
        gsum = sb("gsum", [P, P])
        selh = sb("selh", [MH, MH, P])
        small = sb("small", [P, 8])
        vcol = sb("vcol", [P, V_COLS])
        idx = sb("idx", [P, NB], I32)
        xT = sb("xT", [P, KD, T])
        xnT = sb("xnT", [P, KD, T])
        ring = sb("ring", [P, 2, ROWF])
        RA = sb("RA", [P, 5248])
        RB = sb("RB", [P, 8192])
        RC = sb("RC", [P, 17412])
        ktT = sb("ktT", [P, 2, T])
        kcT_s = sb("kcT_s", [P, 4, P])
        vc_s = sb("vc_s", [P, 4, P])
        kcT_p = sb("kcT_p", [P, 16])
        vc_p = sb("vc_p", [16, P])
        gsig = sb("gsig", [P, NTILE, HEADS * 3])
        gb = sb("gb", [MH, 2])
        m0 = sb("m0", [MH, NB])
        hb = sb("hb", [P, 2])

        c = carve(RC, [("qT", GRP * T), ("Qbd", NB * 64), ("uT", MH * UPW + 152), ("kv", NTILE * 768),
                       ("ucT", MH * T), ("moT", MH * T), ("mv", NTILE * MH * (P + 1))])
        ring2 = RC[:, 9220:9220 + 2 * ROWF].rearrange("p (s n) -> p s n", s=2)
        qT = c["qT"].rearrange("p (g t) -> p g t", g=GRP)
        Qbd = c["Qbd"].rearrange("p (b r) -> p b r", b=NB)
        uT = c["uT"][:, 0:MH * UPW].rearrange("p (k t) -> p k t", k=MH)
        oatt = c["uT"][:, 0:NTILE * 512].rearrange("p (i f) -> p i f", i=NTILE)
        ucT = c["ucT"].rearrange("p (k t) -> p k t", k=MH)
        moT = c["moT"].rearrange("p (k t) -> p k t", k=MH)
        kv = c["kv"].rearrange("p (i f) -> p i f", i=NTILE)
        mv = c["mv"].rearrange("p (i h e) -> p i h e", i=NTILE, h=MH)

        a1 = carve(RA, [("xtok", NTILE * D)])
        xtok = a1["xtok"].rearrange("p (i f) -> p i f", i=NTILE)
        b1 = carve(RB, [("sq", 2 * T), ("rms", T), ("rstd", T), ("vrows", P), ("mcs", MH * P), ("nrows", P),
                        ("wrow", WIN), ("mod", P), ("part", 8), ("newk", 8)])
        sq = b1["sq"].rearrange("p (s t) -> p s t", s=2)
        rms, rstd, vrows, nrows = b1["rms"], b1["rstd"], b1["vrows"], b1["nrows"]
        mcs = b1["mcs"]
        packed = xnT[:, :, :].rearrange("p k t -> p (k t)")[:, 0:4096].rearrange("p (k n) -> p k n", k=2)
        a3 = carve(RA, [("XT", 4 * 512), ("hid", 2 * 2 * P), ("", 1536), ("irow", T), ("frow", T)])
        XT = a3["XT"].rearrange("p (s n) -> p s n", s=4)
        hid = a3["hid"].rearrange("p (s k n) -> p s k n", s=2, k=2)
        irow, frow = a3["irow"][0:MH, :], a3["frow"][0:MH, :]
        b3 = carve(RB, [("w1c", 2 * 16 * P), ("w2c", 2 * HD), ("wg", KD * 36)])
        w1c = b3["w1c"].rearrange("p (k c n) -> p k c n", k=2, c=16)
        w2c = b3["w2c"].rearrange("p (k n) -> p k n", k=2)
        wg = b3["wg"].rearrange("p (k n) -> p k n", k=KD)

        a4 = carve(RA, [("hs", NTILE * MH * (P + 1)), ("vw", NTILE * P), ("rcol", 64), ("s2", 20), ("f1", 20), ("f2", 20),
                        ("f3", 20), ("slc", NB), ("wlb", NB), ("mcg", MH * 27), ("cpo", MH * P)])
        hs = a4["hs"].rearrange("p (i h e) -> p i h e", i=NTILE, h=MH)
        vw = a4["vw"].rearrange("p (i e) -> p i e", i=NTILE)
        rcol = a4["rcol"][:, 0:60].rearrange("p (k i h) -> p k i h", k=3, i=NTILE)
        slcol = a4["rcol"][0:NB, 60:64]
        s2, f1, f2, f3 = a4["s2"], a4["f1"], a4["f2"], a4["f3"]
        slc, wlb = a4["slc"], a4["wlb"]
        mcg = a4["mcg"].rearrange("p (k n) -> p k n", k=MH)
        cpo = a4["cpo"].rearrange("p (h d) -> p h d", h=MH)
        EW = 1280
        b4 = carve(RB, [("E", EW + NSMP), ("W", EW + NSMP), ("mqT", T), ("mkT", T), ("mk", NTILE * P), ("Cst", NB * P),
                        ("CT", NB * (P + 1)), ("kbd", NB * P), ("Qm", NB * NSMP)])
        E, W, mqT, mkT = b4["E"], b4["W"], b4["mqT"], b4["mkT"]
        conv = b4["E"][:, 0:2 * CVW].rearrange("p (s t) -> p s t", s=2)
        mk = b4["mk"].rearrange("p (i d) -> p i d", i=NTILE)
        Cst = b4["Cst"].rearrange("p (b d) -> p b d", b=NB)
        CT = b4["CT"].rearrange("p (b e) -> p b e", b=NB)
        kbd = b4["kbd"].rearrange("p (b d) -> p b d", b=NB)
        Qm = b4["Qm"].rearrange("p (b t) -> p b t", b=NB)
        EOFF = [0, 512, 896, 1152]
        xrows = xnT[:, :, :].rearrange("p k t -> p (k t)")
        nbh, npo, mco = xrows[0:NB, 0:512], xrows[0:1, 512:1024], xrows[0:27, 1024:1536]
        r0, r1, r2, r3 = (xnT[0:MH, 4 + n, :] for n in range(4))
        restart, down = b4["W"][0:MH, 0:T], b4["W"][0:MH, T:2 * T]
        wqk = ktT[:, :, :].rearrange("p s t -> p (s t)")[:, 0:2 * MH * P].rearrange("p (w h e) -> p w h e", w=2, h=MH)

        a5 = carve(RA, [("S", PAST + TS), ("Sw", WIN + TS), ("PTw", 4 * P), ("PTn", 2 * P), ("PTc", P), ("Qp", P), ("vcp", P),
                        ("pcd", P), ("outT", 3 * P), ("orow", 3 * HD), ("col", 16), ("pri", 3 * 40), ("top", 16), ("add", 40),
                        ("vnp", 4 * P)])
        Ss, Sw, PTc, Qp, vcp, pcd = a5["S"], a5["Sw"], a5["PTc"], a5["Qp"], a5["vcp"], a5["pcd"]
        PTw = a5["PTw"].rearrange("p (j r) -> p j r", j=4)
        PTn = a5["PTn"][0:TS, :].rearrange("p (w r) -> p w r", w=2)
        outT = a5["outT"].rearrange("p (w r) -> p w r", w=3)
        orow = a5["orow"].rearrange("p (w d) -> p w d", w=3)
        col = a5["col"]
        pri = a5["pri"].rearrange("p (s j) -> p s j", s=3)[:, :, 0:NSEL + 1]
        top = a5["top"].rearrange("p (s j) -> p s j", s=2)
        add = a5["add"][:, 0:NSEL + 1]
        vnp = a5["vnp"][0:TS, :].rearrange("p (b w d) -> p b w d", b=2, w=2)
        b5 = carve(RB, [("PT", 16 * P), ("KTb", 2 * 512), ("wkv", 4 * 4 * 256), ("kcp", P), ("ktn", 32)])
        kcp, ktn = b5["kcp"], b5["ktn"].rearrange("p (w n) -> p w n", w=2)
        PT = b5["PT"].rearrange("p (j r) -> p j r", j=16)
        KTb = b5["KTb"].rearrange("p (s n) -> p s n", s=2)
        wkv = b5["wkv"].rearrange("p (s n) -> p s n", s=4)
        vnew = xnT[0:TS, 4:8, :].rearrange("p k t -> p (k t)")[:, 0:NB * 2 * P].rearrange("p (b w d) -> p b w d", b=NB, w=2)
        osc = nc.dram_tensor("osc", (3, NB * 64, HD), F32, kind="Internal").ap()
        slots = [ring[:, 0, :], ring[:, 1, :], ring2[:, 0, :], ring2[:, 1, :]]
        b6 = carve(RB, [("qst", SEQ), ("gst", 4 * 2 * 2), ("Pb", 2 * 2 * SEQ), ("PTp", 2 * 2 * SEQ), ("cst", 16), ("tmp", 2 * P),
                        ("Pc", SEQ), ("PcT", SEQ), ("Vbd", SEQ), ("cmk", 4 * 16), ("cm", 2 * 32)])
        qst = b6["qst"]
        gst = b6["gst"].rearrange("p (i h w) -> p i h w", i=4, h=2)
        Pb = b6["Pb"].rearrange("p (s w n) -> p s w n", s=2, w=2)
        PTp = b6["PTp"].rearrange("p (s w n) -> p s w n", s=2, w=2)
        cst = b6["cst"].rearrange("p (s k w) -> p s k w", s=2, k=4)
        tmp = b6["tmp"].rearrange("p (s w d) -> p s w d", s=2, w=2)
        Pc, PcT, Vbd = b6["Pc"], b6["PcT"].rearrange("p (i t) -> p i t", i=4), b6["Vbd"]
        cmk = b6["cmk"].rearrange("p (i n) -> p i n", i=4)
        cm = b6["cm"].rearrange("p (s n) -> p s n", s=2)
        a6 = carve(RA, [("osm", 3 * 512), ("nss", 16)])
        osm = a6["osm"].rearrange("p (w f) -> p w f", w=3)
        nss = a6["nss"]
        sqo = RB[:, 0:NTILE * 512].rearrange("p (i f) -> p i f", i=NTILE)
        a7 = carve(RA, [("pad", 2 * 2 * FPW), ("ca", FVW), ("cg", FVW), ("fin", 2 * 512), ("fcol", 2 * 2 * 19), ("l18", 2 * 18),
                        ("fo", 256)])
        pad = a7["pad"].rearrange("p (s w t) -> p s w t", s=2, w=2)
        ca, cg = a7["ca"], a7["cg"]
        fin = a7["fin"][0:19, :].rearrange("p (s w n) -> p s w n", s=2, w=2)
        fcol = a7["fcol"].rearrange("p (s w n) -> p s w n", s=2, w=2)
        l18 = a7["l18"].rearrange("p (w n) -> p w n", w=2)
        fo = a7["fo"][0:18, :].rearrange("p (w n) -> p w n", w=2)
        actT = RC[:, 0:NFF * FVW].rearrange("p (k t) -> p k t", k=NFF)
        wdn = RB[:, 2304:2304 + 2 * NFF * P].rearrange("p (s k n) -> p s k n", s=2, k=NFF)
        ytok = RA[:, 0:NTILE * D].rearrange("p (i f) -> p i f", i=NTILE)

        def gfac(slot):
            return cst[:, slot, 3, :].unsqueeze(2).to_broadcast([P, 2, HD])

        UNITS = [(i, h) for i in range(4) for h in range(KVH)]

        w_in = A["w_in"][0].rearrange("(k p) n -> p k n", p=P)
        SLABS = [(0, 512), (1304, 512), (512, 512), (1024, 280), (1816, 512), (2328, 512)]
        jobs = [(0, "q", i) for i in range(4)] + [(0, "gates", 0)] + [(1, "mu", i) for i in range(4)]
        jobs += [(2, "kvA", i) for i in range(5)] + [(3, "kvB", i) for i in range(5)]
        jobs += [(4, "mv", i) for i in range(5)] + [(5, "mo", i) for i in range(4)]
        slab_last = [max(n for n, j in enumerate(jobs) if j[0] == s) for s in range(6)]
        evac, na, nv = [], 0, 0
        for _, kind, i in jobs:
            if kind in ("q", "mu"):
                na, nv = na + 1, nv + 1
            elif kind in ("mo", "kvB"):
                na += 1
            elif kind == "gates":
                nv += 1
            elif i % 2:
                na += 1
            else:
                nv += 1
            evac.append((na, nv))

        pool_cmp = A["cache_cmp"][0].rearrange("n (c j) k h d -> (n c) (j k h d)", j=16)
        pool_sel = A["cache_sel"][0].rearrange("n (c j) k h d -> (n c) (j k h d)", j=16)

        outs = [0]

        def out_dma(eng, dst, src, slow=False):
            outs[0] += 16
            return eng.dma_start(dst, src, allow_slow_non_contiguous=slow).then_inc(S("stored"), 16)

        def conv_sample(k):
            cv = conv[:, k % 2, SEQ + 3:CVW]
            full = bass.AP(cv.tensor, cv.offset, [list(cv.ap[0]), [3 + TS, NB], [1, TS]])
            return full

        block = ctx.enter_context(nc.Block())

        @block.gpsimd
        def _(pool):
            g = nc.gpsimd
            wrow = b1["wrow"].bitcast(I32).rearrange("p (j q) -> p j q", j=4)
            mod = b1["mod"].bitcast(I32).rearrange("p (q g t) -> p q g t", q=4, g=GRP)
            src = A["page_table"]
            for b in range(NB):
                pool.dma_start(idx[:, b:b + 1], bass.AP(src.tensor, src.offset + 16 * b, [[1, 16], [0, 8], [1, 1]]),
                               allow_slow_non_contiguous=True).then_inc(S("idx_in"), 16)
            g.memset(ident[:], 0.0)
            g.memset(wg, 0.0)
            g.memset(small[:, 0:1], EPS)
            g.memset(small[:, 2:3], 0.0)
            g.memset(small[:, 3:5], 1.0)
            g.memset(ones[:], 1.0).then_inc(S("filled"), 1)
            pool.wait_ge(S("filled"), 1)
            g.affine_select(out=ident[:], in_=ident[:], compare_op=ALU.not_equal, fill=1.0, base=0,
                            pattern=[[-1, P]], channel_multiplier=1).then_inc(S("ident_ready"), 1)
            g.iota(b1["part"].bitcast(I32)[:, 0:1], [[0, 1]], base=0, channel_multiplier=1)
            g.iota(b1["newk"].bitcast(I32), [[1, TS]], base=0, channel_multiplier=0)
            g.iota(mod, [[0, 4], [0, GRP], [1, TS]], base=0, channel_multiplier=0)
            g.iota(wrow, [[1, 4], [4, P]], base=0, channel_multiplier=0).then_inc(S("numbers"), 1)
            g.memset(uT, 0.0)
            g.memset(mv[:, :, :, P:P + 1], 1.0)
            g.memset(Qbd, 0.0).then_inc(S("padded"), 1)
            g.memset(causal[:], 0.0)
            g.memset(causalT[:], 0.0)
            g.memset(smask[:], 0.0)
            g.memset(gsum[:], 1.0)
            g.memset(selh[:], 1.0).then_inc(S("filled"), 1)
            pool.wait_ge(S("filled"), 2)
            g.affine_select(out=causal[:], in_=causal[:], compare_op=ALU.is_ge, fill=NEG, base=0,
                            pattern=[[-1, P]], channel_multiplier=1)
            g.affine_select(out=causalT[:], in_=causalT[:], compare_op=ALU.is_ge, fill=NEG, base=0,
                            pattern=[[1, P]], channel_multiplier=-1)
            g.affine_select(out=small[:, 4:5], in_=small[:, 4:5], compare_op=ALU.is_ge, fill=0.0, base=-31,
                            pattern=[[0, 1]], channel_multiplier=1)
            g.affine_select(out=selh[:], in_=selh[:], compare_op=ALU.is_equal, fill=0.0, base=0,
                            pattern=[[-1, MH], [0, P]], channel_multiplier=1)
            sv = smask[0:NSMP, :].rearrange("p (b t) -> p b t", b=NB)
            g.affine_select(out=sv, in_=sv, compare_op=ALU.is_ge, fill=NEG, base=0,
                            pattern=[[-TS, NB], [0, TS]], channel_multiplier=1)
            gv = gsum[:, :].rearrange("p (q r) -> p q r", q=4)
            g.affine_select(out=gv, in_=gv, compare_op=ALU.is_ge, fill=0.0, base=0,
                            pattern=[[-32, 4], [0, 32]], channel_multiplier=1).then_inc(S("filled"), 1)
            pool.wait_ge(S("filled"), 3)
            g.affine_select(out=sv, in_=sv, compare_op=ALU.is_ge, fill=NEG, base=0,
                            pattern=[[TS, NB], [1, TS]], channel_multiplier=-1)
            g.affine_select(out=gv, in_=gv, compare_op=ALU.is_ge, fill=0.0, base=31,
                            pattern=[[32, 4], [0, 32]], channel_multiplier=-1).then_inc(S("band"), 1)
            kv_job = [n for n, j in enumerate(jobs) if j[1] == "kvB"][-1]
            pool.wait_ge(S("ev_act"), evac[kv_job][0])
            pool.wait_ge(S("ev_dve"), evac[kv_job][1])
            for br, (op, os) in enumerate((("cmp_p", "cmp_s"), ("sel_p", "sel_s"), ("win_p", None))):
                out_dma(pool, O[op][0, 0].rearrange("(i p) k h d -> p i (k h d)", p=P), kv[:, 0:4, br * 256:br * 256 + 256])
                if os:
                    out_dma(pool, O[os][0].rearrange("b t k h d -> (b t) (k h d)"), kv[0:NSMP, 4, br * 256:br * 256 + 256])
            for b in range(NB):
                out_dma(pool, O["win_s"][0, b, WIN - TS:WIN].rearrange("t k h d -> t (k h d)"),
                        kv[b * TS:(b + 1) * TS, 4, 512:768])
            out_dma(pool, O["win_s"][0, :, 0:WIN - TS].rearrange("b r k h d -> b (r k h d)"),
                    A["state_win"][0, :, TS:WIN].rearrange("b r k h d -> b (r k h d)"))
            pool.wait_ge(S("idx_ready"), 1)

            def gather(pool_rows, slot, col):
                g.indirect_dma_start(ring[:, slot, :], None, pool_rows,
                                     bass.IndirectOffsetOnAxis(ap=col, axis=0)).then_inc(S(f"rows_in{slot}"), 16)

            for b in range(2):
                pool.wait_ge(S("job"), slab_last[4 + b] + 1)
                gather(pool_cmp, b, idx[:, b:b + 1])
            for b in range(2, NB):
                pool.wait_ge(S("c_packed"), 2 * (b - 1))
                gather(pool_cmp, b % 2, idx[:, b:b + 1])
            pool.wait_ge(S("c_packed"), 2 * 7)
            for i in range(4):
                pool.dma_start(ring[8 * i:8 * i + 8, 0, :].rearrange("r (j n) -> r j n", j=16),
                               kv[:, i, 0:256]).then_inc(S("own_in"), 16)
            pool.wait_ge(S("c_packed"), 2 * 9)
            for b in range(2):
                g.indirect_dma_start(slots[b], None, pool_sel,
                                     bass.IndirectOffsetOnAxis(ap=idx[:, b:b + 1], axis=0)).then_inc(S(f"sel_in{b}"), 16)
            pool.wait_ge(S("m_mcod"), 1)
            pool.dma_start(O["mconv_p"][0, 0], mco[0:3, :]).then_inc(S("m_stored"), 16)
            pool.dma_start(O["mconv_s"][0].rearrange("b j f -> (b j) f"), mco[3:27, :]).then_inc(S("m_stored"), 16)
            pool.wait_ge(S("m_pre"), 1)
            pool.dma_start(O["m_p"][0].rearrange("a h -> h a"), r3[:, SEQ - 1:SEQ],
                           allow_slow_non_contiguous=True).then_inc(S("m_stored"), 16)
            pool.dma_start(O["m_s"][0].rearrange("b h -> h b"), r3[:, SEQ + TS - 1:T:TS],
                           allow_slow_non_contiguous=True).then_inc(S("m_stored"), 16)
            for h in range(MH):
                pool.wait_ge(S("m_p7d"), 5 * h + 4)
                pool.dma_start(O["C_s"][0, :, h].rearrange("b e d -> e b d"), Cst[:, :, :]).then_inc(S("m_cout"), 16)
                pool.wait_ge(S("m_p7d"), 5 * h + 5)
                out_dma(pool, O["C_p"][0, 0, h], cpo[:, h, :])
            pool.dma_start(O["n_p"][0].rearrange("a h d -> a (h d)"), npo).then_inc(S("m_stored"), 16)
            pool.dma_start(O["n_s"][0].rearrange("b h d -> b (h d)"), nbh).then_inc(S("m_stored"), 16)
            pool.wait_ge(S("m_stored"), 6 * 16)
            pool.wait_ge(S("m_cout"), 4 * 16)
            pool.wait_ge(S("m_mix"), MH)
            for b in range(2, NB):
                if b >= 4:
                    pool.wait_ge(S("s_pv"), b // 2 - 1)
                g.indirect_dma_start(slots[b % 4], None, pool_sel,
                                     bass.IndirectOffsetOnAxis(ap=idx[:, b:b + 1], axis=0)).then_inc(S(f"sel_in{b % 4}"), 16)
            pool.wait_ge(S("s_pv"), 4)
            g.memset(cmk, 0.0).then_inc(S("p_cm0"), 1)
            pool.wait_ge(S("p_cm0"), 1)
            g.affine_select(out=cmk, in_=cmk, compare_op=ALU.is_ge, fill=NEG, base=-31,
                            pattern=[[P, 4], [-32, 16]], channel_multiplier=1).then_inc(S("p_cmk"), 1)
            pool.sem_inc(S("u_fof"), 1)
            for q in range(NFF):
                pool.wait_ge(S("u_fo"), q + 2)
                cols = slice(q * P, (q + 1) * P)
                pool.dma_start(O["fconv_p"][0, 0].rearrange("j (w n) -> j w n", w=2)[:, :, cols], fo[0:2]).then_inc(S("u_fos"), 16)
                pool.dma_start(O["fconv_s"][0].rearrange("b j (w n) -> (b j) w n", w=2)[:, :, cols], fo[2:18])\
                    .then_inc(S("u_fos"), 16)
                pool.wait_ge(S("u_fos"), 32 * (q + 1))
                pool.sem_inc(S("u_fof"), 1)

        def square_sum_act(act, n, ready, src):
            for k in range(KD):
                ready(act, k)
                if k >= 2:
                    act.wait_ge(S("norm_summed"), KD * (n - 1) + k - 1)
                nc.scalar.activation(sq[:, k % 2, :], src[:, k, :], ACT.Square).then_inc(S("norm_sq"), 1)
            act.wait_ge(S("norm_summed"), KD * n)
            nc.scalar.activation(rms[:, 0:SEQ], ps[6][:, :], ACT.Sqrt, bias=small[:, 0:1], scale=1.0 / D)
            nc.scalar.activation(rms[:, SEQ:T], ps[7][:, 0:NSMP], ACT.Sqrt, bias=small[:, 0:1],
                                 scale=1.0 / D).then_inc(S("norm_root"), 1)

        def square_sum_pe(pe, n, k):
            pe.wait_ge(S("norm_sq"), KD * (n - 1) + k + 1)
            nc.tensor.matmul(ps[6][:, :], ones[:], sq[:, k % 2, 0:SEQ], start=(k == 0), stop=(k == KD - 1))
            nc.tensor.matmul(ps[7][:, 0:NSMP], ones[:], sq[:, k % 2, SEQ:T], start=(k == 0),
                             stop=(k == KD - 1)).then_inc(S("norm_summed"), 1)

        def norm_dve(dve, n, src, dst, gain):
            dve.wait_ge(S("norm_root"), n)
            nc.vector.reciprocal(rstd, rms).then_inc(S("norm_rstd"), 1)
            dve.wait_ge(S("norm_rstd"), n)
            for k in range(KD):
                nc.vector.scalar_tensor_tensor(out=dst[:, k, :], in0=src[:, k, :], scalar=vcol[:, gain + k:gain + k + 1],
                                               in1=rstd, op0=ALU.mult, op1=ALU.mult).then_inc(S("normed"), 1)

        @block.scalar
        def _(act):
            a = nc.scalar
            for k in range(1, KD, 2):
                act.wait_ge(S("x_turned"), k + 1)
                a.activation(xT[:, k, 0:SEQ], ps[1 + k % 4][:, :], ACT.Copy).then_inc(S("x_act"), 1)

            def x_ready(act, k):
                act.wait_ge(S("x_act"), 4)
                act.wait_ge(S("x_dve"), 5)

            act.wait_ge(S("filled"), 1)
            square_sum_act(act, 1, x_ready, xT)
            act.wait_ge(S("padded"), 1)
            for n, (_, kind, i) in enumerate(jobs):
                bank, smp = ps[n % 3], ps[3 + n % 2][:, 0:NSMP]
                rows = TROWS[i]
                if kind in ("q", "mu", "mo") or kind == "kvB" or (kind in ("kvA", "mv") and i % 2):
                    act.wait_ge(S("job"), n + 1)
                if kind == "q":
                    a.activation(qT[:, i, 0:SEQ], bank[:, :], ACT.Copy).then_inc(S("ev_act"), 1)
                elif kind == "mu":
                    a.activation(uT[:, i, 3:3 + SEQ], bank[:, :], ACT.Copy).then_inc(S("ev_act"), 1)
                elif kind == "mo":
                    a.activation(moT[:, i, 0:SEQ], bank[:, :], ACT.Sigmoid)
                    a.activation(moT[:, i, SEQ:T], smp, ACT.Sigmoid).then_inc(S("ev_act"), 1)
                elif kind == "kvB":
                    a.activation(kv[0:rows, i, 512:768], bank[0:rows, 0:256], ACT.Copy)
                    a.activation(gsig[0:rows, i, :], bank[0:rows, 256:280], ACT.Sigmoid).then_inc(S("ev_act"), 1)
                elif kind == "kvA" and i % 2:
                    a.activation(kv[0:rows, i, 0:512], bank[0:rows, :], ACT.Copy).then_inc(S("ev_act"), 1)
                elif kind == "mv" and i % 2:
                    a.activation(mv[0:rows, i, :, 0:P], bank[0:rows, :].rearrange("p (h e) -> p h e", h=MH),
                                 ACT.Copy).then_inc(S("ev_act"), 1)
            act.sem_inc(S("c_xa"), 2)
            act.wait_ge(S("hb_made"), 1)
            a.activation(hb[:, 0:1], ps[5][:, 0:1], ACT.Copy)
            a.activation(hb[:, 1:2], ps[5][:, 1:2], ACT.Copy).then_inc(S("c_hid"), 2)
            act.wait_ge(S("c_hid"), 2)

            def compress_act(b, s, w):
                for kvi in range(2):
                    for f in (1, 3):
                        n = b * 8 + (4 * kvi + f)
                        act.wait_ge(S("c_turned"), n + 9)
                        act.wait_ge(S("c_mm"), n + 1)
                        a.activation(XT[:, f, 0:4 * w], ps[f][:, 0:4 * w], ACT.Copy).then_inc(S("c_xa"), 1)
                    act.wait_ge(S("c_mm"), b * 8 + (4 * kvi + 4 + 4))
                    act.wait_ge(S("c_kc"), b * 2 + (kvi + 1))
                    a.activation(hid[:, s, kvi, 0:w], ps[4 + kvi][:, 0:w], ACT.Silu,
                                 bias=hb[:, kvi:kvi + 1]).then_inc(S("c_hid"), 1)

            with act.Fori(0, NB // 2) as it:
                for s in range(2):
                    compress_act(it * 2 + s, s, P)
            compress_act(NB, 0, 32)

            for k in range(MH):
                act.wait_ge(S("m_conv"), k + 1)
                a.activation(ucT[:, k, 0:SEQ], conv[:, k % 2, 0:SEQ], ACT.Silu, bias=vcol[:, V_BCONV + k:V_BCONV + k + 1])
                a.activation(ucT[:, k, SEQ:T].rearrange("p (b t) -> p b t", b=NB),
                             conv_sample(k), ACT.Silu,
                             bias=vcol[:, V_BCONV + k:V_BCONV + k + 1]).then_inc(S("m_uc"), 1)
            act.wait_ge(S("m_abs"), 1)
            a.activation(r0, r0, ACT.Exp, scale=-1.0).then_inc(S("m_ln"), 1)
            act.wait_ge(S("m_ln"), 1)
            a.activation(r0, r0, ACT.Ln, bias=small[0:MH, 3:4]).then_inc(S("m_ln"), 1)
            act.wait_ge(S("m_pre"), 1)
            a.activation(frow, r3, ACT.Exp, scale=-1.0)
            a.activation(r0, r0, ACT.Exp)
            a.activation(r2[:, 0:NSMP], r2[:, 0:NSMP], ACT.Exp).then_inc(S("m_rows"), 1)
            for h in range(MH):
                act.wait_ge(S("m_proj"), h + 1)
                a.activation(mqT[:, 0:SEQ], ps[0][:, :], ACT.Copy)
                a.activation(mkT[:, 0:SEQ], ps[2][:, :], ACT.Copy, scale=KSCALE).then_inc(S("m_proja"), 1)
                act.wait_ge(S("m_e"), h + 1)
                for j in range(4):
                    dg = E[:, EOFF[j]:EOFF[j] + P]
                    a.activation(dg, dg, ACT.Exp)
                    if j < 3:
                        a.activation(E[:, EOFF[j] + P:EOFF[j + 1]], ps[3][:, (j + 1) * P:SEQ], ACT.Exp,
                                     bias=rcol[:, 0, j, h:h + 1])
                a.activation(E[0:NSMP, EW:EW + NSMP], E[0:NSMP, EW:EW + NSMP], ACT.Exp).then_inc(S("m_x"), 1)
                act.wait_ge(S("m_numd"), h + 1)
                for i in range(NTILE):
                    rows = TROWS[i]
                    last = a.activation(W[0:rows, i * P:(i + 1) * P], hs[0:rows, i, h, 0:P], ACT.Square,
                                        accum_out=s2[0:rows, 4 * i + h:4 * i + h + 1])
                last.then_inc(S("m_sq"), 1)
            act.wait_ge(S("m_ms"), 1)
            a.activation(f2, f2, ACT.Sqrt, bias=small[:, 0:1], scale=1.0 / P).then_inc(S("m_root"), 1)

            act.sem_inc(S("s_kt"), 1)
            with act.Fori(0, 2) as it:
                for x in range(2):
                    p10 = it * 20 + 10 * x
                    p1 = it * 2 + x

                    def keys(n):
                        act.wait_ge(S("s_t"), p10 + (n + 1))
                        act.wait_ge(S("s_sc"), p10 + (n + 1))
                        a.activation(KTb[:, n % 2, :], ps[4 + n % 2], ACT.Copy).then_inc(S("s_kt"), 1)

                    keys(0)
                    keys(1)
                    act.wait_ge(S("s_cb"), p1 + 1)
                    for b2 in range(2):
                        r = slice(64 * b2, 64 * b2 + 64)
                        last = a.activation(pcd[r, r], ps[7][r, 16:80], ACT.Exp, bias=col[r, 0:1], scale=SCALE,
                                            accum_out=col[r, 1:2])
                    last.then_inc(S("s_ce"), 1)
                    for n in range(2, 7):
                        keys(n)
                    act.wait_ge(S("s_wb"), p1 + 1)
                    a.activation(Sw, Sw, ACT.Exp, bias=col[:, 2:3], scale=SCALE, accum_out=col[:, 5:6]).then_inc(S("s_we"), 1)
                    for n in range(7, 10):
                        keys(n)
                    act.wait_ge(S("s_sb"), p1 + 1)
                    a.activation(Ss, Ss, ACT.Exp, bias=col[:, 3:4], scale=SCALE, accum_out=col[:, 4:5]).then_inc(S("s_se"), 1)
                    act.wait_ge(S("s_pv"), p1 + 1)
                    a.activation(a5["outT"], ps[4][:, 0:3 * P], ACT.Copy).then_inc(S("s_ot"), 1)
            act.sem_inc(S("p_exp"), 2)
            act.sem_inc(S("p_pta"), 1)
            act.wait_ge(S("p_csub"), 1)
            a.activation(Pc, Pc, ACT.Exp, scale=SCALE).then_inc(S("p_cexp"), 1)
            with act.Fori(0, GRP) as g:
                for step in range(10):
                    if step < 8:
                        u = step
                        i, h = UNITS[u]
                        n = (i + 1) * P
                        act.wait_ge(S("p_max"), g * 8 + (u + 1))
                        act.wait_ge(S("p_tr"), g * 8 + (u + 1))
                        for w in range(2):
                            last = a.activation(Pb[:, u % 2, w, 0:n], ps[2 * (u % 2) + w][:, 0:n], ACT.Exp,
                                                bias=cst[:, u % 2, 1, w:w + 1], scale=SCALE, accum_out=cst[:, u % 2, 2, w:w + 1])
                        last.then_inc(S("p_exp"), 1)
                    if 1 <= step < 9:
                        u = step - 1
                        n = (UNITS[u][0] + 1) * P
                        act.wait_ge(S("p_tr"), g * 8 + (u + 3))
                        act.wait_ge(S("p_pv"), g * 8 + (u + 1))
                        a.activation(PTp[:, u % 2, 1, 0:n], ps[5][:, 0:n], ACT.Copy).then_inc(S("p_pta"), 1)
            act.wait_ge(S("o_all"), 1)
            for i in range(NTILE):
                rows = TROWS[i]
                last = a.activation(sqo[0:rows, i, :],
                                    oatt[0:rows, i, :], ACT.Square, accum_out=nss[0:rows, i:i + 1])
            last.then_inc(S("o_sq"), 1)
            act.wait_ge(S("o_sq"), 1)
            a.activation(nss[:, 8:13], nss[:, 0:5], ACT.Sqrt, bias=small[:, 0:1], scale=1.0 / 512).then_inc(S("o_root"), 1)
            square_sum_act(act, 2, lambda act, k: act.wait_ge(S("h_done"), k + 1), xT)
            def up_act(q2, par, qn):
                act.wait_ge(S("u_mm"), qn + 1)
                act.wait_ge(S("u_conv"), qn + 1)
                for w in range(2):
                    last = a.activation(pad[:, par, w, 2:2 + SEQ], ps[2 * w + par], ACT.Copy)
                last.then_inc(S("u_pad"), 1)
                act.wait_ge(S("u_cg"), qn + 1)
                a.activation(cg, cg, ACT.Silu).then_inc(S("u_silu"), 1)
            with act.Fori(0, 5) as it:
                for q in range(4):
                    up_act(q, q % 2, it * 4 + q)
            for q in range(20, 22):
                up_act(q, q % 2, q)
            square_sum_act(act, 3, lambda act, k: act.wait_ge(S("d_done"), k + 1), xT)
            act.wait_ge(S("u_fof"), 1 + NFF)
            for n in range(10):
                act.wait_ge(S("y_turned"), n + 1)
                rows = TROWS[n // 2]
                if n % 2 == 0:
                    a.activation(ytok[0:rows, n // 2, 0:512], ps[n % 6][0:rows, :], ACT.Copy).then_inc(S("y_act"), 1)


        @block.tensor
        def _(pe):
            t = nc.tensor
            pe.wait_ge(S("ident_ready"), 1)
            pe.wait_ge(S("vec_in"), 14 * 16)
            t.transpose(ps[0][:, 0:V_ROWS], vrows[0:V_ROWS, :], ident[0:V_ROWS, 0:V_ROWS])
            for k in range(MH):
                t.transpose(ps[0][:, V_MCS + 24 * k:V_MCS + 24 * k + 24], mcs[0:24, k * P:(k + 1) * P], ident[0:24, 0:24])
            t.transpose(ps[0][:, V_N:V_N + 32], nrows[0:32, :], ident[0:32, 0:32]).then_inc(S("vec_turned"), 1)
            pe.wait_ge(S("x_in"), 5 * 16)
            for k in range(KD):
                if k >= 4:
                    pe.wait_ge(S("x_act" if k % 2 else "x_dve"), k // 2 - 1)
                for i in range(4):
                    t.transpose(ps[1 + k % 4][:, i * P:(i + 1) * P], xtok[:, i, k * P:(k + 1) * P], ident[:])
                t.transpose(ps[5][:, k * NSMP:(k + 1) * NSMP], xtok[0:NSMP, 4, k * P:(k + 1) * P],
                            ident[0:NSMP, 0:NSMP]).then_inc(S("x_turned"), 1)
            for k in range(KD):
                square_sum_pe(pe, 1, k)
            pe.wait_ge(S("x_dve"), 5)
            pe.wait_ge(S("x_act"), 4)
            pe.wait_ge(S("vcol_ready"), 1)
            arrived = 0
            for n, (sl, kind, i) in enumerate(jobs):
                if n == 0:
                    pe.wait_ge(S("normed"), KD)
                if n >= 2 and evac[n - 2][0]:
                    pe.wait_ge(S("ev_act"), evac[n - 2][0])
                if n >= 2 and evac[n - 2][1]:
                    pe.wait_ge(S("ev_dve"), evac[n - 2][1])
                if kind == "gates":
                    pe.wait_ge(S("wg_in"), 32)
                elif n == 0:
                    pe.wait_ge(S("q_in"), 8 * 16)
                elif sl != jobs[n - 1][0]:
                    pe.wait_ge(S(f"slab_in{sl % 2}"), 16 * (sl // 2 + sl % 2))
                wt = ring[:, sl % 2, :].rearrange("p (k n) -> p k n", k=KD)
                bank, smp = ps[n % 3], ps[3 + n % 2]
                for k in range(KD):
                    on = dict(start=(k == 0), stop=(k == KD - 1))
                    if kind in ("q", "mu", "mo", "gates"):
                        if kind == "gates":
                            w = wg[:, k, :]
                        else:
                            w = wt[:, k, i * P:(i + 1) * P]
                        m = 36 if kind == "gates" else P
                        t.matmul(bank[0:m, :], w, xnT[:, k, 0:SEQ], **on)
                        last = t.matmul(smp[0:m, 0:NSMP], w, xnT[:, k, SEQ:T], **on)
                    else:
                        w = SLABS[sl][1]
                        last = t.matmul(bank[0:TROWS[i], 0:w], xnT[:, k, i * P:i * P + TROWS[i]], wt[:, k, 0:w], **on)
                last.then_inc(S("job"), 1)
            pe.wait_ge(S("ev_act"), evac[-1][0])
            pe.wait_ge(S("ev_dve"), evac[-1][1])
            pe.wait_ge(S("w1_in"), 4 * 16)
            for kvi in range(2):
                for cc in range(16):
                    last = t.matmul(ps[5][:, kvi:kvi + 1], w1c[:, kvi, cc, :],
                                    vcol[:, V_PE + 16 * kvi + cc:V_PE + 16 * kvi + cc + 1],
                                    start=(cc == 0), stop=(cc == 15))
            last.then_inc(S("hb_made"), 1)
            pe.sem_inc(S("c_turned"), 8)
            pe.sem_inc(S("c_mm"), 4)
            pe.sem_inc(S("c_kc"), 4)

            def turn(b, s, n, rows):
                kvi, f = n // 4, n % 4
                ct = packed[0:rows, kvi, :].rearrange("p (h j d) -> p h j d", h=2, j=16)
                if f == 0:
                    pe.wait_ge(S("c_packed"), b * 2 + (kvi + 1))
                if f % 2:
                    pe.wait_ge(S("c_xa"), b * 4 + (n // 2 + 1))
                else:
                    pe.wait_ge(S("c_xd"), b * 4 + (n // 2 + 1))
                for c2 in range(2):
                    for h in range(2):
                        j = 2 * (2 * f + c2)
                        at = (2 * c2 + h) * rows
                        last = t.transpose(ps[f][:, at:at + rows], ct[:, h, j:j + 2, :], ident[0:rows, 0:rows])
                last.then_inc(S("c_turned"), 1)

            def hidden(b, s, n, rows):
                kvi, f = n // 4, n % 4
                if f == 0:
                    pe.wait_ge(S("c_hid"), b * 2 + (kvi + 1))
                if f % 2:
                    pe.wait_ge(S("c_xa"), b * 4 + (n // 2 + 3))
                else:
                    pe.wait_ge(S("c_xd"), b * 4 + (n // 2 + 3))
                nb = rows // 2
                for c2 in range(2):
                    for half in range(2):
                        x = XT[:, f, 2 * c2 * rows:2 * (c2 + 1) * rows].rearrange("p (h n f) -> p h n f", h=2, f=2)[:, :, :, half]
                        last = t.matmul(ps[4 + kvi][:, 0:rows], w1c[:, kvi, half * 8 + 2 * f + c2, :], x,
                                        start=(f == 0 and c2 == 0 and half == 0), stop=(f == 3 and c2 == 1 and half == 1))
                last.then_inc(S("c_mm"), 1)

            def second(b, s, kvi, rows):
                pe.wait_ge(S("c_hid"), b * 2 + (kvi + 3))
                pe.wait_ge(S("c_kcd"), b * 2 + (kvi + 1))
                nb = rows // 2
                for h in range(2):
                    hv = hid[:, s, kvi, h * nb:(h + 1) * nb]
                    if kvi == 0:
                        last = t.matmul(ps[6][64 * h:64 * h + 64, 0:nb], w2c[:, 0, :], hv, start=True, stop=True)
                    else:
                        last = t.matmul(ps[7][64 * s:64 * s + nb, 64 * h:64 * h + 64], hv, w2c[:, 1, :],
                                        start=True, stop=True)
                last.then_inc(S("c_kc"), 1)

            def compress_pe(b, s, rows):
                turn(b, s, 0, rows)
                for n in range(8):
                    if n < 7:
                        turn(b, s, n + 1, rows)
                    hidden(b, s, n, rows)
                    if n == 5:
                        second(b, s, 0, rows)
                second(b, s, 1, rows)

            with pe.Fori(0, NB // 2) as it:
                for s in range(2):
                    compress_pe(it * 2 + s, s, P)
            compress_pe(NB, 0, 32)

            pe.wait_ge(S("c_xa"), 2 + 4 * 9)
            pe.wait_ge(S("c_xd"), 2 + 4 * 9)
            pe.wait_ge(S("c_hid"), 2 + 2 * 9)
            pe.wait_ge(S("c_kcd"), 2 + 2 * 9)
            pe.wait_ge(S("m_mcg"), 1)
            for k in range(MH):
                last = t.transpose(ps[5][0:27, k * P:(k + 1) * P], mcg[:, k, :], ident[:])
            last.then_inc(S("m_mco"), 1)
            pe.wait_ge(S("wqk_in"), 48)

            def project(h):
                if h:
                    pe.wait_ge(S("m_w"), h)
                    pe.wait_ge(S("m_e"), h)
                pe.wait_ge(S("m_uc"), h + 1)
                for w, b in ((0, 0), (1, 2)):
                    t.matmul(ps[b][:, :], wqk[:, w, h, :], ucT[:, h, 0:SEQ], start=True, stop=True)
                    t.matmul(ps[1][:, NSMP * w:NSMP * (w + 1)], wqk[:, w, h, :], ucT[:, h, SEQ:T], start=True, stop=True)
                for i in range(4):
                    t.matmul(ps[4][:, i * P:(i + 1) * P], ucT[:, h, i * P:(i + 1) * P], wqk[:, 1, h, :], start=True, stop=True)
                t.matmul(ps[1][0:NSMP, P:2 * P], ucT[:, h, SEQ:T], wqk[:, 1, h, :], start=True,
                         stop=True).then_inc(S("m_proj"), 1)

            project(0)
            pe.wait_ge(S("m_rows"), 1)
            for kind, row in enumerate((irow, frow, r0)):
                for i in range(NTILE):
                    at = (kind * NTILE + i) * MH
                    t.transpose(ps[3][0:TROWS[i], at:at + MH], row[:, i * P:i * P + TROWS[i]], ident[0:MH, 0:MH])
            t.transpose(ps[3][0:NB, 60:64], r2[:, TS - 1:NSMP:TS], ident[0:MH, 0:MH]).then_inc(S("m_cols"), 1)
            pe.wait_ge(S("m_rcol"), 1)
            for h in range(MH):
                if h:
                    project(h)
                pe.wait_ge(S("m_projd"), h + 1)
                pe.wait_ge(S("m_rows"), 1)
                if h:
                    pe.wait_ge(S("m_x"), h)
                t.matmul(ps[3][:, :], selh[:, h, :], r1[:, 0:SEQ], start=True, stop=True)
                t.matmul(ps[1][0:NSMP, 0:NSMP], selh[:, h, 0:NSMP], r1[:, SEQ:T], start=True, stop=True)
                t.matmul(ps[1][:, NSMP:2 * NSMP], selh[:, h, :], r2[:, 0:NSMP], start=True, stop=True)
                t.matmul(ps[1][:, 2 * NSMP:2 * NSMP + NB], selh[:, h, :], r2[:, TS - 1:NSMP:TS], start=True,
                         stop=True).then_inc(S("m_spread"), 1)
                pe.wait_ge(S("m_proja"), h + 1)
                for j in range(4):
                    out = (ps[0][:, :], ps[2][:, 0:384], ps[4][:, 0:256], ps[4][:, 256:384])[j]
                    t.matmul(out, mkT[:, j * P:(j + 1) * P], mqT[:, j * P:SEQ], start=True, stop=True)
                t.matmul(ps[4][0:NSMP, 384:384 + NSMP], mkT[:, SEQ:T], mqT[:, SEQ:T], start=True,
                         stop=True).then_inc(S("m_qk"), 1)
                pe.wait_ge(S("m_cin"), 16 * (h + 1))
                for x in range(2):
                    if 5 * h + x:
                        pe.wait_ge(S("m_p7d"), 5 * h + x)
                    for b in range(4):
                        last = t.transpose(ps[7][:, b * P:(b + 1) * P], Cst[:, 4 * x + b, :], ident[:])
                    last.then_inc(S("m_p7"), 1)
                pe.wait_ge(S("m_w"), h + 1)
                pe.wait_ge(S("m_p7d"), 5 * h + 2)
                if h:
                    pe.wait_ge(S("m_numd"), h)
                else:
                    pe.wait_ge(S("m_mcod"), 1)
                for i in range(4):
                    out = ps[5][:, i * (P + 1):(i + 1) * (P + 1)] if i < 3 else ps[6][:, 0:P + 1]
                    for j in range(i + 1):
                        at = EOFF[j] + (i - j) * P
                        t.matmul(out, W[:, at:at + P], mv[:, j, h, :], start=(j == 0), stop=(j == i))
                out = ps[6][0:NSMP, P + 1:2 * (P + 1)]
                t.matmul(out, W[0:NSMP, EW:EW + NSMP], mv[0:NSMP, 4, h, :], start=True, stop=False)
                for b in range(NB):
                    last = t.matmul(out, Qm[:, b, :], CT[:, b, :], start=False, stop=(b == NB - 1))
                last.then_inc(S("m_num"), 1)
                pe.wait_ge(S("m_upd"), h + 1)
                for x in range(2):
                    t.matmul(ps[7][:, :], vw[0:NSMP, 4, :], kbd[0:NSMP, 4 * x:4 * x + 4, :].rearrange("p b d -> p (b d)"),
                             start=True, stop=True).then_inc(S("m_p7"), 1)
                    pe.wait_ge(S("m_p7d"), 5 * h + 3 + x)
                for i in range(4):
                    t.matmul(ps[7][:, 0:P], vw[:, i, :], mk[:, i, :], start=(i == 0), stop=(i == 3))
                for i in range(4):
                    t.matmul(ps[7][0:1, P:2 * P], rcol[:, 2, i, h:h + 1], mk[:, i, :], start=(i == 0), stop=(i == 3))
                t.matmul(ps[7][0:NB, 2 * P:3 * P], wlb[0:NSMP, :], mk[0:NSMP, 4, :], start=True,
                         stop=True).then_inc(S("m_p7"), 1)
            pe.wait_ge(S("m_hn"), 1)
            pe.wait_ge(S("m_w"), MH)
            pe.wait_ge(S("m_x"), MH)
            for h in range(MH):
                for i in range(4):
                    t.transpose(ps[h][:, i * P:(i + 1) * P], hs[:, i, h, 0:P], ident[:])
                t.transpose(ps[4 + h][:, 0:NSMP], hs[0:NSMP, 4, h, 0:P],
                            ident[0:NSMP, 0:NSMP]).then_inc(S("m_hT"), 1)

            pe.wait_ge(S("m_mix"), MH)
            for w in range(2):
                for i in range(NTILE):
                    rows = TROWS[i]
                    out = ps[2 * w][:, i * P:(i + 1) * P] if i < 4 else ps[2 * w + 1][:, 0:NSMP]
                    last = t.transpose(out, kv[0:rows, i, 256 + 256 * w:384 + 256 * w], ident[0:rows, 0:rows])
            last.then_inc(S("k_turned"), 1)
            pe.wait_ge(S("k_ready"), 1)
            pe.sem_inc(S("s_sc"), 2)
            with pe.Fori(0, 2) as it:
                for x in range(2):
                    p10 = it * 20 + 10 * x
                    p1 = it * 2 + x
                    kvs = [slots[2 * x], slots[2 * x + 1]]
                    kvw = [wkv[:, 2 * x, :], wkv[:, 2 * x + 1, :]]
                    pe.wait_ge(S("s_stage"), p1 + 1)
                    pe.wait_ge(S("s_out"), p1 + 1)
                    for b2 in range(2):
                        r = slice(64 * b2, 64 * b2 + 64)
                        q = Qp[:, 64 * b2:64 * b2 + 64]
                        for w in range(2):
                            t.matmul(ps[7][r, 8 * w:8 * w + 8], q, ktn[:, w, b2 * TS:(b2 + 1) * TS], start=True, stop=True)
                        last = t.matmul(ps[7][r, 16:80], q, kcp[:, 64 * b2:64 * b2 + 64], start=True, stop=True)
                    last.then_inc(S("s_cmp"), 1)

                    def turn_keys(n):
                        if n == 0:
                            pe.wait_ge(S(f"win_in{x}"), it * 32 + 32)
                        if n == 2:
                            pe.wait_ge(S(f"sel_in{2 * x}"), it * 16 + 16)
                        if n == 6:
                            pe.wait_ge(S(f"sel_in{2 * x + 1}"), it * 16 + 16)
                        if n < 2:
                            src, j0 = kvw[n], 0
                            pe.wait_ge(S("s_kt"), p10 + (n + 0 if n else 1))
                        else:
                            src, j0 = kvs[(n - 2) // 4], 4 * ((n - 2) % 4)
                            pe.wait_ge(S("s_kt"), p10 + n)
                        for j in range(4):
                            last = t.transpose(ps[4 + n % 2][:, j * P:(j + 1) * P],
                                               src[:, (j0 + j) * 256:(j0 + j) * 256 + P], ident[:])
                        last.then_inc(S("s_t"), 1)

                    def score(n):
                        pe.wait_ge(S("s_kt"), p10 + (n + 2))
                        b2 = n if n < 2 else (n - 2) // 4
                        bank = ps[6] if n < 2 else ps[(n - 2) % 4]
                        if n == 2:
                            pe.wait_ge(S("s_pt"), p1 + 1)
                        t.matmul(bank[64 * b2:64 * b2 + 64, :], Qp[:, 64 * b2:64 * b2 + 64], KTb[:, n % 2, :], start=True,
                                 stop=True).then_inc(S("s_sc"), 1)

                    turn_keys(0)
                    for n in range(10):
                        if n < 9:
                            turn_keys(n + 1)
                        score(n)
                        if n == 4:
                            pe.wait_ge(S("s_pn"), p1 + 1)
                            t.matmul(ps[7][:, P:2 * P], gsum[:], pcd, start=True, stop=True)
                            t.transpose(ps[7][:, 2 * P:3 * P], pcd, ident[:]).then_inc(S("s_imp"), 1)
                    pe.wait_ge(S("s_we"), p1 + 1)
                    for j in range(4):
                        t.transpose(ps[6][:, j * P:(j + 1) * P], Sw[:, j * P:(j + 1) * P], ident[:])
                    pe.wait_ge(S("s_pc"), p1 + 1)
                    t.transpose(ps[7][0:TS, P:2 * P], Sw[:, WIN:WIN + TS], ident[:]).then_inc(S("s_wT"), 1)
                    pe.wait_ge(S("s_se"), p1 + 1)
                    for j in range(16):
                        t.transpose(ps[j // 4][:, (j % 4) * P:(j % 4 + 1) * P], Ss[:, j * P:(j + 1) * P], ident[:])
                    t.transpose(ps[5][0:TS, 0:P], Ss[:, PAST:PAST + TS], ident[:]).then_inc(S("s_sT"), 1)
                    pe.wait_ge(S("s_pt"), p1 + 2)
                    t.matmul(ps[4][:, 2 * P:3 * P], vcp, PTc, start=True, stop=True)
                    for b2 in range(2):
                        c = slice(64 * b2, 64 * b2 + 64)
                        for j in range(4):
                            t.matmul(ps[4][:, P + 64 * b2:P + 64 * b2 + 64], kvw[b2][:, j * 256 + P:(j + 1) * 256], PTw[:, j, c],
                                     start=(j == 0), stop=False)
                        t.matmul(ps[4][:, P + 64 * b2:P + 64 * b2 + 64], vnp[:, b2, 1, :], PTn[:, 1, c], start=False, stop=True)
                        for j in range(16):
                            t.matmul(ps[4][:, c], kvs[b2][:, j * 256 + P:(j + 1) * 256], PT[:, j, c], start=(j == 0), stop=False)
                        last = t.matmul(ps[4][:, c], vnp[:, b2, 0, :], PTn[:, 0, c], start=False, stop=True)
                    last.then_inc(S("s_pv"), 1)
                    pe.wait_ge(S("s_ot"), p1 + 1)
                    for w in range(3):
                        last = t.transpose(ps[5][:, w * P:(w + 1) * P], outT[:, w, :], ident[:])
                    last.then_inc(S("s_oT"), 1)
            pe.wait_ge(S("s_out"), 5)
            pe.wait_ge(S("s_pt"), 5)
            for i in range(4):
                for hd in range(HEADS):
                    h, g = hd // GRP, hd % GRP
                    at = (i * GRP + g) * 16
                    last = t.matmul(ps[h][:, at:at + 16], qT[64 * h:64 * h + 64, g, i * P:(i + 1) * P], kcT_p[64 * h:64 * h + 64, :],
                                    start=True, stop=True)
            last.then_inc(S("p_csc"), 1)
            pe.wait_ge(S("p_cn"), 1)
            for i in range(4):
                last = t.transpose(ps[1][:, i * P:(i + 1) * P], Pc[:, i * P:(i + 1) * P], ident[:])
            last.then_inc(S("p_cT"), 1)
            pe.wait_ge(S("p_cTd"), 1)
            pe.wait_ge(S("vbd_in"), HEADS * 16)
            for i in range(4):
                last = t.matmul(ps[2 + i], PcT[:, i, :], Vbd, start=True, stop=True)
            last.then_inc(S("p_co"), 1)
            pe.wait_ge(S("p_cod"), 1)
            pe.sem_inc(S("p_tr"), 2)
            pe.sem_inc(S("p_pv"), 2)
            with pe.Fori(0, GRP) as g:
                for step in range(10):
                    if step < 8:
                        u = step
                        i, h = UNITS[u]
                        n = (i + 1) * P
                        if u == 0:
                            pe.wait_ge(S("p_stage"), g + 1)
                        pe.wait_ge(S("p_exp"), g * 8 + (u + 1))
                        for w in range(2):
                            last = t.matmul(ps[2 * (u % 2) + w][:, 0:n], qst[64 * h:64 * h + 64, i * P:(i + 1) * P],
                                            ktT[64 * h:64 * h + 64, w, 0:n], start=True, stop=True)
                        last.then_inc(S("p_sc"), 1)
                    if 1 <= step < 9:
                        u = step - 1
                        i = UNITS[u][0]
                        pe.wait_ge(S("p_exp"), g * 8 + (u + 3))
                        pe.wait_ge(S("p_pta"), g * 8 + (u + 1))
                        pe.wait_ge(S("p_ptd"), g * 8 + (u + 1))
                        for w in range(2):
                            for j in range(i + 1):
                                last = t.transpose(ps[4 + w][:, j * P:(j + 1) * P], Pb[:, u % 2, w, j * P:(j + 1) * P], ident[:])
                        last.then_inc(S("p_tr"), 1)
                    if step >= 2:
                        u = step - 2
                        i, h = UNITS[u]
                        pe.wait_ge(S("p_pta"), g * 8 + (u + 2))
                        pe.wait_ge(S("p_ptd"), g * 8 + (u + 2))
                        pe.wait_ge(S("p_fin"), g * 8 + (u + 1))
                        for w in range(2):
                            for j in range(i + 1):
                                at = 384 + 256 * w + 64 * h
                                last = t.matmul(ps[6 + u % 2][:, w * HD:(w + 1) * HD], PTp[:, u % 2, w, j * P:(j + 1) * P],
                                                kv[:, j, at:at + HD], start=(j == 0), stop=(j == i))
                        last.then_inc(S("p_pv"), 1)
            pe.wait_ge(S("o_norm"), 1)
            for f in range(4):
                for i in range(4):
                    t.transpose(ps[f][:, i * P:(i + 1) * P], oatt[:, i, f * P:(f + 1) * P], ident[:])
                t.transpose(ps[4 + f][:, 0:NSMP], oatt[0:NSMP, 4, f * P:(f + 1) * P],
                            ident[0:NSMP, 0:NSMP]).then_inc(S("o_turned"), 1)
            pe.wait_ge(S("o_mix"), 4)
            for m in range(KD):
                if m % 4 == 0:
                    pe.wait_ge(S(f"slab_in{m // 4}"), 48 + m // 4 * 16)
                if m >= 2:
                    pe.wait_ge(S("h_done"), m - 1)
                wt = ring[:, m // 4, :].rearrange("p (k n) -> p k n", k=KD)
                for k in range(KD):
                    w = wt[:, k, (m % 4) * P:(m % 4 + 1) * P]
                    t.matmul(ps[m % 2], w, xnT[:, k, 0:SEQ], start=(k == 0), stop=(k == KD - 1))
                    last = t.matmul(ps[2 + m % 2][:, 0:NSMP], w, xnT[:, k, SEQ:T], start=(k == 0), stop=(k == KD - 1))
                last.then_inc(S("h_mm"), 1)
            for k in range(KD):
                square_sum_pe(pe, 2, k)
            pe.wait_ge(S("h_done"), KD)
            pe.wait_ge(S("normed"), 2 * KD)

            def up_pe(slot, sub, par, qn):
                wt = ring[:, slot, :].rearrange("p (w k n) -> p w k n", w=2, k=KD)
                pe.wait_ge(S("u_pad"), qn + 1)
                pe.wait_ge(S("u_smp"), qn + 1)
                pe.wait_ge(S("u_fc"), qn + 1)
                for w in range(2):
                    for k in range(KD):
                        if w == 0 and k == 1:
                            for z in range(2):
                                last = t.transpose(ps[6][:, 32 * z:32 * z + 19], fin[:, slot, z, sub * P:(sub + 1) * P],
                                                   ident[0:19, 0:19])
                            last.then_inc(S("u_ft"), 1)
                        wk = wt[:, w, k, sub * P:(sub + 1) * P]
                        t.matmul(ps[2 * w + par], wk, xnT[:, k, 0:SEQ], start=(k == 0), stop=(k == KD - 1))
                        last = t.matmul(ps[4 + par][:, w * NSMP:(w + 1) * NSMP], wk, xnT[:, k, SEQ:T],
                                        start=(k == 0 and w == 0), stop=(k == KD - 1), skip_group_check=True)
                last.then_inc(S("u_mm"), 1)

            def last_cols(qn):
                pe.wait_ge(S("u_l18"), qn + 1)
                pe.wait_ge(S("u_fo"), qn + 1)
                for w in range(2):
                    last = t.transpose(ps[7][0:18, w * P:(w + 1) * P], l18[:, w, :], ident[:])
                last.then_inc(S("u_lT"), 1)

            pe.wait_ge(S("slab_in0"), 48 + 64)
            up_pe(0, 0, 0, 0)
            with pe.Fori(0, 5) as it:
                for q in range(4):
                    if q == 1:
                        pe.wait_ge(S("slab_in1"), it * 64 + (64 + 64))
                    if q == 3:
                        pe.wait_ge(S("slab_in0"), it * 64 + (48 + 128))
                    up_pe((q + 1) // 2 % 2, (q + 1) % 2, (q + 1) % 2, it * 4 + (q + 1))
                    last_cols(it * 4 + q)
            up_pe(0, 1, 1, 21)
            last_cols(20)
            last_cols(21)
            pe.wait_ge(S("u_act"), NFF + 1)
            pe.sem_inc(S("d_mm"), 1)

            def down_pe(s, mn, first):
                pe.wait_ge(S(f"dn_in{s}"), first)
                pe.wait_ge(S("d_done0"), mn + 1)
                for k in range(NFF):
                    w = wdn[:, s, k, :]
                    a0 = actT[:, k, SEQ + 2:FVW]
                    smp = bass.AP(a0.tensor, a0.offset, [list(a0.ap[0]), [2 + TS, NB], [1, TS]])
                    t.matmul(ps[s], w, actT[:, k, 0:SEQ], start=(k == 0), stop=(k == NFF - 1))
                    last = t.matmul(ps[2 + s][:, 0:NSMP], w, smp, start=(k == 0), stop=(k == NFF - 1))
                last.then_inc(S("d_mm"), 1)

            with pe.Fori(0, KD // 2) as it:
                for s in range(2):
                    down_pe(s, it * 2 + s, it * 16 + 16)
            for k in range(KD):
                square_sum_pe(pe, 3, k)
            for n in range(10):
                i, half = n // 2, n % 2
                if half == 0:
                    pe.wait_ge(S("normed"), 3 * KD)
                if n >= 6:
                    if n % 2 == 0:
                        pe.wait_ge(S("y_act"), n // 2 - 2)
                    else:
                        pe.wait_ge(S("y_dve"), n // 2 - 2)
                rows = TROWS[i]
                for f in range(4):
                    k = 4 * half + f
                    last = t.transpose(ps[n % 6][0:rows, f * P:(f + 1) * P], xnT[:, k, i * P:i * P + rows], ident[:])
                last.then_inc(S("y_turned"), 1)


        @block.vector
        def _(dve):
            v = nc.vector
            links = [0]

            def link(ins):
                links[0] += 1
                ins.then_inc(S("v_link"), 1)
                dve.wait_ge(S("v_link"), links[0])

            dve.wait_ge(S("numbers"), 1)
            dve.wait_ge(S("idx_in"), NB * 16)
            part = b1["part"].bitcast(I32)
            link(v.tensor_scalar(part[:, 1:2], part[:, 0:1], 7, None, ALU.bitwise_and))
            link(v.tensor_copy(small[:, 1:2], part[:, 1:2]))
            v.tensor_scalar(idx[:], idx[:], 8.0, small[:, 1:2], ALU.mult, ALU.add).then_inc(S("idx_ready"), 1)
            v.tensor_scalar(winmask[:], b1["wrow"].bitcast(I32), small[:, 1:2], NEG, ALU.is_le, ALU.mult)
            v.tensor_scalar(newmask[:], b1["newk"].bitcast(I32), small[:, 1:2], NEG, ALU.is_gt, ALU.mult)
            dve.wait_ge(S("band"), 1)
            v.scalar_tensor_tensor(out=gsum[:], in0=b1["mod"].bitcast(I32), scalar=small[:, 1:2], in1=gsum[:],
                                   op0=ALU.is_equal, op1=ALU.mult)
            dve.wait_ge(S("vec_turned"), 1)
            v.tensor_copy(vcol[:], ps[0][:, 0:V_COLS]).then_inc(S("vcol_ready"), 1)
            for k in range(0, KD, 2):
                dve.wait_ge(S("x_turned"), k + 1)
                v.tensor_copy(xT[:, k, 0:SEQ], ps[1 + k % 4][:, :]).then_inc(S("x_dve"), 1)
            dve.wait_ge(S("x_turned"), KD)
            v.tensor_copy(xT[:, :, SEQ:T], ps[5][:, :].rearrange("p (k t) -> p k t", k=KD)).then_inc(S("x_dve"), 1)
            dve.wait_ge(S("x_dve"), 5)
            dve.wait_ge(S("x_act"), 4)
            dve.wait_ge(S("vcol_ready"), 1)
            norm_dve(dve, 1, xT, xnT, V_GMIX)
            dve.wait_ge(S("padded"), 1)
            for n, (_, kind, i) in enumerate(jobs):
                bank, smp = ps[n % 3], ps[3 + n % 2]
                rows = TROWS[i]
                if kind in ("q", "mu", "gates") or (kind in ("kvA", "mv") and i % 2 == 0):
                    dve.wait_ge(S("job"), n + 1)
                if kind == "q":
                    sv = smp[:, 0:NSMP]
                    v.tensor_copy(qT[:, i, SEQ:T], sv)
                    for h in range(KVH):
                        last = v.tensor_copy(Qbd[64 * h:64 * h + 64, :, h * 32 + i * TS:h * 32 + i * TS + TS],
                                             sv[64 * h:64 * h + 64, :].rearrange("p (b t) -> p b t", b=NB))
                    last.then_inc(S("ev_dve"), 1)
                elif kind == "mu":
                    uv = uT[:, i, 3 + SEQ:UPW].rearrange("p (b t) -> p b t", b=NB)
                    v.tensor_copy(uv[:, :, 0:3],
                                  vcol[:, V_MCS + 24 * i:V_MCS + 24 * i + 24].rearrange("p (b j) -> p b j", b=NB))
                    v.tensor_copy(uv[:, :, 3:3 + TS],
                                  smp[:, 0:NSMP].rearrange("p (b t) -> p b t", b=NB)).then_inc(S("ev_dve"), 1)
                elif kind == "gates":
                    v.tensor_scalar(irow[:, 0:SEQ], bank[0:MH, :], gb[:, 0:1], None, ALU.add)
                    v.tensor_scalar(irow[:, SEQ:T], smp[0:MH, 0:NSMP], gb[:, 0:1], None, ALU.add)
                    v.tensor_copy(frow[:, 0:SEQ], bank[32:32 + MH, :])
                    v.tensor_copy(frow[:, SEQ:T], smp[32:32 + MH, 0:NSMP]).then_inc(S("ev_dve"), 1)
                elif kind == "kvA" and i % 2 == 0:
                    v.tensor_copy(kv[0:rows, i, 0:512], bank[0:rows, :]).then_inc(S("ev_dve"), 1)
                elif kind == "mv" and i % 2 == 0:
                    v.tensor_copy(mv[0:rows, i, :, 0:P],
                                  bank[0:rows, :].rearrange("p (h e) -> p h e", h=MH)).then_inc(S("ev_dve"), 1)
            dve.sem_inc(S("c_xd"), 2)
            dve.sem_inc(S("c_kcd"), 2)

            def pack(b, slot, kvi, rows):
                src = ring[0:rows, slot, :].rearrange("p (j k h d) -> p j k h d", j=16, k=2, h=2)
                dst = packed[0:rows, kvi, :].rearrange("p (h j d) -> p h j d", h=2, j=16)
                dve.wait_ge(S("c_turned"), b * 8 + 4 * (kvi + 1))
                v.tensor_copy(dst, src[:, :, kvi, :, :].rearrange("p j h d -> p h j d")).then_inc(S("c_packed"), 1)

            def compress_dve(b, s, w, kdst, vdst, follow):
                nb = w // 2
                for kvi in range(2):
                    for f in (0, 2):
                        n = b * 8 + (4 * kvi + f)
                        dve.wait_ge(S("c_turned"), n + 9)
                        dve.wait_ge(S("c_mm"), n + 1)
                        v.tensor_copy(XT[:, f, 0:4 * w], ps[f][:, 0:4 * w]).then_inc(S("c_xd"), 1)
                    follow(kvi)
                dve.wait_ge(S("c_kc"), b * 2 + 5)
                v.tensor_copy(kdst, ps[6][:, 0:nb]).then_inc(S("c_kcd"), 1)
                dve.wait_ge(S("c_kc"), b * 2 + 6)
                v.tensor_copy(vdst, ps[7][64 * s:64 * s + nb, 0:P]).then_inc(S("c_kcd"), 1)

            def past(it, s, follow):
                compress_dve(it * 2 + s, s, P, kcT_s[:, bass.ds(it, 1), 64 * s:64 * s + 64],
                             vc_s[64 * s:64 * s + 64, bass.ds(it, 1), :], follow)

            def next_batch(it, s):
                def follow(kvi):
                    if kvi == 0:
                        dve.wait_ge(S(f"rows_in{1 - s}"), (it + 1 + s) * 16)
                    pack(it * 2 + (s + 1), 1 - s, kvi, P)
                return follow

            def own_rows(kvi):
                if kvi == 0:
                    dve.wait_ge(S("own_in"), 4 * 16)
                pack(NB, 0, kvi, 32)

            dve.wait_ge(S("job"), len(jobs))
            dve.wait_ge(S("rows_in0"), 16)
            pack(0, 0, 0, P)
            pack(0, 0, 1, P)
            with dve.Fori(0, NB // 2 - 1) as it:
                for s in range(2):
                    past(it, s, next_batch(it, s))
            past(NB // 2 - 1, 0, next_batch(NB // 2 - 1, 0))
            past(NB // 2 - 1, 1, own_rows)
            compress_dve(NB, 0, 32, kcT_p[:, :], vc_p[:, :], lambda kvi: None)

            for k in range(MH):
                if k >= 2:
                    dve.wait_ge(S("m_uc"), k - 1)
                wc = V_WCONV + k
                cv = conv[:, k % 2, :]
                link(v.tensor_scalar(cv, uT[:, k, 0:CVW], vcol[:, wc:wc + 1], None, ALU.mult))
                for j in range(1, 4):
                    ins = v.scalar_tensor_tensor(out=cv, in0=uT[:, k, j:j + CVW], scalar=vcol[:, wc + 4 * j:wc + 4 * j + 1],
                                                 in1=cv, op0=ALU.mult, op1=ALU.add)
                    if j < 3:
                        link(ins)
                ins.then_inc(S("m_conv"), 1)
            for k in range(MH):
                v.tensor_copy(mcg[:, k, 0:3], uT[:, k, SEQ:SEQ + 3])
                last = v.tensor_copy(mcg[:, k, 3:27].rearrange("p (b j) -> p b j", b=NB),
                                     uT[:, k, 3 + SEQ:UPW].rearrange("p (b t) -> p b t", b=NB)[:, :, TS:TS + 3])
            last.then_inc(S("m_mcg"), 1)
            starts = slice(SEQ, T, TS)
            v.memset(restart, 1.0)
            link(v.memset(down, 0.0))
            v.memset(restart[:, starts], 0.0)
            v.memset(down[:, starts], NEG)
            link(v.tensor_scalar(frow, frow, gb[:, 1:2], None, ALU.add))
            v.scalar_tensor_tensor(out=r0, in0=frow, scalar=-1.0, in1=frow, op0=ALU.mult, op1=ALU.max).then_inc(S("m_abs"), 1)
            dve.wait_ge(S("m_ln"), 2)
            link(v.scalar_tensor_tensor(out=frow, in0=frow, scalar=0.0, in1=r0, op0=ALU.min, op1=ALU.subtract))
            link(v.tensor_tensor_scan(r1, restart, frow, 0.0, ALU.mult, ALU.add))
            link(v.tensor_tensor(irow, irow, r1, ALU.subtract))
            link(v.tensor_copy(r0, irow))
            link(v.tensor_tensor(r0[:, starts], r0[:, starts], m0[:, :], ALU.max))
            link(v.tensor_tensor_scan(r2, down, r0, 0.0, ALU.add, ALU.max))
            link(v.tensor_tensor(r3, r1, r2, ALU.add))
            link(v.tensor_scalar(r1, r2, -1.0, None, ALU.mult))
            negm = r1[:, SEQ:T].rearrange("p (b t) -> p b t", b=NB)
            v.tensor_scalar(r0[:, 0:SEQ], irow[:, 0:SEQ], r1[:, SEQ - 1:SEQ], None, ALU.add)
            v.tensor_tensor(r0[:, SEQ:T].rearrange("p (b t) -> p b t", b=NB),
                            irow[:, SEQ:T].rearrange("p (b t) -> p b t", b=NB),
                            negm[:, :, TS - 1:TS].to_broadcast([MH, NB, TS]), ALU.add)
            v.tensor_tensor(r2[:, 0:NSMP].rearrange("p (b t) -> p b t", b=NB), negm,
                            m0[:, :].unsqueeze(2).to_broadcast([MH, NB, TS]), ALU.add).then_inc(S("m_pre"), 1)
            v.memset(Qm, 0.0)
            v.memset(a4["rcol"], 0.0)
            v.memset(s2, 1.0)
            link(v.memset(hs[64:128, 4, :, :], 1.0))
            dve.wait_ge(S("m_mco"), 1)
            v.tensor_copy(mco, ps[5][0:27, :]).then_inc(S("m_mcod"), 1)

            def projected(h):
                dve.wait_ge(S("m_proj"), h + 1)
                v.tensor_copy(mqT[:, SEQ:T], ps[1][:, 0:NSMP])
                v.tensor_scalar(mkT[:, SEQ:T], ps[1][:, NSMP:2 * NSMP], KSCALE, None, ALU.mult)
                v.tensor_scalar(mk[0:NSMP, 4, :], ps[1][0:NSMP, P:2 * P], KSCALE, None, ALU.mult)
                if h:
                    dve.wait_ge(S("m_p7"), 5 * h)
                v.tensor_scalar(mk[:, 0:4, :], ps[4][:, :].rearrange("p (i d) -> p i d", i=4), KSCALE, None,
                                ALU.mult).then_inc(S("m_projd"), 1)

            projected(0)
            dve.wait_ge(S("m_cols"), 1)
            kinds = ps[3][:, 0:60].rearrange("p (k i h) -> p k i h", k=3, i=NTILE)
            v.tensor_copy(rcol[:, :, 0:4, :], kinds[:, :, 0:4, :])
            v.tensor_copy(rcol[0:NSMP, :, 4, :], kinds[0:NSMP, :, 4, :])
            v.tensor_copy(slcol, ps[3][0:NB, 60:64]).then_inc(S("m_rcol"), 1)
            dve.wait_ge(S("m_rcol"), 1)
            dve.wait_ge(S("wqk_in"), 48)
            bmask = smask[0:NSMP, TS - 1:NSMP:TS]
            for h in range(MH):
                if h:
                    projected(h)
                dve.wait_ge(S("m_spread"), h + 1)
                qd = Qm[:, 0, 0:1]
                dst = bass.AP(qd.tensor, qd.offset, [list(qd.ap[0]), [NSMP + TS, NB], [1, TS]])
                v.tensor_tensor(dst, mqT[:, SEQ:T].rearrange("p (b t) -> p b t", b=NB),
                                ps[1][:, NSMP:2 * NSMP].rearrange("p (b t) -> p b t", b=NB), ALU.mult)
                v.tensor_copy(slc, ps[1][:, 2 * NSMP:2 * NSMP + NB])
                for j in range(4):
                    v.scalar_tensor_tensor(out=E[:, EOFF[j]:EOFF[j] + P], in0=ps[3][:, j * P:(j + 1) * P],
                                           scalar=rcol[:, 0, j, h:h + 1], in1=causalT[:], op0=ALU.add, op1=ALU.add)
                v.scalar_tensor_tensor(out=E[0:NSMP, EW:EW + NSMP], in0=ps[1][0:NSMP, 0:NSMP],
                                       scalar=rcol[0:NSMP, 0, 4, h:h + 1], in1=smask[0:NSMP, :], op0=ALU.add,
                                       op1=ALU.add).then_inc(S("m_e"), 1)
                v.tensor_copy(CT[:, :, P], vcol[:, V_N + h:V_N + 32:MH])
                for x in range(2):
                    dve.wait_ge(S("m_p7"), 5 * h + x + 1)
                    v.tensor_copy(CT[:, 4 * x:4 * x + 4, 0:P],
                                  ps[7][:, :].rearrange("p (b e) -> p b e", b=4)).then_inc(S("m_p7d"), 1)
                dve.wait_ge(S("m_x"), h + 1)
                dve.wait_ge(S("m_qk"), h + 1)
                if h:
                    dve.wait_ge(S("m_sq"), h)
                v.tensor_tensor(W[:, 0:512], E[:, 0:512], ps[0][:, :], ALU.mult)
                v.tensor_tensor(W[:, 512:896], E[:, 512:896], ps[2][:, 0:384], ALU.mult)
                v.tensor_tensor(W[:, 896:EW], E[:, 896:EW], ps[4][:, 0:384], ALU.mult)
                v.tensor_tensor(W[0:NSMP, EW:EW + NSMP], E[0:NSMP, EW:EW + NSMP], ps[4][0:NSMP, 384:384 + NSMP],
                                ALU.mult).then_inc(S("m_w"), 1)
                v.tensor_tensor(vw[:, 0:4, :], mv[:, 0:4, h, 0:P],
                                rcol[:, 2, 0:4, h:h + 1].to_broadcast([P, 4, P]), ALU.mult)
                v.tensor_scalar(vw[0:NSMP, 4, :], mv[0:NSMP, 4, h, 0:P], rcol[0:NSMP, 2, 4, h:h + 1], None, ALU.mult)
                v.tensor_scalar(wlb[0:NSMP, :], bmask, 0.0, rcol[0:NSMP, 2, 4, h:h + 1], ALU.is_equal, ALU.mult)
                v.scalar_tensor_tensor(out=kbd[0:NSMP, :, :], in0=bmask.unsqueeze(2).to_broadcast([NSMP, NB, P]), scalar=0.0,
                                       in1=mk[0:NSMP, 4:5, :].to_broadcast([NSMP, NB, P]), op0=ALU.is_equal,
                                       op1=ALU.mult).then_inc(S("m_upd"), 1)
                dve.wait_ge(S("m_num"), h + 1)
                v.tensor_copy(hs[:, 0:3, h, :], ps[5][:, 0:3 * (P + 1)].rearrange("p (i e) -> p i e", i=3))
                v.tensor_copy(hs[:, 3, h, :], ps[6][:, 0:P + 1])
                v.tensor_copy(hs[0:NSMP, 4, h, :], ps[6][0:NSMP, P + 1:2 * (P + 1)]).then_inc(S("m_numd"), 1)
                for x in range(2):
                    dve.wait_ge(S("m_p7"), 5 * h + 3 + x)
                    for b in range(4):
                        last = v.scalar_tensor_tensor(out=Cst[:, 4 * x + b, :], in0=Cst[:, 4 * x + b, :],
                                                      scalar=slc[:, 4 * x + b:4 * x + b + 1], in1=ps[7][:, b * P:(b + 1) * P],
                                                      op0=ALU.mult, op1=ALU.add)
                    last.then_inc(S("m_p7d"), 1)
                dve.wait_ge(S("m_p7"), 5 * h + 5)
                v.tensor_copy(cpo[:, h, :], ps[7][:, 0:P])
                v.tensor_copy(npo[:, h * P:(h + 1) * P], ps[7][0:1, P:2 * P])
                v.scalar_tensor_tensor(out=nbh[:, h * P:(h + 1) * P], in0=nbh[:, h * P:(h + 1) * P],
                                       scalar=slcol[:, h:h + 1], in1=ps[7][0:NB, 2 * P:3 * P], op0=ALU.mult,
                                       op1=ALU.add).then_inc(S("m_p7d"), 1)
            den = hs[:, :, :, P]
            sh = lambda x: x.rearrange("p (i h) -> p i h", i=NTILE)
            dve.wait_ge(S("m_numd"), MH)
            link(v.tensor_scalar(sh(f1), den, -1.0, None, ALU.mult))
            link(v.tensor_tensor(sh(f1), sh(f1), den, ALU.max))
            link(v.tensor_tensor(sh(f1), sh(f1), rcol[:, 1, :, :], ALU.max))
            link(v.reciprocal(f1, f1))
            dve.wait_ge(S("m_sq"), MH)
            link(v.tensor_tensor(f3, f1, f1, ALU.mult))
            v.tensor_tensor(f2, f3, s2, ALU.mult).then_inc(S("m_ms"), 1)
            dve.wait_ge(S("m_root"), 1)
            link(v.reciprocal(f3, f2))
            link(v.tensor_tensor(f1, f1, f3, ALU.mult))
            for i in range(NTILE):
                last = v.tensor_tensor(hs[:, i, :, 0:P], hs[:, i, :, 0:P],
                                       sh(f1)[:, i, :].unsqueeze(2).to_broadcast([P, MH, P]), ALU.mult)
            last.then_inc(S("m_hn"), 1)
            for h in range(MH):
                last = v.tensor_scalar(ucT[:, h, :], ucT[:, h, :], vcol[:, V_SKIP + h:V_SKIP + h + 1], None, ALU.mult)
            link(last)
            dve.wait_ge(S("m_stored"), 6 * 16)
            for h in range(MH):
                dve.wait_ge(S("m_hT"), h + 1)
                gh = vcol[:, V_GHEAD + h:V_GHEAD + h + 1]
                v.scalar_tensor_tensor(out=xnT[:, h, 0:SEQ], in0=ps[h][:, :], scalar=gh, in1=ucT[:, h, 0:SEQ],
                                       op0=ALU.mult, op1=ALU.add)
                link(v.scalar_tensor_tensor(out=xnT[:, h, SEQ:T], in0=ps[4 + h][:, 0:NSMP], scalar=gh,
                                            in1=ucT[:, h, SEQ:T], op0=ALU.mult, op1=ALU.add))
                v.tensor_tensor(xnT[:, h, :], xnT[:, h, :], moT[:, h, :], ALU.mult).then_inc(S("m_mix"), 1)

            dve.wait_ge(S("k_turned"), 1)
            for w in range(2):
                v.tensor_copy(ktT[:, w, 0:SEQ], ps[2 * w])
                last = v.tensor_copy(ktT[:, w, SEQ:T], ps[2 * w + 1][:, 0:NSMP])
            last.then_inc(S("k_ready"), 1)
            v.memset(pcd, 0.0)
            v.memset(col[:, 6:7], 1.0)
            link(v.memset(pri[:, 0, :], PRIORITY))
            dve.sem_inc(S("s_pt"), 1)
            dve.sem_inc(S("s_out"), 1)
            dve.wait_ge(S("m_cin"), (MH + NB) * 16)
            s_links = [0]

            def slink(ins, n=[0]):
                s_links[0] += 1
                ins.then_inc(S("v_link"), 1)
                dve.wait_ge(S("v_link"), base + s_links[0])

            PL = 12
            with dve.Fori(0, 2) as it:
                for x in range(2):
                    p10 = it * 20 + 10 * x
                    p1 = it * 2 + x
                    base = it * (2 * PL) + (PL * x + links[0])
                    s_links[0] = 0
                    v.tensor_copy(Qp.rearrange("p (b r) -> p b r", b=2), Qbd[:, bass.ds(it * 4 + 2 * x, 2), :])
                    v.tensor_copy(vcp.unsqueeze(1), vc_s[:, bass.ds(p1, 1), :])
                    v.tensor_copy(kcp.unsqueeze(1), kcT_s[:, bass.ds(p1, 1), :])
                    v.tensor_copy(ktn, ktT[:, :, bass.ds(it * 32 + (16 * x + SEQ), 2 * TS)])
                    v.tensor_copy(vnp, vnew[:, bass.ds(it * 4 + 2 * x, 2), :, :]).then_inc(S("s_stage"), 1)
                    dve.wait_ge(S("s_cmp"), p1 + 1)
                    v.tensor_tensor(Ss[:, PAST:PAST + TS], ps[7][:, 0:8], newmask[:], ALU.add)
                    v.tensor_tensor(Sw[:, WIN:WIN + TS], ps[7][:, 8:16], newmask[:], ALU.add)
                    slink(v.reduce_max(col[:, 0:1], ps[7][:, 16:80], AX.X))
                    v.tensor_scalar(col[:, 0:1], col[:, 0:1], -SCALE, None, ALU.mult).then_inc(S("s_cb"), 1)
                    dve.wait_ge(S("s_ce"), p1 + 1)
                    slink(v.reciprocal(col[:, 1:2], col[:, 1:2]))
                    v.tensor_scalar(pcd, pcd, col[:, 1:2], None, ALU.mult).then_inc(S("s_pn"), 1)
                    dve.wait_ge(S("s_sc"), p10 + 4)
                    slink(v.tensor_tensor(Sw[:, 0:WIN], ps[6], winmask[:], ALU.add))
                    slink(v.reduce_max(col[:, 2:3], Sw, AX.X))
                    v.tensor_scalar(col[:, 2:3], col[:, 2:3], -SCALE, None, ALU.mult).then_inc(S("s_wb"), 1)
                    dve.wait_ge(S("s_imp"), p1 + 1)
                    v.tensor_copy(PTc, ps[7][:, 2 * P:3 * P])
                    imp = ps[7][:, P:2 * P].rearrange("p (f j o) -> p j f o", f=2, o=2)
                    slink(v.tensor_reduce(pri[:, 0, 1:NSEL - 1],
                                          imp[:, 1:NSEL - 1], AX.XY, ALU.add))
                    v.memset(col[:, 10:11], 0.0)
                    slink(v.max(top[:, 0, :], pri[:, 0, :]))
                    v.memset(col[:, 11:12], 0.0)
                    slink(v.match_replace(pri[:, 1, :], top[:, 0, :], pri[:, 0, :], -1.0))
                    v.memset(col[:, 12:13], 0.0)
                    slink(v.max(top[:, 1, :], pri[:, 1, :]))
                    v.memset(col[:, 13:14], 0.0)
                    slink(v.match_replace(pri[:, 2, :], top[:, 1, :], pri[:, 1, :], -1.0))
                    v.tensor_scalar(add, pri[:, 2, :], 0.0, NEG, ALU.is_ge, ALU.mult).then_inc(S("s_pc"), 1)
                    dve.wait_ge(S("s_pc"), p1 + 1)
                    for f in range(4):
                        dve.wait_ge(S("s_sc"), p10 + (2 + 2 + 4 + f + 1))
                        out = Ss[:, f * 512:(f + 1) * 512].rearrange("p (j n o) -> p j n o", j=4, o=4)
                        last = v.tensor_tensor(out, ps[f].rearrange("p (j n o) -> p j n o", j=4, o=4),
                                               add[:, 0:NSEL].unsqueeze(1).unsqueeze(3).to_broadcast([P, 4, NSEL, 4]), ALU.add)
                    slink(last)
                    slink(v.reduce_max(col[:, 3:4], Ss, AX.X))
                    v.tensor_scalar(col[:, 3:4], col[:, 3:4], -SCALE, None, ALU.mult).then_inc(S("s_sb"), 1)
                    dve.wait_ge(S("s_wT"), p1 + 1)
                    v.tensor_copy(a5["PTw"], ps[6])
                    v.tensor_copy(PTn[:, 1, :], ps[7][0:TS, P:2 * P])
                    dve.wait_ge(S("s_sT"), p1 + 1)
                    for f in range(4):
                        v.tensor_copy(PT[:, 4 * f:4 * f + 4, :].rearrange("p j r -> p (j r)"), ps[f])
                    v.tensor_copy(PTn[:, 0, :], ps[5][0:TS, 0:P]).then_inc(S("s_pt"), 1)
                    slink(v.reciprocal(col[:, 8:10], col[:, 4:6]))
                    dve.wait_ge(S("s_oT"), p1 + 1)
                    dve.wait_ge(S("s_sto"), p1 * 16 + 16)
                    for q in range(4):
                        r, c0 = slice(32 * q, 32 * q + 32), 64 * (q % 2)
                        ov = ps[5][r, 0:3 * P].rearrange("p (w d) -> p w d", w=3)[:, :, c0:c0 + HD]
                        v.tensor_tensor(orow[r, 0:2, :], ov[:, 0:2, :], col[r, 8:10].unsqueeze(2).to_broadcast([32, 2, HD]), ALU.mult)
                        last = v.tensor_copy(orow[r, 2, :], ov[:, 2, :])
                    last.then_inc(S("s_out"), 1)
                    assert s_links[0] == PL
            links[0] += 4 * PL
            dve.wait_ge(S("s_pv"), 4)
            v.memset(Vbd, 0.0).then_inc(S("vbd_zero"), 1)
            dve.wait_ge(S("p_csc"), 1)
            dve.wait_ge(S("p_cmk"), 1)
            pcv = Pc.rearrange("p (i h n) -> p i h n", i=4, n=16)
            pcu = Pc.rearrange("p (u n) -> p u n", n=16)
            for h in range(KVH):
                last = v.tensor_tensor(pcv[:, :, GRP * h:GRP * (h + 1), :],
                                       ps[h][:, 0:256].rearrange("p (i g n) -> p i g n", i=4, n=16),
                                       cmk.unsqueeze(2).to_broadcast([P, 4, GRP, 16]), ALU.add)
            link(last)
            link(v.tensor_reduce(cm[:, 0, :], pcu, AX.X, ALU.max))
            v.tensor_tensor(pcu, pcu, cm[:, 0, :].unsqueeze(2).to_broadcast([P, 32, 16]), ALU.subtract).then_inc(S("p_csub"), 1)
            dve.wait_ge(S("p_cexp"), 1)
            link(v.tensor_reduce(cm[:, 0, :], pcu, AX.X, ALU.add))
            link(v.reciprocal(cm[:, 1, :], cm[:, 0, :]))
            link(v.tensor_scalar(cm[:, 1, 0:HEADS], cm[:, 1, 0:HEADS], small[:, 4:5], None, ALU.mult))
            v.tensor_tensor(pcu, pcu, cm[:, 1, :].unsqueeze(2).to_broadcast([P, 32, 16]), ALU.mult).then_inc(S("p_cn"), 1)
            dve.wait_ge(S("p_cT"), 1)
            v.tensor_copy(b6["PcT"], ps[1]).then_inc(S("p_cTd"), 1)
            dve.wait_ge(S("p_co"), 1)
            gv = gsig[:, :, :].rearrange("p i (h w) -> p i h w", w=3)
            for i in range(4):
                last = v.tensor_tensor(oatt[:, i, :].rearrange("p (h d) -> p h d", h=HEADS),
                                       ps[2 + i].rearrange("p (h d) -> p h d", h=HEADS),
                                       gv[:, i, :, 0:1].to_broadcast([P, HEADS, HD]), ALU.mult)
            last.then_inc(S("p_cod"), 1)
            dve.wait_ge(S("p_cod"), 1)
            dve.sem_inc(S("p_ptd"), 1)
            dve.sem_inc(S("p_fin"), 2)
            g4 = gsig[:, 0:4, :].rearrange("p i (h g w) -> p i h g w", h=KVH, g=GRP)
            o4 = oatt[:, 0:4, :].rearrange("p i (h g d) -> p i h g d", h=KVH, g=GRP)
            GL = 8 * 6
            with dve.Fori(0, GRP) as g:
                done = [0]

                def glink(ins):
                    done[0] += 1
                    ins.then_inc(S("v_link"), 1)
                    dve.wait_ge(S("v_link"), g * GL + (links[0] + done[0]))

                v.tensor_copy(qst.unsqueeze(1), qT[:, bass.ds(g, 1), 0:SEQ])
                for h in range(KVH):
                    for i in range(4):
                        last = v.tensor_copy(gst[:, i, h, :].unsqueeze(1), g4[:, i, h, bass.ds(g, 1), 1:3])
                last.then_inc(S("p_stage"), 1)
                dve.wait_ge(S("p_stage"), g + 1)
                for step in range(10):
                    if step < 8:
                        u = step
                        i, h = UNITS[u]
                        both = banks[:, 2 * (u % 2):2 * (u % 2) + 2, :]
                        dve.wait_ge(S("p_sc"), g * 8 + (u + 1))
                        dg = both[:, :, i * P:(i + 1) * P]
                        glink(v.tensor_tensor(dg, dg, causal[:, :].unsqueeze(1).to_broadcast([P, 2, P]), ALU.add))
                        glink(v.tensor_reduce(cst[:, u % 2, 0, :], both[:, :, 0:(i + 1) * P], AX.X, ALU.max))
                        v.tensor_scalar(cst[:, u % 2, 1, :], cst[:, u % 2, 0, :], -SCALE, None, ALU.mult).then_inc(S("p_max"), 1)
                    if 1 <= step < 9:
                        u = step - 1
                        n = (UNITS[u][0] + 1) * P
                        dve.wait_ge(S("p_tr"), g * 8 + (u + 3))
                        dve.wait_ge(S("p_pv"), g * 8 + (u + 1))
                        v.tensor_copy(PTp[:, u % 2, 0, 0:n], ps[4][:, 0:n]).then_inc(S("p_ptd"), 1)
                        glink(v.reciprocal(cst[:, u % 2, 3, :], cst[:, u % 2, 2, :]))
                        i, h = UNITS[u]
                        glink(v.tensor_tensor(cst[:, u % 2, 3, :], cst[:, u % 2, 3, :], gst[:, i, h, :], ALU.mult))
                    if step >= 2:
                        u = step - 2
                        i, h = UNITS[u]
                        dve.wait_ge(S("p_pv"), g * 8 + (u + 3))
                        glink(v.tensor_tensor(tmp[:, u % 2, :, :], ps[6 + u % 2][:, 0:2 * HD].rearrange("p (w d) -> p w d", w=2),
                                              gfac(u % 2), ALU.mult))
                        dst = o4[:, i, h, bass.ds(g, 1), :]
                        glink(v.tensor_tensor(dst, dst, tmp[:, u % 2, 0:1, :], ALU.add))
                        v.tensor_tensor(dst, dst, tmp[:, u % 2, 1:2, :], ALU.add).then_inc(S("p_fin"), 1)
                assert done[0] == GL, done[0]
            links[0] += GRP * GL
            dve.wait_ge(S("s_sto"), (5 + 24) * 16)
            os8 = osm[0:NSMP, :, :].rearrange("p w (h d) -> p w h d", h=HEADS)
            for w, gi in ((0, 1), (1, 2), (2, 0)):
                last = v.tensor_tensor(os8[:, w], os8[:, w], gv[0:NSMP, 4, :, gi:gi + 1].to_broadcast([NSMP, HEADS, HD]), ALU.mult)
            link(last)
            link(v.tensor_tensor(osm[0:NSMP, 0, :], osm[0:NSMP, 0, :], osm[0:NSMP, 1, :], ALU.add))
            v.tensor_tensor(oatt[0:NSMP, 4, :], osm[0:NSMP, 0, :], osm[0:NSMP, 2, :], ALU.add)
            v.memset(nss, 1.0).then_inc(S("o_all"), 1)
            dve.wait_ge(S("p_fin"), 2 + 32)
            dve.wait_ge(S("o_root"), 1)
            link(v.reciprocal(nss[:, 8:13], nss[:, 8:13]))
            for i in range(NTILE):
                rows = TROWS[i]
                last = v.tensor_scalar(oatt[0:rows, i, :], oatt[0:rows, i, :], nss[0:rows, 8 + i:9 + i], None, ALU.mult)
            last.then_inc(S("o_norm"), 1)
            for f in range(4):
                dve.wait_ge(S("o_turned"), f + 1)
                gn = vcol[:, V_GNSA + f:V_GNSA + f + 1]
                v.tensor_scalar(xnT[:, 4 + f, 0:SEQ], ps[f], gn, None, ALU.mult)
                v.tensor_scalar(xnT[:, 4 + f, SEQ:T], ps[4 + f][:, 0:NSMP], gn, None, ALU.mult).then_inc(S("o_mix"), 1)
            for m in range(KD):
                dve.wait_ge(S("h_mm"), m + 1)
                v.tensor_tensor(xT[:, m, 0:SEQ], xT[:, m, 0:SEQ], ps[m % 2], ALU.add)
                v.tensor_tensor(xT[:, m, SEQ:T], xT[:, m, SEQ:T], ps[2 + m % 2][:, 0:NSMP], ALU.add).then_inc(S("h_done"), 1)
            dve.wait_ge(S("h_done"), KD)
            norm_dve(dve, 2, xT, xnT, V_GFFN)
            v.memset(pad[:, :, :, 0:2], 0.0)
            dve.sem_inc(S("u_conv"), 2)
            dve.sem_inc(S("u_smp"), 2)
            dve.sem_inc(S("u_fc"), 1)
            UL = 4

            def up_dve(par, qn):
                n = [0]

                def ulink(ins):
                    n[0] += 1
                    ins.then_inc(S("v_link"), 1)
                    dve.wait_ge(S("v_link"), qn * UL + (links[0] + n[0]))

                dve.wait_ge(S("u_ft"), qn + 1)
                v.tensor_copy(fcol[:, par, :, :], ps[6][:, 0:64].rearrange("p (w n) -> p w n", w=2)[:, :, 0:19]).then_inc(S("u_fc"), 1)
                dve.wait_ge(S("u_fc"), qn + 2)
                dve.wait_ge(S("u_mm"), qn + 1)
                for w in range(2):
                    pv = pad[:, par, w, 2 + SEQ:FPW].rearrange("p (b t) -> p b t", b=NB)
                    v.tensor_copy(pv[:, :, 0:2], fcol[:, par, w, 0:16].rearrange("p (b j) -> p b j", b=NB))
                    last = v.tensor_copy(pv[:, :, 2:2 + TS],
                                         ps[4 + par][:, w * NSMP:(w + 1) * NSMP].rearrange("p (b t) -> p b t", b=NB))
                last.then_inc(S("u_smp"), 1)
                dve.wait_ge(S("u_smp"), qn + 3)
                dve.wait_ge(S("u_pad"), qn + 3)
                dve.wait_ge(S("u_lT"), qn + 1)
                v.tensor_copy(l18[:, :, 0:2], pad[:, par, :, SEQ:SEQ + 2])
                for w in range(2):
                    pv = pad[:, par, w, 2 + SEQ:FPW].rearrange("p (b t) -> p b t", b=NB)
                    last = v.tensor_copy(l18[:, w, 2:18].rearrange("p (b j) -> p b j", b=NB), pv[:, :, TS:TS + 2])
                last.then_inc(S("u_l18"), 1)
                dve.wait_ge(S("u_act"), qn + 1)
                taps = [fcol[:, par, w, 16 + j:17 + j] for w in range(2) for j in range(3)]
                for w, c in ((1, cg), (0, ca)):
                    ulink(v.tensor_scalar(c, pad[:, par, w, 0:FVW], taps[3 * w], None, ALU.mult))
                    ulink(v.scalar_tensor_tensor(out=c, in0=pad[:, par, w, 1:1 + FVW], scalar=taps[3 * w + 1], in1=c,
                                                 op0=ALU.mult, op1=ALU.add))
                    v.scalar_tensor_tensor(out=c, in0=pad[:, par, w, 2:2 + FVW], scalar=taps[3 * w + 2], in1=c,
                                           op0=ALU.mult, op1=ALU.add).then_inc(S("u_cg" if w else "u_conv"), 1)
                dve.wait_ge(S("u_conv"), qn + 3)
                dve.wait_ge(S("u_silu"), qn + 1)
                v.tensor_tensor(actT[:, bass.ds(qn, 1), :] if not isinstance(qn, int) else actT[:, qn:qn + 1, :],
                                cg.unsqueeze(1), ca.unsqueeze(1), ALU.mult).then_inc(S("u_act"), 1)
                dve.wait_ge(S("u_lT"), qn + 2)
                dve.wait_ge(S("u_fof"), qn + 1)
                v.tensor_copy(a7["fo"][0:18, :], ps[7][0:18, 0:256]).then_inc(S("u_fo"), 1)

            dve.sem_inc(S("u_lT"), 1)
            dve.sem_inc(S("u_act"), 1)
            dve.sem_inc(S("u_fo"), 1)
            dve.sem_inc(S("u_pad"), 2)
            with dve.Fori(0, 5) as it:
                for q in range(4):
                    up_dve(q % 2, it * 4 + q)
            for q in range(20, 22):
                up_dve(q % 2, q)
            dve.sem_inc(S("d_done0"), 2)
            with dve.Fori(0, KD // 2) as it:
                for s in range(2):
                    m = it * 2 + s
                    dve.wait_ge(S("d_mm"), m + 2)
                    xp, xs = xT[:, bass.ds(m, 1), 0:SEQ], xT[:, bass.ds(m, 1), SEQ:T]
                    v.tensor_tensor(xp, xp, ps[s].unsqueeze(1), ALU.add)
                    v.tensor_tensor(xs, xs, ps[2 + s][:, 0:NSMP].unsqueeze(1), ALU.add).then_inc(S("d_done0"), 1)
            dve.wait_ge(S("d_done0"), 2 + KD)
            v.memset(fcol[:, 0, 0, 0:1], 0.0).then_inc(S("d_done"), KD)
            dve.wait_ge(S("d_done"), KD)
            norm_dve(dve, 3, xT, xnT, V_GFIN)
            dve.wait_ge(S("u_fof"), 1 + NFF)
            for n in range(1, 10, 2):
                dve.wait_ge(S("y_turned"), n + 1)
                rows = TROWS[n // 2]
                v.tensor_copy(ytok[0:rows, n // 2, 512:D], ps[n % 6][0:rows, :]).then_inc(S("y_dve"), 1)

        @block.sync
        def _(sp):
            sp.dma_start(vrows[V_GMIX:V_GMIX + 8, :], A["g_mix"][0].rearrange("(k p) -> k p", p=P)).then_inc(S("vec_in"), 16)
            sp.dma_start(vrows[V_GFFN:V_GFFN + 8, :], A["g_ffn"][0].rearrange("(k p) -> k p", p=P)).then_inc(S("vec_in"), 16)
            sp.dma_start(vrows[V_GNSA:V_GNSA + 4, :], A["g_nsa"][0].rearrange("(k p) -> k p", p=P)).then_inc(S("vec_in"), 16)
            sp.dma_start(vrows[V_SKIP:V_SKIP + 4, :], A["m_skip"][0].rearrange("(k p) -> k p", p=P)).then_inc(S("vec_in"), 16)
            sp.dma_start(vrows[V_GHEAD:V_GHEAD + 4, :], A["g_mhead"][0]).then_inc(S("vec_in"), 16)
            sp.dma_start(vrows[V_BCONV:V_BCONV + 4, :], A["b_mconv"][0].rearrange("(k p) -> k p", p=P)).then_inc(S("vec_in"), 16)
            sp.dma_start(vrows[V_WCONV:V_WCONV + 16, :], A["w_mconv"][0].rearrange("j (k p) -> (j k) p", p=P)).then_inc(S("vec_in"), 16)
            sp.dma_start(vrows[V_PE:V_PE + 32, :], A["pe_cmp"][0].rearrange("k (c two) d -> (k c) (two d)", two=2)).then_inc(S("vec_in"), 16)
            sp.dma_start(vrows[V_GFIN:V_GFIN + 8, :], A["g_final"].rearrange("(k p) -> k p", p=P)).then_inc(S("vec_in"), 16)
            sp.dma_start(mcs[0:24, :], A["state_mlstm_conv"][0].rearrange("b j f -> (b j) f")).then_inc(S("vec_in"), 16)
            sp.dma_start(nrows[0:32, :], A["state_mlstm_n"][0].rearrange("b h d -> (b h) d")).then_inc(S("vec_in"), 16)
            sp.dma_start(gb[:, 0:1], A["b_ig"].rearrange("a h -> h a"), allow_slow_non_contiguous=True).then_inc(S("vec_in"), 16)
            sp.dma_start(gb[:, 1:2], A["b_fg"].rearrange("a h -> h a"), allow_slow_non_contiguous=True).then_inc(S("vec_in"), 16)
            sp.dma_start(m0[:, :], A["state_mlstm_m"][0].rearrange("b h -> h b"), allow_slow_non_contiguous=True).then_inc(S("vec_in"), 16)
            for i in range(4):
                sp.dma_start(xtok[:, i, :], A["x_prompt"][0, i * P:(i + 1) * P, :]).then_inc(S("x_in"), 16)
            sp.dma_start(xtok[0:NSMP, 4, :], A["x_sample"].rearrange("b t f -> (b t) f")).then_inc(S("x_in"), 16)



            def slab(n):
                c0, w = SLABS[n]
                if n == 0:
                    dq = ring[:, 0, :].rearrange("p (k g h d) -> p k g h d", k=KD, g=GRP, h=KVH)
                    for h in range(KVH):
                        for g in range(GRP):
                            at = (h * GRP + g) * HD
                            sp.dma_start(dq[:, :, g, h, :], w_in[:, :, at:at + HD]).then_inc(S("q_in"), 16)
                    return
                dst = ring[:, n % 2, :].rearrange("p (k n) -> p k n", k=KD)[:, :, 0:w]
                sp.dma_start(dst, w_in[:, :, c0:c0 + w]).then_inc(S(f"slab_in{n % 2}"), 16)

            slab(0)
            slab(1)
            sp.wait_ge(S("filled"), 1)
            sp.dma_start(wg[:, :, 0:MH], w_in[:, :, 2840:2844]).then_inc(S("wg_in"), 16)
            sp.dma_start(wg[:, :, 32:32 + MH], w_in[:, :, 2844:2848]).then_inc(S("wg_in"), 16)
            sp.wait_ge(S("normed"), KD)
            for k in range(2):
                sp.dma_start(w1c[:, k, :, :], A["w_cmp1"][0, k].rearrange("(c p) n -> p c n", p=P)).then_inc(S("w1_in"), 16)
                sp.dma_start(w2c[:, k, :], A["w_cmp2"][0, k]).then_inc(S("w1_in"), 16)
            for n in range(2, 6):
                sp.wait_ge(S("job"), slab_last[n - 2] + 1)
                slab(n)
            for w, name in enumerate(("w_mq", "w_mk")):
                sp.dma_start(wqk[:, w, :, :], A[name][0].rearrange("h d e -> d h e")).then_inc(S("wqk_in"), 16)
            sp.wait_ge(S("c_kc"), 4 + 2 * 9)
            sp.dma_start(nbh.rearrange("b (h d) -> b h d", h=MH), A["state_mlstm_n"][0]).then_inc(S("wqk_in"), 16)
            for h in range(MH):
                if h:
                    sp.wait_ge(S("m_cout"), 16 * h)
                sp.dma_start(Cst[:, :, :], A["state_mlstm_C"][0, :, h].rearrange("b e d -> e b d")).then_inc(S("m_cin"), 16)
            sp.wait_ge(S("m_mix"), MH)
            for b in range(NB):
                sp.dma_start(vnew[:, b, :, :],
                             kv[b * TS:(b + 1) * TS, 4, 256:768].rearrange("t (w k f) -> t w k f", w=2, k=2)[:, :, 1, :])\
                    .then_inc(S("m_cin"), 16)

            def window(p):
                for b2 in range(2):
                    b = 2 * p + b2
                    sp.dma_start(wkv[:, 2 * (p % 2) + b2, :],
                                 A["state_win"][0, b].rearrange("(p j) k h d -> p (j k h d)", p=P)).then_inc(S(f"win_in{p % 2}"), 16)

            window(0)
            window(1)
            sp.sem_inc(S("s_sto"), 16)
            for p in range(4):
                sp.wait_ge(S("s_out"), p + 2)
                sp.dma_start(osc[:, p * P:(p + 1) * P, :].rearrange("w r d -> r w d"), orow).then_inc(S("s_sto"), 16)
                if p < 2:
                    window(p + 2)
            sp.dma_start(ring[:, 0, :].rearrange("p (k n) -> p k n", k=KD),
                         A["w_out"][0].rearrange("(k p) n -> p k n", p=P)[:, :, 0:512]).then_inc(S("slab_in0"), 16)
            sp.dma_start(ring[:, 1, :].rearrange("p (k n) -> p k n", k=KD),
                         A["w_out"][0].rearrange("(k p) n -> p k n", p=P)[:, :, 512:D]).then_inc(S("slab_in1"), 16)
            sp.wait_ge(S("s_sto"), 5 * 16)
            for b in range(NB):
                for w in range(3):
                    sp.dma_start(osm[b * TS:(b + 1) * TS, w, :].rearrange("t (h d) -> t h d", h=HEADS),
                                 osc[w, b * 64:(b + 1) * 64, :].rearrange("(h t) d -> t h d", h=HEADS)).then_inc(S("s_sto"), 16)
            sp.wait_ge(S("vbd_zero"), 1)
            for hd in range(HEADS):
                sp.dma_start(Vbd[hd * 16:hd * 16 + 16, hd * HD:(hd + 1) * HD],
                             vc_p[:, (hd // GRP) * HD:(hd // GRP + 1) * HD]).then_inc(S("vbd_in"), 16)
            w_up = A["w_up"][0].rearrange("(k p) (w n) -> p w k n", p=P, w=2)
            w_dn = A["w_down"][0].rearrange("(k p) n -> p k n", p=P)
            f_st = A["state_ffn_conv"][0].rearrange("b j (w n) -> (b j) w n", w=2)
            f_wt = A["w_fconv"][0].rearrange("j (w n) -> j w n", w=2)

            def up_slab(n):
                s = n % 2
                dst = ring[:, s, :].rearrange("p (w k n) -> p w k n", w=2, k=KD)
                for w in range(2):
                    sp.dma_start(dst[:, w], w_up[:, w, :, n * 256:(n + 1) * 256]).then_inc(S(f"slab_in{s}"), 16)
                sp.dma_start(fin[0:16, s, :, :], f_st[:, :, n * 256:(n + 1) * 256]).then_inc(S(f"slab_in{s}"), 16)
                sp.dma_start(fin[16:19, s, :, :], f_wt[:, :, n * 256:(n + 1) * 256]).then_inc(S(f"slab_in{s}"), 16)

            sp.wait_ge(S("o_norm"), 1)
            for n in range(2):
                sp.wait_ge(S("h_mm"), 4 * (n + 1))
                up_slab(n)
            for n in range(2, 11):
                sp.wait_ge(S("u_mm"), 2 * (n - 1))
                up_slab(n)
                if n == 3:
                    for s in range(2):
                        sp.dma_start(wdn[:, s, :, :], w_dn[:, :, s * P:(s + 1) * P]).then_inc(S(f"dn_in{s}"), 16)
            for m in range(2, KD):
                sp.wait_ge(S("d_mm"), m)
                sp.dma_start(wdn[:, m % 2, :, :], w_dn[:, :, m * P:(m + 1) * P]).then_inc(S(f"dn_in{m % 2}"), 16)
            for i in range(NTILE):
                sp.wait_ge(S("y_act"), i + 1)
                sp.wait_ge(S("y_dve"), i + 1)
                dst = O["y_p"][0, i * P:(i + 1) * P, :] if i < 4 else O["y_s"].rearrange("b t f -> (b t) f")
                sp.dma_start(dst, ytok[0:TROWS[i], i, :]).then_inc(S("y_stored"), 16)
            sp.wait_ge(S("y_stored"), NTILE * 16)
            sp.wait_ge(S("stored"), outs[0])



_INS = ['x_prompt', 'x_sample', 'cache_cmp', 'cache_sel', 'state_win', 'state_mlstm_C', 'state_mlstm_n',
        'state_mlstm_m', 'state_mlstm_conv', 'state_ffn_conv', 'page_table',
        'g_mix', 'w_in', 'w_out', 'w_mconv', 'b_mconv', 'w_mq', 'w_mk', 'b_ig', 'b_fg', 'g_mhead', 'm_skip',
        'pe_cmp', 'w_cmp1', 'w_cmp2', 'g_nsa', 'g_ffn', 'w_up', 'w_fconv', 'w_down', 'g_final']
_OUTS = [('y_p', (1, 512, 1024)), ('y_s', (8, 8, 1024)),
         ('cmp_p', (1, 1, 512, 2, 2, 64)), ('cmp_s', (1, 8, 8, 2, 2, 64)),
         ('sel_p', (1, 1, 512, 2, 2, 64)), ('sel_s', (1, 8, 8, 2, 2, 64)),
         ('win_p', (1, 1, 512, 2, 2, 64)), ('win_s', (1, 8, 512, 2, 2, 64)),
         ('C_p', (1, 1, 4, 128, 128)), ('C_s', (1, 8, 4, 128, 128)),
         ('n_p', (1, 1, 4, 128)), ('n_s', (1, 8, 4, 128)),
         ('m_p', (1, 1, 4)), ('m_s', (1, 8, 4)),
         ('mconv_p', (1, 1, 3, 512)), ('mconv_s', (1, 8, 3, 512)),
         ('fconv_p', (1, 1, 2, 5632)), ('fconv_s', (1, 8, 2, 5632))]


def kernel(**inputs):
    import numpy as _np
    import concourse.bacc as _bacc
    from concourse import mybir as _mybir
    from concourse.bass_utils import run_bass_kernel_spmd as _run

    nc = _bacc.Bacc("TRN2", target_bir_lowering=False, num_devices=1)
    arrays, ins, outs = {}, {}, {}
    for name in _INS:
        a = _np.ascontiguousarray(inputs[name])
        arrays[f"in_{name}_dram"] = a
        ins[name] = nc.dram_tensor(f"in_{name}_dram", a.shape, _mybir.dt.from_np(a.dtype), kind="ExternalInput").ap()
    for name, shape in _OUTS:
        outs[name] = nc.dram_tensor(f"out_{name}_dram", shape, _mybir.dt.float32, kind="ExternalOutput").ap()
    hybrid_decoder_layer(nc, ins, outs)
    r = _run(nc, [arrays], core_ids=[0])
    return tuple(r.results[0][f"out_{name}_dram"] for name, _ in _OUTS)
```

```python
import concourse.bass as bass
from concourse import mybir
from contextlib import ExitStack

F32 = mybir.dt.float32
I32 = mybir.dt.int32
F32R = mybir.dt.float32r
ALU = mybir.AluOpType
ACT = mybir.ActivationFunctionType
AX = mybir.AxisListType

P = 128
D = 1024
KD = D // P
SEQ = 512
NB, TS = 8, 8
NSMP = NB * TS
T = SEQ + NSMP
TA, TB = 384, 192
UA, UB = 256, 320
SBUF_END = 229375
NTILE = 5
TROWS = [P] * 4 + [NSMP]
PAST, PAGE = 2048, 128
HD, KVH, GRP = 64, 2, 4
HEADS = KVH * GRP
MH = 4
DFF = 2816
NFF = DFF // P
WIN = 512
NIN = 2848
EPS = 1e-6
NEG = -1e30
SCALE = HD ** -0.5
KSCALE = P ** -0.5
NSEL = PAST // 64
PRIORITY = 1e4
ROWF = 4096
UPW = 3 + SEQ + NB * (3 + TS)
CVW = UPW - 3
FPW = 2 + SEQ + NB * (2 + TS)
FVW = FPW - 2

V_GMIX, V_GFFN, V_GNSA, V_SKIP, V_GHEAD, V_BCONV, V_WCONV, V_PE, V_GFIN = 0, 8, 16, 20, 24, 28, 32, 48, 80
V_ROWS = 88
V_MCS = 88
V_N = V_MCS + 4 * 24
V_COLS = V_N + NB * MH


def hybrid_decoder_layer(nc, A, O):
    ctx = ExitStack()
    with ctx:
        def sb(name, shape, dt=F32):
            return ctx.enter_context(nc.sbuf_tensor(name, shape, dt))

        def sb2(name, shape):
            at = (SBUF_END - nc.sbuf_bytes_remaining) // 32 * 32
            return sb(name, shape), nc.alloc_sbuf_tensor_at(name + "_r", shape, F32R, offset=at)

        made = {}

        def S(name):
            if name not in made:
                made[name] = ctx.enter_context(nc.semaphore(name))
            return made[name]

        banks = ctx.enter_context(nc.psum_tensor("banks", [P, 8, 512], F32))
        ps = [banks[:, i, :] for i in range(8)]

        def carve(region, sizes):
            at, out = 0, {}
            for name, n in sizes:
                out[name] = region[:, at:at + n]
                at += n
            assert at <= region.shape[1], (at, region.shape)
            return out

        ident = sb("ident", [P, P])
        ones = sb("ones", [P, P])
        causal = sb("causal", [P, P])
        causalT = sb("causalT", [P, P])
        smask = sb("smask", [P, NSMP])
        winmask = sb("winmask", [P, WIN])
        newmask = sb("newmask", [P, TS])
        gsum = sb("gsum", [P, P])
        selh = sb("selh", [MH, MH, P])
        small = sb("small", [P, 8])
        vcol = sb("vcol", [P, V_COLS])
        idx = sb("idx", [P, NB], I32)
        xT = sb("xT", [P, KD, T])
        xnT, xnT_r = sb2("xnT", [P, KD, T])
        ring, ring_r = sb2("ring", [P, 2, ROWF])
        RA = sb("RA", [P, 5248])
        RB, RB_r = sb2("RB", [P, 8192])
        RC, RC_r = sb2("RC", [P, 17412])
        ktT = sb("ktT", [P, 2, T])
        kcT_s = sb("kcT_s", [P, 4, P])
        vc_s = sb("vc_s", [P, 4, P])
        kcT_p = sb("kcT_p", [P, 16])
        vc_p = sb("vc_p", [16, P])
        gsig = sb("gsig", [P, NTILE, HEADS * 3])
        gb = sb("gb", [MH, 2])
        m0 = sb("m0", [MH, NB])
        hb = sb("hb", [P, 2])

        c = carve(RC, [("qT", GRP * T), ("Qbd", NB * 64), ("uT", MH * UPW + 152), ("kv", NTILE * 768),
                       ("ucT", MH * T), ("moT", MH * T), ("mv", NTILE * MH * (P + 1))])
        ring2 = RC[:, 9220:9220 + 2 * ROWF].rearrange("p (s n) -> p s n", s=2)
        qT = c["qT"].rearrange("p (g t) -> p g t", g=GRP)
        Qbd = c["Qbd"].rearrange("p (b r) -> p b r", b=NB)
        uT = c["uT"][:, 0:MH * UPW].rearrange("p (k t) -> p k t", k=MH)
        oatt = c["uT"][:, 0:NTILE * 512].rearrange("p (i f) -> p i f", i=NTILE)
        ucT = c["ucT"].rearrange("p (k t) -> p k t", k=MH)
        moT = c["moT"].rearrange("p (k t) -> p k t", k=MH)
        kv = c["kv"].rearrange("p (i f) -> p i f", i=NTILE)
        mv = c["mv"].rearrange("p (i h e) -> p i h e", i=NTILE, h=MH)

        a1 = carve(RA, [("xtok", NTILE * D)])
        xtok = a1["xtok"].rearrange("p (i f) -> p i f", i=NTILE)
        xs = RC[:, 5380:5380 + NTILE * D].rearrange("p (i f) -> p i f", i=NTILE)
        ss = sb("ss", [P, 2, NTILE])
        b1 = carve(RB, [("", 4 * T), ("vrows", P), ("mcs", MH * P), ("nrows", P),
                        ("wrow", WIN), ("mod", P), ("part", 8), ("newk", 8)])
        vrows, nrows = b1["vrows"], b1["nrows"]
        mcs = b1["mcs"]
        packed = xnT[:, :, :].rearrange("p k t -> p (k t)")[:, 0:4096].rearrange("p (k n) -> p k n", k=2)
        a3 = carve(RA, [("XT", 4 * 512), ("hid", 2 * 2 * P), ("", 1536), ("irow", T), ("frow", T)])
        XT = a3["XT"].rearrange("p (s n) -> p s n", s=4)
        hid = a3["hid"].rearrange("p (s k n) -> p s k n", s=2, k=2)
        irow, frow = a3["irow"][0:MH, :], a3["frow"][0:MH, :]
        b3 = carve(RB, [("w1c", 2 * 16 * P), ("w2c", 2 * HD), ("wg", KD * 36)])
        w1c = b3["w1c"].rearrange("p (k c n) -> p k c n", k=2, c=16)
        w2c = b3["w2c"].rearrange("p (k n) -> p k n", k=2)
        wg = b3["wg"].rearrange("p (k n) -> p k n", k=KD)

        a4 = carve(RA, [("hs", NTILE * MH * (P + 1)), ("vw", NTILE * P), ("rcol", 64), ("s2", 20), ("f1", 20), ("f2", 20),
                        ("f3", 20), ("slc", NB), ("wlb", NB), ("mcg", MH * 27), ("cpo", MH * P)])
        hs = a4["hs"].rearrange("p (i h e) -> p i h e", i=NTILE, h=MH)
        vw = a4["vw"].rearrange("p (i e) -> p i e", i=NTILE)
        rcol = a4["rcol"][:, 0:60].rearrange("p (k i h) -> p k i h", k=3, i=NTILE)
        slcol = a4["rcol"][0:NB, 60:64]
        s2, f1, f2, f3 = a4["s2"], a4["f1"], a4["f2"], a4["f3"]
        slc, wlb = a4["slc"], a4["wlb"]
        mcg = a4["mcg"].rearrange("p (k n) -> p k n", k=MH)
        cpo = a4["cpo"].rearrange("p (h d) -> p h d", h=MH)
        EW = 1280
        b4 = carve(RB, [("E", EW + NSMP), ("W", EW + NSMP), ("mqT", T), ("mkT", T), ("mk", NTILE * P), ("Cst", NB * P),
                        ("CT", NB * (P + 1)), ("kbd", NB * P), ("Qm", NB * NSMP)])
        E, W, mqT, mkT = b4["E"], b4["W"], b4["mqT"], b4["mkT"]
        conv = RA[:, 0:2 * CVW].rearrange("p (s t) -> p s t", s=2)
        mk = b4["mk"].rearrange("p (i d) -> p i d", i=NTILE)
        Cst = b4["Cst"].rearrange("p (b d) -> p b d", b=NB)
        CT = b4["CT"].rearrange("p (b e) -> p b e", b=NB)
        kbd = b4["kbd"].rearrange("p (b d) -> p b d", b=NB)
        Qm = b4["Qm"].rearrange("p (b t) -> p b t", b=NB)
        EOFF = [0, 512, 896, 1152]
        xrows = xnT[:, :, :].rearrange("p k t -> p (k t)")
        nbh, npo, mco = xrows[0:NB, 0:512], xrows[0:1, 512:1024], xrows[0:27, 1024:1536]
        r0, r1, r2, r3 = (c["uT"][0:MH, n * T:(n + 1) * T] for n in range(4))
        restart, down = RA[0:MH, 2 * CVW:2 * CVW + T], RA[0:MH, 2 * CVW + T:2 * (CVW + T)]
        wqk = ktT[:, :, :].rearrange("p s t -> p (s t)")[:, 0:2 * MH * P].rearrange("p (w h e) -> p w h e", w=2, h=MH)

        a5 = carve(RA, [("S", PAST + TS), ("Sw", WIN + TS), ("PTw", 4 * P), ("PTn", 2 * P), ("PTc", P), ("Qp", P), ("vcp", P),
                        ("pcd", P), ("outT", 3 * P), ("orow", 3 * HD), ("col", 16), ("pri", 3 * 40), ("top", 16), ("add", 40),
                        ("vnp", 4 * P)])
        Ss, Sw, PTc, Qp, vcp, pcd = a5["S"], a5["Sw"], a5["PTc"], a5["Qp"], a5["vcp"], a5["pcd"]
        PTw = a5["PTw"].rearrange("p (j r) -> p j r", j=4)
        PTn = a5["PTn"][0:TS, :].rearrange("p (w r) -> p w r", w=2)
        outT = a5["outT"].rearrange("p (w r) -> p w r", w=3)
        orow = a5["orow"].rearrange("p (w d) -> p w d", w=3)
        col = a5["col"]
        pri = a5["pri"].rearrange("p (s j) -> p s j", s=3)[:, :, 0:NSEL + 1]
        top = a5["top"].rearrange("p (s j) -> p s j", s=2)
        add = a5["add"][:, 0:NSEL + 1]
        vnp = a5["vnp"][0:TS, :].rearrange("p (b w d) -> p b w d", b=2, w=2)
        b5 = carve(RB, [("PT", 16 * P), ("KTb", 2 * 512), ("wkv", 4 * 4 * 256), ("kcp", P), ("ktn", 32)])
        kcp, ktn = b5["kcp"], b5["ktn"].rearrange("p (w n) -> p w n", w=2)
        PT = b5["PT"].rearrange("p (j r) -> p j r", j=16)
        KTb = b5["KTb"].rearrange("p (s n) -> p s n", s=2)
        wkv = b5["wkv"].rearrange("p (s n) -> p s n", s=4)
        vnew = xnT[0:TS, 4:8, :].rearrange("p k t -> p (k t)")[:, 0:NB * 2 * P].rearrange("p (b w d) -> p b w d", b=NB, w=2)
        osc = nc.dram_tensor("osc", (3, NB * 64, HD), F32, kind="Internal").ap()
        slots = [ring[:, 0, :], ring[:, 1, :], ring2[:, 0, :], ring2[:, 1, :]]
        b6 = carve(RB, [("qst", KVH * SEQ), ("gst", 4 * 2 * 2), ("Pb", 2 * 2 * SEQ), ("PTp", 2 * 2 * SEQ), ("cst", 16), ("tmp", 2 * P),
                        ("Pc", SEQ), ("PcT", SEQ), ("cmk", 4 * 16), ("cm", 2 * 32)])
        qst = b6["qst"].rearrange("p (h t) -> p h t", h=KVH)
        gst = b6["gst"].rearrange("p (i h w) -> p i h w", i=4, h=2)
        Pb = b6["Pb"].rearrange("p (s w n) -> p s w n", s=2, w=2)
        PTp = b6["PTp"].rearrange("p (s w n) -> p s w n", s=2, w=2)
        cst = b6["cst"].rearrange("p (s k w) -> p s k w", s=2, k=4)
        tmp = b6["tmp"].rearrange("p (s w d) -> p s w d", s=2, w=2)
        Pc, PcT, Vbd = b6["Pc"], b6["PcT"].rearrange("p (i t) -> p i t", i=4), c["uT"][:, 0:SEQ]
        cmk = b6["cmk"].rearrange("p (i n) -> p i n", i=4)
        cm = b6["cm"].rearrange("p (s n) -> p s n", s=2)
        a6 = carve(RA, [("osm", 3 * 512), ("nss", 16)])
        osm = a6["osm"].rearrange("p (w f) -> p w f", w=3)
        nss = a6["nss"]
        sqo = RB[:, 0:NTILE * 512].rearrange("p (i f) -> p i f", i=NTILE)
        a7 = carve(RA, [("pad", 2 * 2 * FPW), ("ca", FVW), ("cg", FVW), ("fin", 2 * 512), ("fcol", 2 * 2 * 19), ("l18", 2 * 18),
                        ("fo", 256)])
        pad = a7["pad"].rearrange("p (s w t) -> p s w t", s=2, w=2)
        ca, cg = a7["ca"], a7["cg"]
        fin = a7["fin"][0:19, :].rearrange("p (s w n) -> p s w n", s=2, w=2)
        fcol = a7["fcol"].rearrange("p (s w n) -> p s w n", s=2, w=2)
        l18 = a7["l18"].rearrange("p (w n) -> p w n", w=2)
        fo = a7["fo"][0:18, :].rearrange("p (w n) -> p w n", w=2)
        an = carve(RA, [("sq", 2 * T), ("rms", T), ("rstd", T), ("xn", 2 * T)])
        assert 6 * T <= 2 * 2 * FPW + 2 * FVW
        sq = an["sq"].rearrange("p (s t) -> p s t", s=2)
        xn = an["xn"].rearrange("p (s t) -> p s t", s=2)
        rms, rstd = an["rms"], an["rstd"]
        actT = RC[:, 0:NFF * T].rearrange("p (k t) -> p k t", k=NFF)
        xhi = xnT_r[:, :, :]
        xlo = RC_r[:, NFF * T:(NFF + KD) * T].rearrange("p (k t) -> p k t", k=KD)
        whi = [RB_r[:, 4096 * s:4096 * (s + 1)] for s in range(2)]
        draw = [ring[:, 1 - s, 0:NFF * P].rearrange("p (k n) -> p k n", k=NFF) for s in range(2)]
        dlo = [ring_r[:, 1 - s, 0:NFF * P].rearrange("p (k n) -> p k n", k=NFF) for s in range(2)]
        dhi_runs = [[(0, 22, RB_r[:, 4096:6912])], [(0, 10, RB_r[:, 6912:8192]), (10, 5, RB_r[:, 3456:4096]),
                                                    (15, 7, ring_r[:, 0, 2816:3712])]]
        dhi = [[where[:, P * k:P * (k + 1)] for _, n, where in runs for k in range(n)] for runs in dhi_runs]
        ahi = [xhi[:, k, :] for k in range(8)] + [xlo[:, k, :] for k in range(8)] + \
              [RB_r[:, T * k:T * (k + 1)] for k in range(6)]
        alo = [RC_r[:, T * k:T * (k + 1)] for k in range(NFF)]
        assert len(ahi) == NFF and 6 * T == 3456
        hst = ring[:, 1, 2816:2816 + 2 * T].rearrange("p (s t) -> p s t", s=2)
        gB = ktT[:, :, :].rearrange("p s t -> p (s t)")[:, 0:D]
        sqs = kcT_s
        ssy = sb("ssy", [P, NTILE, KD])
        yrt = ss[:, 0, :]
        ytok = RA[:, 0:NTILE * D].rearrange("p (i f) -> p i f", i=NTILE)

        def gfac(slot):
            return cst[:, slot, 3, :].unsqueeze(2).to_broadcast([P, 2, HD])

        UNITS = [(i, h) for i in range(4) for h in range(KVH)]

        w_in = A["w_in"][0].rearrange("(k p) n -> p k n", p=P)
        SLABS = [(0, 512), (1304, 512), (512, 512), (1024, 280), (1816, 512), (2328, 512)]
        jobs = [(0, "q", i) for i in range(4)] + [(0, "gates", 0)] + [(1, "mu", i) for i in range(4)]
        jobs += [(2, "kvA", i) for i in range(5)] + [(3, "kvB", i) for i in range(5)]
        jobs += [(4, "mv", i) for i in range(5)] + [(5, "mo", i) for i in range(4)]
        slab_last = [max(n for n, j in enumerate(jobs) if j[0] == s) for s in range(6)]
        evac, na, nv = [], 0, 0
        for _, kind, i in jobs:
            if kind in ("q", "mu"):
                na, nv = na + 1, nv + 1
            elif kind in ("mo", "kvB"):
                na += 1
            elif kind == "gates":
                nv += 1
            elif i % 2:
                na += 1
            else:
                nv += 1
            evac.append((na, nv))

        CONV_JOB = jobs.index((2, "kvA", 0))
        GATE_JOB = jobs.index((3, "kvB", 0))

        pool_cmp = A["cache_cmp"][0].rearrange("n (c j) k h d -> (n c) (j k h d)", j=16)
        pool_sel = A["cache_sel"][0].rearrange("n (c j) k h d -> (n c) (j k h d)", j=16)

        outs = [0]

        def out_dma(eng, dst, src, slow=False):
            outs[0] += 16
            return eng.dma_start(dst, src, allow_slow_non_contiguous=slow).then_inc(S("stored"), 16)

        def conv_sample(k):
            cv = conv[:, k % 2, SEQ + 3:CVW]
            full = bass.AP(cv.tensor, cv.offset, [list(cv.ap[0]), [3 + TS, NB], [1, TS]])
            return full

        def ffn_sample(cv):
            at = cv[:, SEQ + 2:FVW]
            return bass.AP(at.tensor, at.offset, [list(at.ap[0]), [2 + TS, NB], [1, TS]])

        block = ctx.enter_context(nc.Block())

        @block.gpsimd
        def _(pool):
            g = nc.gpsimd
            wrow = b1["wrow"].bitcast(I32).rearrange("p (j q) -> p j q", j=4)
            mod = b1["mod"].bitcast(I32).rearrange("p (q g t) -> p q g t", q=4, g=GRP)
            src = A["page_table"]
            for b in range(NB):
                pool.dma_start(idx[:, b:b + 1], bass.AP(src.tensor, src.offset + 16 * b, [[1, 16], [0, 8], [1, 1]]),
                               allow_slow_non_contiguous=True).then_inc(S("idx_in"), 16)
            g.memset(ident[:], 0.0)
            g.memset(wg, 0.0)
            g.memset(small[:, 0:1], EPS)
            g.memset(small[:, 2:3], 0.0)
            g.memset(ss[:], 1.0)
            g.memset(small[:, 3:5], 1.0)
            g.memset(ones[:], 1.0).then_inc(S("filled"), 1)
            pool.wait_ge(S("filled"), 1)
            g.affine_select(out=ident[:], in_=ident[:], compare_op=ALU.not_equal, fill=1.0, base=0,
                            pattern=[[-1, P]], channel_multiplier=1).then_inc(S("pool_step"), 1)
            g.iota(b1["part"].bitcast(I32)[:, 0:1], [[0, 1]], base=0, channel_multiplier=1)
            g.iota(b1["newk"].bitcast(I32), [[1, TS]], base=0, channel_multiplier=0)
            g.iota(mod, [[0, 4], [0, GRP], [1, TS]], base=0, channel_multiplier=0)
            g.iota(wrow, [[1, 4], [4, P]], base=0, channel_multiplier=0).then_inc(S("pool_step"), 1)
            g.memset(uT, 0.0)
            g.memset(mv[:, :, :, P:P + 1], 1.0)
            g.memset(Qbd, 0.0).then_inc(S("pool_step"), 1)
            g.memset(causal[:], 0.0)
            g.memset(causalT[:], 0.0)
            g.memset(smask[:], 0.0)
            g.memset(gsum[:], 1.0)
            g.memset(selh[:], 1.0).then_inc(S("filled"), 1)
            pool.wait_ge(S("filled"), 2)
            g.affine_select(out=causal[:], in_=causal[:], compare_op=ALU.is_ge, fill=NEG, base=0,
                            pattern=[[-1, P]], channel_multiplier=1)
            g.affine_select(out=causalT[:], in_=causalT[:], compare_op=ALU.is_ge, fill=NEG, base=0,
                            pattern=[[1, P]], channel_multiplier=-1)
            g.affine_select(out=small[:, 4:5], in_=small[:, 4:5], compare_op=ALU.is_ge, fill=0.0, base=-31,
                            pattern=[[0, 1]], channel_multiplier=1)
            g.affine_select(out=selh[:], in_=selh[:], compare_op=ALU.is_equal, fill=0.0, base=0,
                            pattern=[[-1, MH], [0, P]], channel_multiplier=1)
            sv = smask[0:NSMP, :].rearrange("p (b t) -> p b t", b=NB)
            g.affine_select(out=sv, in_=sv, compare_op=ALU.is_ge, fill=NEG, base=0,
                            pattern=[[-TS, NB], [0, TS]], channel_multiplier=1)
            gv = gsum[:, :].rearrange("p (q r) -> p q r", q=4)
            g.affine_select(out=gv, in_=gv, compare_op=ALU.is_ge, fill=0.0, base=0,
                            pattern=[[-32, 4], [0, 32]], channel_multiplier=1).then_inc(S("filled"), 1)
            pool.wait_ge(S("filled"), 3)
            g.affine_select(out=sv, in_=sv, compare_op=ALU.is_ge, fill=NEG, base=0,
                            pattern=[[TS, NB], [1, TS]], channel_multiplier=-1)
            g.affine_select(out=gv, in_=gv, compare_op=ALU.is_ge, fill=0.0, base=31,
                            pattern=[[32, 4], [0, 32]], channel_multiplier=-1).then_inc(S("pool_step"), 1)
            kv_job = [n for n, j in enumerate(jobs) if j[1] == "kvB"][-1]
            pool.wait_ge(S("ev_act"), evac[kv_job][0])
            pool.wait_ge(S("ev_dve"), evac[kv_job][1])
            for br, (op, os) in enumerate((("cmp_p", "cmp_s"), ("sel_p", "sel_s"), ("win_p", None))):
                out_dma(pool, O[op][0, 0].rearrange("(i p) k h d -> p i (k h d)", p=P), kv[:, 0:4, br * 256:br * 256 + 256])
                if os:
                    out_dma(pool, O[os][0].rearrange("b t k h d -> (b t) (k h d)"), kv[0:NSMP, 4, br * 256:br * 256 + 256])
            for b in range(NB):
                out_dma(pool, O["win_s"][0, b, WIN - TS:WIN].rearrange("t k h d -> t (k h d)"),
                        kv[b * TS:(b + 1) * TS, 4, 512:768])
            out_dma(pool, O["win_s"][0, :, 0:WIN - TS].rearrange("b r k h d -> b (r k h d)"),
                    A["state_win"][0, :, TS:WIN].rearrange("b r k h d -> b (r k h d)"))
            pool.wait_ge(S("setup_dve"), 1)

            def gather(pool_rows, slot, col):
                g.indirect_dma_start(ring[:, slot, :], None, pool_rows,
                                     bass.IndirectOffsetOnAxis(ap=col, axis=0)).then_inc(S(f"rows_in{slot}"), 16)

            for b in range(2):
                pool.wait_ge(S("job"), slab_last[4 + b] + 1)
                gather(pool_cmp, b, idx[:, b:b + 1])
            for b in range(2, NB):
                pool.wait_ge(S("c_packed"), 2 * (b - 1))
                gather(pool_cmp, b % 2, idx[:, b:b + 1])
            pool.wait_ge(S("c_packed"), 2 * 7)
            for i in range(4):
                pool.dma_start(ring[8 * i:8 * i + 8, 0, :].rearrange("r (j n) -> r j n", j=16),
                               kv[:, i, 0:256]).then_inc(S("own_in"), 16)
            pool.wait_ge(S("c_packed"), 2 * 9)
            for b in range(2):
                g.indirect_dma_start(slots[b], None, pool_sel,
                                     bass.IndirectOffsetOnAxis(ap=idx[:, b:b + 1], axis=0)).then_inc(S(f"sel_in{b}"), 16)
            pool.wait_ge(S("m_mcod"), 1)
            pool.dma_start(O["mconv_p"][0, 0], mco[0:3, :]).then_inc(S("m_stored"), 16)
            pool.dma_start(O["mconv_s"][0].rearrange("b j f -> (b j) f"), mco[3:27, :]).then_inc(S("m_stored"), 16)
            pool.wait_ge(S("gates_dve"), 2)
            pool.dma_start(O["m_p"][0].rearrange("a h -> h a"), r3[:, SEQ - 1:SEQ],
                           allow_slow_non_contiguous=True).then_inc(S("m_stored"), 16)
            pool.dma_start(O["m_s"][0].rearrange("b h -> h b"), r3[:, SEQ + TS - 1:T:TS],
                           allow_slow_non_contiguous=True).then_inc(S("m_stored"), 16)
            for h in range(MH):
                pool.wait_ge(S("m_p7d"), 5 * h + 4)
                pool.dma_start(O["C_s"][0, :, h].rearrange("b e d -> e b d"), Cst[:, :, :]).then_inc(S("m_cout"), 16)
                pool.wait_ge(S("m_p7d"), 5 * h + 5)
                out_dma(pool, O["C_p"][0, 0, h], cpo[:, h, :])
            pool.dma_start(O["n_p"][0].rearrange("a h d -> a (h d)"), npo).then_inc(S("m_stored"), 16)
            pool.dma_start(O["n_s"][0].rearrange("b h d -> b (h d)"), nbh).then_inc(S("m_stored"), 16)
            pool.wait_ge(S("m_stored"), 6 * 16)
            pool.wait_ge(S("m_cout"), 4 * 16)
            pool.wait_ge(S("m_mix"), MH)
            for b in range(2, NB):
                if b >= 4:
                    pool.wait_ge(S("s_pv"), b // 2 - 1)
                g.indirect_dma_start(slots[b % 4], None, pool_sel,
                                     bass.IndirectOffsetOnAxis(ap=idx[:, b:b + 1], axis=0)).then_inc(S(f"sel_in{b % 4}"), 16)
            pool.wait_ge(S("s_pv"), 4)
            g.memset(cmk, 0.0).then_inc(S("cmk_pool"), 1)
            pool.wait_ge(S("cmk_pool"), 1)
            g.affine_select(out=cmk, in_=cmk, compare_op=ALU.is_ge, fill=NEG, base=-31,
                            pattern=[[P, 4], [-32, 16]], channel_multiplier=1).then_inc(S("cmk_pool"), 1)
            pool.sem_inc(S("u_fof"), 1)
            for q in range(NFF):
                pool.wait_ge(S("u_fo"), q + 2)
                cols = slice(q * P, (q + 1) * P)
                pool.dma_start(O["fconv_p"][0, 0].rearrange("j (w n) -> j w n", w=2)[:, :, cols], fo[0:2]).then_inc(S("u_fos"), 16)
                pool.dma_start(O["fconv_s"][0].rearrange("b j (w n) -> (b j) w n", w=2)[:, :, cols], fo[2:18])\
                    .then_inc(S("u_fos"), 16)
                pool.wait_ge(S("u_fos"), 32 * (q + 1))
                pool.sem_inc(S("u_fof"), 1)

        def square_sum_act(act, n, ready, src):
            for k in range(KD):
                ready(act, k)
                if k >= 2:
                    act.wait_ge(S("norm_summed"), KD * (n - 2) + k - 1)
                nc.scalar.activation(sq[:, k % 2, :], src[:, k, :], ACT.Square).then_inc(S("norm_sq"), 1)
            act.wait_ge(S("norm_summed"), KD * (n - 1))
            nc.scalar.activation(rms[:, 0:TA], ps[6][:, 0:TA], ACT.Sqrt, bias=small[:, 0:1], scale=1.0 / D)
            nc.scalar.activation(rms[:, TA:T], ps[7][:, 0:TB], ACT.Sqrt, bias=small[:, 0:1],
                                 scale=1.0 / D).then_inc(S("norm_root"), 1)

        def square_sum_pe(pe, n, k):
            pe.wait_ge(S("norm_sq"), KD * (n - 2) + k + 1)
            nc.tensor.matmul(ps[6][:, 0:TA], ones[:], sq[:, k % 2, 0:TA], start=(k == 0), stop=(k == KD - 1))
            nc.tensor.matmul(ps[7][:, 0:TB], ones[:], sq[:, k % 2, TA:T], start=(k == 0),
                             stop=(k == KD - 1)).then_inc(S("norm_summed"), 1)

        def norm_dve(dve, src, gain):
            dve.wait_ge(S("norm_root"), 1)
            nc.vector.reciprocal(rstd, rms).then_inc(S("norm_rstd"), 1)
            dve.wait_ge(S("norm_rstd"), 1)
            for k in range(KD + 1):
                if k < KD:
                    if k >= 2:
                        dve.wait_ge(S("xn_lo"), k - 1)
                    nc.vector.scalar_tensor_tensor(out=xn[:, k % 2, :], in0=src[:, k, :], scalar=vcol[:, gain + k:gain + k + 1],
                                                   in1=rstd, op0=ALU.mult, op1=ALU.mult).then_inc(S("normed"), 1)
                if k:
                    dve.wait_ge(S("normed"), k)
                    dve.wait_ge(S("xn_hi"), k)
                    nc.vector.tensor_tensor(xlo[:, k - 1, :], xn[:, (k - 1) % 2, :], xhi[:, k - 1, :].bitcast(F32),
                                            ALU.subtract).then_inc(S("xn_lo"), 1)

        @block.scalar
        def _(act):
            a = nc.scalar
            act.wait_ge(S("filled"), 1)
            act.wait_ge(S("x_in"), 5 * 16)
            for i in range(NTILE):
                last = a.activation(xs[0:TROWS[i], i, :], xtok[0:TROWS[i], i, :], ACT.Square, accum_out=ss[0:TROWS[i], 0, i:i + 1])
            last.then_inc(S("x_stat"), 1)
            act.wait_ge(S("x_stat"), 1)
            a.activation(ss[:, 1, :], ss[:, 0, :], ACT.Sqrt, bias=small[:, 0:1], scale=1.0 / D).then_inc(S("x_stat"), 1)
            act.wait_ge(S("setup_dve"), 2)
            for k in range(1, KD, 2):
                act.wait_ge(S("x_turned"), KD + k + 1)
                a.activation(xnT[:, k, 0:SEQ], ps[1 + k % 4][:, :], ACT.Copy,
                             scale=vcol[:, V_GMIX + k:V_GMIX + k + 1]).then_inc(S("xn_act"), 1)
            act.wait_ge(S("pool_step"), 3)
            for n, (_, kind, i) in enumerate(jobs):
                bank, rest = ps[n % 3][:, 0:TA], ps[3 + n % 2][:, 0:TB]
                rows = TROWS[i]
                if kind in ("q", "mu", "mo") or kind == "kvB" or (kind in ("kvA", "mv") and i % 2):
                    act.wait_ge(S("job"), n + 1)
                if kind == "q":
                    a.activation(qT[:, i, 0:TA], bank, ACT.Copy).then_inc(S("ev_act"), 1)
                elif kind == "mu":
                    a.activation(uT[:, i, 3:3 + TA], bank, ACT.Copy).then_inc(S("ev_act"), 1)
                elif kind == "mo":
                    a.activation(moT[:, i, 0:TA], bank, ACT.Sigmoid)
                    a.activation(moT[:, i, TA:T], rest, ACT.Sigmoid).then_inc(S("ev_act"), 1)
                elif kind == "kvB":
                    a.activation(kv[0:rows, i, 512:768], ps[n % 3][0:rows, 0:256], ACT.Copy)
                    a.activation(gsig[0:rows, i, :], ps[n % 3][0:rows, 256:280], ACT.Sigmoid).then_inc(S("ev_act"), 1)
                elif kind == "kvA" and i % 2:
                    a.activation(kv[0:rows, i, 0:512], ps[n % 3][0:rows, :], ACT.Copy).then_inc(S("ev_act"), 1)
                elif kind == "mv" and i % 2:
                    a.activation(mv[0:rows, i, :, 0:P], ps[n % 3][0:rows, :].rearrange("p (h e) -> p h e", h=MH),
                                 ACT.Copy).then_inc(S("ev_act"), 1)
                if CONV_JOB + 1 <= n < CONV_JOB + 1 + MH:
                    k = n - CONV_JOB - 1
                    act.wait_ge(S("m_conv"), k + 1)
                    a.activation(ucT[:, k, 0:SEQ], conv[:, k % 2, 0:SEQ], ACT.Silu, bias=vcol[:, V_BCONV + k:V_BCONV + k + 1])
                    a.activation(ucT[:, k, SEQ:T].rearrange("p (b t) -> p b t", b=NB),
                                 conv_sample(k), ACT.Silu,
                                 bias=vcol[:, V_BCONV + k:V_BCONV + k + 1]).then_inc(S("m_uc"), 1)
                if n == GATE_JOB:
                    act.wait_ge(S("gates_dve"), 1)
                    a.activation(r0, r0, ACT.Exp, scale=-1.0).then_inc(S("m_ln"), 1)
                    act.wait_ge(S("m_ln"), 1)
                    a.activation(r0, r0, ACT.Ln, bias=small[0:MH, 3:4]).then_inc(S("m_ln"), 1)
                if n == GATE_JOB + 3:
                    act.wait_ge(S("gates_dve"), 2)
                    a.activation(frow, r3, ACT.Exp, scale=-1.0)
                    a.activation(r0, r0, ACT.Exp)
                    a.activation(r2[:, 0:NSMP], r2[:, 0:NSMP], ACT.Exp).then_inc(S("m_rows"), 1)
            act.sem_inc(S("c_xa"), 2)
            act.wait_ge(S("hb_made"), 1)
            a.activation(hb[:, 0:1], ps[5][:, 0:1], ACT.Copy)
            a.activation(hb[:, 1:2], ps[5][:, 1:2], ACT.Copy).then_inc(S("c_hid"), 2)
            act.wait_ge(S("c_hid"), 2)

            def compress_act(b, s, w):
                for kvi in range(2):
                    for f in (1, 3):
                        n = b * 8 + (4 * kvi + f)
                        act.wait_ge(S("c_turned"), n + 9)
                        act.wait_ge(S("c_mm"), n + 1)
                        a.activation(XT[:, f, 0:4 * w], ps[f][:, 0:4 * w], ACT.Copy).then_inc(S("c_xa"), 1)
                    act.wait_ge(S("c_mm"), b * 8 + (4 * kvi + 4 + 4))
                    act.wait_ge(S("c_kc"), b * 2 + (kvi + 1))
                    a.activation(hid[:, s, kvi, 0:w], ps[4 + kvi][:, 0:w], ACT.Silu,
                                 bias=hb[:, kvi:kvi + 1]).then_inc(S("c_hid"), 1)

            with act.Fori(0, NB // 2) as it:
                for s in range(2):
                    compress_act(it * 2 + s, s, P)
            compress_act(NB, 0, 32)

            for h in range(MH):
                act.wait_ge(S("m_proj"), h + 1)
                a.activation(mqT[:, 0:SEQ], ps[0][:, :], ACT.Copy)
                a.activation(mkT[:, 0:SEQ], ps[2][:, :], ACT.Copy, scale=KSCALE).then_inc(S("m_proja"), 1)
                act.wait_ge(S("m_e"), h + 1)
                for j in range(4):
                    dg = E[:, EOFF[j]:EOFF[j] + P]
                    a.activation(dg, dg, ACT.Exp)
                    if j < 3:
                        a.activation(E[:, EOFF[j] + P:EOFF[j + 1]], ps[3][:, (j + 1) * P:SEQ], ACT.Exp,
                                     bias=rcol[:, 0, j, h:h + 1])
                a.activation(E[0:NSMP, EW:EW + NSMP], E[0:NSMP, EW:EW + NSMP], ACT.Exp).then_inc(S("m_x"), 1)
                act.wait_ge(S("m_numd"), h + 1)
                for i in range(NTILE):
                    rows = TROWS[i]
                    last = a.activation(W[0:rows, i * P:(i + 1) * P], hs[0:rows, i, h, 0:P], ACT.Square,
                                        accum_out=s2[0:rows, 4 * i + h:4 * i + h + 1])
                last.then_inc(S("m_sq"), 1)
            act.wait_ge(S("heads_dve"), 1)
            a.activation(f2, f2, ACT.Sqrt, bias=small[:, 0:1], scale=1.0 / P).then_inc(S("m_root"), 1)

            act.sem_inc(S("s_kt"), 1)
            with act.Fori(0, 2) as it:
                for x in range(2):
                    p10 = it * 20 + 10 * x
                    p1 = it * 2 + x

                    def keys(n):
                        act.wait_ge(S("s_t"), p10 + (n + 1))
                        act.wait_ge(S("s_sc"), p10 + (n + 1))
                        a.activation(KTb[:, n % 2, :], ps[4 + n % 2], ACT.Copy).then_inc(S("s_kt"), 1)

                    keys(0)
                    keys(1)
                    act.wait_ge(S("s_cb"), p1 + 1)
                    for b2 in range(2):
                        r = slice(64 * b2, 64 * b2 + 64)
                        last = a.activation(pcd[r, r], ps[7][r, 16:80], ACT.Exp, bias=col[r, 0:1], scale=SCALE,
                                            accum_out=col[r, 1:2])
                    last.then_inc(S("s_ce"), 1)
                    for n in range(2, 7):
                        keys(n)
                    act.wait_ge(S("s_wb"), p1 + 1)
                    a.activation(Sw, Sw, ACT.Exp, bias=col[:, 2:3], scale=SCALE, accum_out=col[:, 5:6]).then_inc(S("s_we"), 1)
                    for n in range(7, 10):
                        keys(n)
                    act.wait_ge(S("s_sb"), p1 + 1)
                    a.activation(Ss, Ss, ACT.Exp, bias=col[:, 3:4], scale=SCALE, accum_out=col[:, 4:5]).then_inc(S("s_se"), 1)
            act.sem_inc(S("p_exp"), 2)
            act.sem_inc(S("p_pta"), 1)
            act.wait_ge(S("cmp_dve"), 1)
            a.activation(Pc, Pc, ACT.Exp, scale=SCALE).then_inc(S("p_cexp"), 1)
            with act.Fori(0, GRP) as g:
                for step in range(10):
                    if step < 8:
                        u = step
                        i, h = UNITS[u]
                        n = (i + 1) * P
                        act.wait_ge(S("p_max"), g * 8 + (u + 1))
                        act.wait_ge(S("p_tr"), g * 8 + (u + 1))
                        for w in range(2):
                            last = a.activation(Pb[:, u % 2, w, 0:n], ps[2 * (u % 2) + w][:, 0:n], ACT.Exp,
                                                bias=cst[:, u % 2, 1, w:w + 1], scale=SCALE, accum_out=cst[:, u % 2, 2, w:w + 1])
                        last.then_inc(S("p_exp"), 1)
                    if 1 <= step < 9:
                        u = step - 1
                        n = (UNITS[u][0] + 1) * P
                        act.wait_ge(S("p_tr"), g * 8 + (u + 3))
                        act.wait_ge(S("p_pv"), g * 8 + (u + 1))
                        a.activation(PTp[:, u % 2, 1, 0:n], ps[5][:, 0:n], ACT.Copy).then_inc(S("p_pta"), 1)
            act.wait_ge(S("o_dve"), 1)
            for i in range(NTILE):
                rows = TROWS[i]
                last = a.activation(sqo[0:rows, i, :],
                                    oatt[0:rows, i, :], ACT.Square, accum_out=nss[0:rows, i:i + 1])
            last.then_inc(S("o_act"), 1)
            act.wait_ge(S("o_act"), 1)
            a.activation(nss[:, 8:13], nss[:, 0:5], ACT.Sqrt, bias=small[:, 0:1], scale=1.0 / 512).then_inc(S("o_act"), 1)
            def split_up_act(slot, arrived):
                act.wait_ge(S(f"slab_in{slot}"), arrived)
                for w in range(2):
                    a.activation(whi[slot][:, 2048 * w:2048 * (w + 1)], ring[:, slot, 2048 * w:2048 * (w + 1)],
                                 ACT.Copy).then_inc(S("u_hi"), 1)

            def h_ready(act, k):
                if k == 6:
                    split_up_act(0, 48 + 64)
                act.wait_ge(S("h_done"), k + 1)

            square_sum_act(act, 2, h_ready, xT)
            for k in range(KD):
                act.wait_ge(S("normed"), k + 1)
                a.activation(xhi[:, k, :], xn[:, k % 2, :], ACT.Copy).then_inc(S("xn_hi"), 1)

            def up_act(par, qn, split):
                act.wait_ge(S("u_mm"), qn + 1)
                act.wait_ge(S("u_conv"), qn + 1)
                a.activation(pad[:, par, :, 2:2 + UA], ps[4 + par].rearrange("p (w t) -> p w t", w=2), ACT.Copy)
                for w in range(2):
                    a.activation(pad[:, par, w, 2 + UA:2 + SEQ], ps[2 * w + par][:, 0:SEQ - UA], ACT.Copy)
                    last = a.activation(pad[:, par, w, 2 + SEQ:FPW].rearrange("p (b t) -> p b t", b=NB)[:, :, 2:2 + TS],
                                        ps[2 * w + par][:, SEQ - UA:UB].rearrange("p (b t) -> p b t", b=NB), ACT.Copy)
                last.then_inc(S("u_pad"), 1)
                split()
                act.wait_ge(S("u_cg"), qn + 1)
                a.activation(cg, cg, ACT.Silu).then_inc(S("u_silu"), 1)

            with act.Fori(0, 5) as it:
                for q in range(4):
                    if q == 0:
                        up_act(0, it * 4, lambda: split_up_act(1, it * 64 + (64 + 64)))
                    elif q == 2:
                        up_act(0, it * 4 + 2, lambda: split_up_act(0, it * 64 + (48 + 128)))
                    else:
                        up_act(1, it * 4 + q, lambda: None)

            def split_down_act(s, first):
                act.wait_ge(S(f"dn_in{s}"), first)
                for k0, n, where in dhi_runs[s]:
                    last = a.activation(where, draw[s][:, k0:k0 + n, :].rearrange("p k n -> p (k n)"), ACT.Copy)
                last.then_inc(S("d_hi"), 1)

            def act_hi(k):
                act.wait_ge(S("u_act"), k + 2)
                a.activation(ahi[k], actT[:, k, :], ACT.Copy).then_inc(S("a_hi"), 1)

            up_act(0, 20, lambda: split_down_act(0, 16))
            up_act(1, 21, lambda: [act_hi(k) for k in range(12)])
            for k in range(12, NFF):
                act_hi(k)

            def down_act(s, mn, first, split, turned):
                if split:
                    split_down_act(1 - s, first)
                if turned:
                    squares(1 - s, mn)

            def squares(s, mn):
                act.wait_ge(S("d_turned"), mn)
                act.wait_ge(S("d_sq"), mn)
                for i in range(NTILE):
                    rows = TROWS[i]
                    src = ps[4 + s][:, i * P:(i + 1) * P] if i < 4 else ps[6 + s][0:rows, 0:P]
                    dst = sqs[:, i, :] if i < 4 else vc_s[0:rows, 0, :]
                    m1 = mn + (-1)
                    last = a.activation(dst, src, ACT.Square, accum_out=ssy[0:rows, i, bass.ds(m1, 1)])
                last.then_inc(S("d_sq"), 1)

            act.sem_inc(S("d_sq"), 1)
            down_act(0, 0, 16, True, False)
            with act.Fori(0, 3) as it:
                for x in range(2):
                    down_act((1 + x) % 2, it * 2 + (1 + x), it * 16 + (32 if x == 0 else 32), True, True)
            down_act(1, 7, 0, False, True)
            squares(1, 8)
            act.wait_ge(S("y_sum"), 1)
            a.activation(yrt, yrt, ACT.Sqrt, bias=small[:, 0:1], scale=1.0 / D).then_inc(S("y_root"), 1)
            act.wait_ge(S("y_sum"), 2)
            for i in range(0, NTILE, 2):
                rows = TROWS[i]
                a.activation(ytok[0:rows, i, :], ytok[0:rows, i, :], ACT.Copy, scale=yrt[0:rows, i:i + 1]).then_inc(S("y_act"), 1)


        @block.tensor
        def _(pe):
            t = nc.tensor
            pe.wait_ge(S("pool_step"), 1)
            pe.wait_ge(S("x_in"), 5 * 16)

            def turn_tokens(src, k, smp):
                for i in range(4):
                    t.transpose(ps[1 + k % 4][:, i * P:(i + 1) * P], src[:, i, k * P:(k + 1) * P], ident[:])
                return t.transpose(smp[:, k * NSMP:(k + 1) * NSMP], src[0:NSMP, 4, k * P:(k + 1) * P], ident[0:NSMP, 0:NSMP])

            for k in range(KD):
                if k >= 4:
                    pe.wait_ge(S("x_dve"), k - 3)
                turn_tokens(xtok, k, ps[5]).then_inc(S("x_turned"), 1)
            pe.wait_ge(S("vec_in"), 14 * 16)
            t.transpose(ps[0][:, 0:V_ROWS], vrows[0:V_ROWS, :], ident[0:V_ROWS, 0:V_ROWS])
            for k in range(MH):
                t.transpose(ps[0][:, V_MCS + 24 * k:V_MCS + 24 * k + 24], mcs[0:24, k * P:(k + 1) * P], ident[0:24, 0:24])
            t.transpose(ps[0][:, V_N:V_N + 32], nrows[0:32, :], ident[0:32, 0:32]).then_inc(S("vec_turned"), 1)
            pe.wait_ge(S("x_dve"), KD + 1)
            pe.wait_ge(S("x_scaled"), 1)
            for k in range(KD):
                if k >= 4:
                    pe.wait_ge(S("xn_act" if k % 2 else "xn_dve"), k // 2 - 1)
                turn_tokens(xs, k, ps[6]).then_inc(S("x_turned"), 1)
            pe.wait_ge(S("setup_dve"), 2)
            arrived = 0
            for n, (sl, kind, i) in enumerate(jobs):
                if n == 0:
                    pe.wait_ge(S("xn_act"), 4)
                    pe.wait_ge(S("xn_dve"), 5)
                if n >= 2 and evac[n - 2][0]:
                    pe.wait_ge(S("ev_act"), evac[n - 2][0])
                if n >= 2 and evac[n - 2][1]:
                    pe.wait_ge(S("ev_dve"), evac[n - 2][1])
                if kind == "gates":
                    pe.wait_ge(S("wg_in"), 32)
                elif n == 0:
                    pe.wait_ge(S("q_in"), 8 * 16)
                elif sl != jobs[n - 1][0]:
                    pe.wait_ge(S(f"slab_in{sl % 2}"), 16 * (sl // 2 + sl % 2))
                wt = ring[:, sl % 2, :].rearrange("p (k n) -> p k n", k=KD)
                bank, smp = ps[n % 3], ps[3 + n % 2]
                for k in range(KD):
                    on = dict(start=(k == 0), stop=(k == KD - 1))
                    if kind in ("q", "mu", "mo", "gates"):
                        if kind == "gates":
                            w = wg[:, k, :]
                        else:
                            w = wt[:, k, i * P:(i + 1) * P]
                        m = 36 if kind == "gates" else P
                        t.matmul(bank[0:m, 0:TA], w, xnT[:, k, 0:TA], **on)
                        last = t.matmul(smp[0:m, 0:TB], w, xnT[:, k, TA:T], **on)
                    else:
                        w = SLABS[sl][1]
                        last = t.matmul(bank[0:TROWS[i], 0:w], xnT[:, k, i * P:i * P + TROWS[i]], wt[:, k, 0:w], **on)
                last.then_inc(S("job"), 1)
            pe.wait_ge(S("ev_act"), evac[-1][0])
            pe.wait_ge(S("ev_dve"), evac[-1][1])
            pe.wait_ge(S("w1_in"), 4 * 16)
            for kvi in range(2):
                for cc in range(16):
                    last = t.matmul(ps[5][:, kvi:kvi + 1], w1c[:, kvi, cc, :],
                                    vcol[:, V_PE + 16 * kvi + cc:V_PE + 16 * kvi + cc + 1],
                                    start=(cc == 0), stop=(cc == 15))
            last.then_inc(S("hb_made"), 1)
            pe.sem_inc(S("c_turned"), 8)
            pe.sem_inc(S("c_mm"), 4)
            pe.sem_inc(S("c_kc"), 4)

            def turn(b, s, n, rows):
                kvi, f = n // 4, n % 4
                ct = packed[0:rows, kvi, :].rearrange("p (h j d) -> p h j d", h=2, j=16)
                if f == 0:
                    pe.wait_ge(S("c_packed"), b * 2 + (kvi + 1))
                if f % 2:
                    pe.wait_ge(S("c_xa"), b * 4 + (n // 2 + 1))
                else:
                    pe.wait_ge(S("c_xd"), b * 4 + (n // 2 + 1))
                for c2 in range(2):
                    for h in range(2):
                        j = 2 * (2 * f + c2)
                        at = (2 * c2 + h) * rows
                        last = t.transpose(ps[f][:, at:at + rows], ct[:, h, j:j + 2, :], ident[0:rows, 0:rows])
                last.then_inc(S("c_turned"), 1)

            def hidden(b, s, n, rows):
                kvi, f = n // 4, n % 4
                if f == 0:
                    pe.wait_ge(S("c_hid"), b * 2 + (kvi + 1))
                if f % 2:
                    pe.wait_ge(S("c_xa"), b * 4 + (n // 2 + 3))
                else:
                    pe.wait_ge(S("c_xd"), b * 4 + (n // 2 + 3))
                nb = rows // 2
                for c2 in range(2):
                    for half in range(2):
                        x = XT[:, f, 2 * c2 * rows:2 * (c2 + 1) * rows].rearrange("p (h n f) -> p h n f", h=2, f=2)[:, :, :, half]
                        last = t.matmul(ps[4 + kvi][:, 0:rows], w1c[:, kvi, half * 8 + 2 * f + c2, :], x,
                                        start=(f == 0 and c2 == 0 and half == 0), stop=(f == 3 and c2 == 1 and half == 1))
                last.then_inc(S("c_mm"), 1)

            def second(b, s, kvi, rows):
                pe.wait_ge(S("c_hid"), b * 2 + (kvi + 3))
                pe.wait_ge(S("c_kcd"), b * 2 + (kvi + 1))
                nb = rows // 2
                for h in range(2):
                    hv = hid[:, s, kvi, h * nb:(h + 1) * nb]
                    if kvi == 0:
                        last = t.matmul(ps[6][64 * h:64 * h + 64, 0:nb], w2c[:, 0, :], hv, start=True, stop=True)
                    else:
                        last = t.matmul(ps[7][64 * s:64 * s + nb, 64 * h:64 * h + 64], hv, w2c[:, 1, :],
                                        start=True, stop=True)
                last.then_inc(S("c_kc"), 1)

            def compress_pe(b, s, rows):
                turn(b, s, 0, rows)
                for n in range(8):
                    if n < 7:
                        turn(b, s, n + 1, rows)
                    hidden(b, s, n, rows)
                    if n == 5:
                        second(b, s, 0, rows)
                second(b, s, 1, rows)

            with pe.Fori(0, NB // 2) as it:
                for s in range(2):
                    compress_pe(it * 2 + s, s, P)
            compress_pe(NB, 0, 32)

            pe.wait_ge(S("c_xa"), 2 + 4 * 9)
            pe.wait_ge(S("c_xd"), 2 + 4 * 9)
            pe.wait_ge(S("c_hid"), 2 + 2 * 9)
            pe.wait_ge(S("c_kcd"), 2 + 2 * 9)
            pe.wait_ge(S("m_mcg"), 1)
            for k in range(MH):
                last = t.transpose(ps[5][0:27, k * P:(k + 1) * P], mcg[:, k, :], ident[:])
            last.then_inc(S("m_mco"), 1)
            pe.wait_ge(S("wqk_in"), 48)

            def project(h):
                if h:
                    pe.wait_ge(S("m_w"), h)
                    pe.wait_ge(S("m_e"), h)
                pe.wait_ge(S("m_uc"), h + 1)
                for w, b in ((0, 0), (1, 2)):
                    t.matmul(ps[b][:, :], wqk[:, w, h, :], ucT[:, h, 0:SEQ], start=True, stop=True)
                    t.matmul(ps[1][:, NSMP * w:NSMP * (w + 1)], wqk[:, w, h, :], ucT[:, h, SEQ:T], start=True, stop=True)
                for i in range(4):
                    t.matmul(ps[4][:, i * P:(i + 1) * P], ucT[:, h, i * P:(i + 1) * P], wqk[:, 1, h, :], start=True, stop=True)
                t.matmul(ps[1][0:NSMP, P:2 * P], ucT[:, h, SEQ:T], wqk[:, 1, h, :], start=True,
                         stop=True).then_inc(S("m_proj"), 1)

            project(0)
            pe.wait_ge(S("m_rows"), 1)
            for kind, row in enumerate((irow, frow, r0)):
                for i in range(NTILE):
                    at = (kind * NTILE + i) * MH
                    t.transpose(ps[3][0:TROWS[i], at:at + MH], row[:, i * P:i * P + TROWS[i]], ident[0:MH, 0:MH])
            t.transpose(ps[3][0:NB, 60:64], r2[:, TS - 1:NSMP:TS], ident[0:MH, 0:MH]).then_inc(S("m_cols"), 1)
            pe.wait_ge(S("m_rcol"), 1)
            for h in range(MH):
                if h:
                    project(h)
                pe.wait_ge(S("m_projd"), h + 1)
                pe.wait_ge(S("m_rows"), 1)
                if h:
                    pe.wait_ge(S("m_x"), h)
                t.matmul(ps[3][:, :], selh[:, h, :], r1[:, 0:SEQ], start=True, stop=True)
                t.matmul(ps[1][0:NSMP, 0:NSMP], selh[:, h, 0:NSMP], r1[:, SEQ:T], start=True, stop=True)
                t.matmul(ps[1][:, NSMP:2 * NSMP], selh[:, h, :], r2[:, 0:NSMP], start=True, stop=True)
                t.matmul(ps[1][:, 2 * NSMP:2 * NSMP + NB], selh[:, h, :], r2[:, TS - 1:NSMP:TS], start=True,
                         stop=True).then_inc(S("m_spread"), 1)
                pe.wait_ge(S("m_proja"), h + 1)
                for j in range(4):
                    out = (ps[0][:, :], ps[2][:, 0:384], ps[4][:, 0:256], ps[4][:, 256:384])[j]
                    t.matmul(out, mkT[:, j * P:(j + 1) * P], mqT[:, j * P:SEQ], start=True, stop=True)
                t.matmul(ps[4][0:NSMP, 384:384 + NSMP], mkT[:, SEQ:T], mqT[:, SEQ:T], start=True,
                         stop=True).then_inc(S("m_qk"), 1)
                pe.wait_ge(S("m_cin"), 16 * (NB + h + 1))
                for x in range(2):
                    if 5 * h + x:
                        pe.wait_ge(S("m_p7d"), 5 * h + x)
                    for b in range(4):
                        last = t.transpose(ps[7][:, b * P:(b + 1) * P], Cst[:, 4 * x + b, :], ident[:])
                    last.then_inc(S("m_p7"), 1)
                pe.wait_ge(S("m_w"), h + 1)
                pe.wait_ge(S("m_p7d"), 5 * h + 2)
                if h:
                    pe.wait_ge(S("m_numd"), h)
                else:
                    pe.wait_ge(S("m_mcod"), 1)
                for i in range(4):
                    out = ps[5][:, i * (P + 1):(i + 1) * (P + 1)] if i < 3 else ps[6][:, 0:P + 1]
                    for j in range(i + 1):
                        at = EOFF[j] + (i - j) * P
                        t.matmul(out, W[:, at:at + P], mv[:, j, h, :], start=(j == 0), stop=(j == i))
                out = ps[6][0:NSMP, P + 1:2 * (P + 1)]
                t.matmul(out, W[0:NSMP, EW:EW + NSMP], mv[0:NSMP, 4, h, :], start=True, stop=False)
                for b in range(NB):
                    last = t.matmul(out, Qm[:, b, :], CT[:, b, :], start=False, stop=(b == NB - 1))
                last.then_inc(S("m_num"), 1)
                pe.wait_ge(S("m_upd"), h + 1)
                for x in range(2):
                    t.matmul(ps[7][:, :], vw[0:NSMP, 4, :], kbd[0:NSMP, 4 * x:4 * x + 4, :].rearrange("p b d -> p (b d)"),
                             start=True, stop=True).then_inc(S("m_p7"), 1)
                    pe.wait_ge(S("m_p7d"), 5 * h + 3 + x)
                for i in range(4):
                    t.matmul(ps[7][:, 0:P], vw[:, i, :], mk[:, i, :], start=(i == 0), stop=(i == 3))
                for i in range(4):
                    t.matmul(ps[7][0:1, P:2 * P], rcol[:, 2, i, h:h + 1], mk[:, i, :], start=(i == 0), stop=(i == 3))
                t.matmul(ps[7][0:NB, 2 * P:3 * P], wlb[0:NSMP, :], mk[0:NSMP, 4, :], start=True,
                         stop=True).then_inc(S("m_p7"), 1)
            pe.wait_ge(S("heads_dve"), 2)
            pe.wait_ge(S("m_w"), MH)
            pe.wait_ge(S("m_x"), MH)
            for h in range(MH):
                for i in range(4):
                    t.transpose(ps[h][:, i * P:(i + 1) * P], hs[:, i, h, 0:P], ident[:])
                t.transpose(ps[4 + h][:, 0:NSMP], hs[0:NSMP, 4, h, 0:P],
                            ident[0:NSMP, 0:NSMP]).then_inc(S("m_hT"), 1)

            pe.wait_ge(S("m_mix"), MH)
            for w in range(2):
                for i in range(NTILE):
                    rows = TROWS[i]
                    out = ps[2 * w][:, i * P:(i + 1) * P] if i < 4 else ps[2 * w + 1][:, 0:NSMP]
                    last = t.transpose(out, kv[0:rows, i, 256 + 256 * w:384 + 256 * w], ident[0:rows, 0:rows])
            last.then_inc(S("k_turned"), 1)
            pe.wait_ge(S("kv_dve"), 2)
            pe.sem_inc(S("s_sc"), 2)
            with pe.Fori(0, 2) as it:
                for x in range(2):
                    p10 = it * 20 + 10 * x
                    p1 = it * 2 + x
                    kvs = [slots[2 * x], slots[2 * x + 1]]
                    kvw = [wkv[:, 2 * x, :], wkv[:, 2 * x + 1, :]]
                    pe.wait_ge(S("s_stage"), p1 + 1)
                    pe.wait_ge(S("s_out"), p1 + 1)
                    pe.wait_ge(S("s_pt"), p1 + 1)
                    for b2 in range(2):
                        r = slice(64 * b2, 64 * b2 + 64)
                        q = Qp[:, 64 * b2:64 * b2 + 64]
                        for w in range(2):
                            t.matmul(ps[7][r, 8 * w:8 * w + 8], q, ktn[:, w, b2 * TS:(b2 + 1) * TS], start=True, stop=True)
                        last = t.matmul(ps[7][r, 16:80], q, kcp[:, 64 * b2:64 * b2 + 64], start=True, stop=True)
                    last.then_inc(S("s_cmp"), 1)

                    def turn_keys(n):
                        if n == 0:
                            pe.wait_ge(S(f"win_in{x}"), it * 32 + 32)
                        if n == 2:
                            pe.wait_ge(S(f"sel_in{2 * x}"), it * 16 + 16)
                        if n == 6:
                            pe.wait_ge(S(f"sel_in{2 * x + 1}"), it * 16 + 16)
                        if n < 2:
                            src, j0 = kvw[n], 0
                            pe.wait_ge(S("s_kt"), p10 + (n + 0 if n else 1))
                        else:
                            src, j0 = kvs[(n - 2) // 4], 4 * ((n - 2) % 4)
                            pe.wait_ge(S("s_kt"), p10 + n)
                        for j in range(4):
                            last = t.transpose(ps[4 + n % 2][:, j * P:(j + 1) * P],
                                               src[:, (j0 + j) * 256:(j0 + j) * 256 + P], ident[:])
                        last.then_inc(S("s_t"), 1)

                    def score(n):
                        pe.wait_ge(S("s_kt"), p10 + (n + 2))
                        b2 = n if n < 2 else (n - 2) // 4
                        bank = ps[6] if n < 2 else ps[(n - 2) % 4]
                        t.matmul(bank[64 * b2:64 * b2 + 64, :], Qp[:, 64 * b2:64 * b2 + 64], KTb[:, n % 2, :], start=True,
                                 stop=True).then_inc(S("s_sc"), 1)

                    turn_keys(0)
                    for n in range(10):
                        if n < 9:
                            turn_keys(n + 1)
                        score(n)
                        if n == 4:
                            pe.wait_ge(S("s_pn"), p1 + 1)
                            t.matmul(ps[7][:, P:2 * P], gsum[:], pcd, start=True, stop=True)
                            t.transpose(ps[7][:, 2 * P:3 * P], pcd, ident[:]).then_inc(S("s_imp"), 1)
                    pe.wait_ge(S("s_we"), p1 + 1)
                    for j in range(4):
                        t.transpose(ps[6][:, j * P:(j + 1) * P], Sw[:, j * P:(j + 1) * P], ident[:])
                    pe.wait_ge(S("s_pc"), p1 + 1)
                    t.transpose(ps[7][0:TS, P:2 * P], Sw[:, WIN:WIN + TS], ident[:]).then_inc(S("s_wT"), 1)
                    pe.wait_ge(S("s_se"), p1 + 1)
                    for j in range(16):
                        t.transpose(ps[j // 4][:, (j % 4) * P:(j % 4 + 1) * P], Ss[:, j * P:(j + 1) * P], ident[:])
                    t.transpose(ps[5][0:TS, 0:P], Ss[:, PAST:PAST + TS], ident[:]).then_inc(S("s_sT"), 1)
                    pe.wait_ge(S("s_pt"), p1 + 2)
                    both = (ring if x == 0 else ring2)[:, :, :].rearrange("p s (j k n) -> p s j k n", j=16, k=2)
                    wins = wkv[:, 2 * x:2 * x + 2, :].rearrange("p s (j k n) -> p s j k n", j=4, k=2)
                    for j in range(4):
                        t.matmul(ps[1][:, 0:256], PTw[:, j, :], wins[:, :, j, 1, :], start=(j == 0), stop=False)
                    t.matmul(ps[1][:, 0:256], PTn[:, 1, :], vnp[:, :, 1, :], start=False, stop=True)
                    t.matmul(ps[2][:, 0:P], PTc, vcp, start=True, stop=True)
                    for j in range(16):
                        t.matmul(ps[0][:, 0:256], PT[:, j, :], both[:, :, j, 1, :], start=(j == 0), stop=False)
                    t.matmul(ps[0][:, 0:256], PTn[:, 0, :], vnp[:, :, 0, :], start=False, stop=True).then_inc(S("s_pv"), 1)
            pe.wait_ge(S("s_out"), 5)
            pe.wait_ge(S("s_pt"), 5)
            for i in range(4):
                for hd in range(HEADS):
                    h, g = hd // GRP, hd % GRP
                    at = (i * GRP + g) * 16
                    last = t.matmul(ps[h][:, at:at + 16], qT[64 * h:64 * h + 64, g, i * P:(i + 1) * P], kcT_p[64 * h:64 * h + 64, :],
                                    start=True, stop=True)
            last.then_inc(S("cmp_pe"), 1)
            pe.wait_ge(S("cmp_dve"), 2)
            for i in range(4):
                last = t.transpose(ps[1][:, i * P:(i + 1) * P], Pc[:, i * P:(i + 1) * P], ident[:])
            last.then_inc(S("cmp_pe"), 1)
            pe.wait_ge(S("cmp_dve"), 3)
            pe.wait_ge(S("vbd_in"), HEADS * 16)
            for i in range(4):
                last = t.matmul(ps[2 + i], PcT[:, i, :], Vbd, start=True, stop=True)
            last.then_inc(S("cmp_pe"), 1)
            pe.wait_ge(S("cmp_dve"), 4)
            pe.sem_inc(S("p_tr"), 2)
            pe.sem_inc(S("p_pv"), 2)
            with pe.Fori(0, GRP) as g:
                for step in range(10):
                    if step < 8:
                        u = step
                        i, h = UNITS[u]
                        n = (i + 1) * P
                        if u == 0:
                            pe.wait_ge(S("p_stage"), g + 1)
                        pe.wait_ge(S("p_exp"), g * 8 + (u + 1))
                        for w in range(2):
                            last = t.matmul(ps[2 * (u % 2) + w][:, 0:n], qst[:, h, i * P:(i + 1) * P],
                                            ktT[:, w, 0:n], start=True, stop=True)
                        last.then_inc(S("p_sc"), 1)
                    if 1 <= step < 9:
                        u = step - 1
                        i = UNITS[u][0]
                        pe.wait_ge(S("p_exp"), g * 8 + (u + 3))
                        pe.wait_ge(S("p_pta"), g * 8 + (u + 1))
                        pe.wait_ge(S("p_ptd"), g * 8 + (u + 1))
                        for w in range(2):
                            for j in range(i + 1):
                                last = t.transpose(ps[4 + w][:, j * P:(j + 1) * P], Pb[:, u % 2, w, j * P:(j + 1) * P], ident[:])
                        last.then_inc(S("p_tr"), 1)
                    if step >= 2:
                        u = step - 2
                        i, h = UNITS[u]
                        pe.wait_ge(S("p_pta"), g * 8 + (u + 2))
                        pe.wait_ge(S("p_ptd"), g * 8 + (u + 2))
                        pe.wait_ge(S("p_fin"), g * 8 + (u + 1))
                        for w in range(2):
                            for j in range(i + 1):
                                at = 384 + 256 * w + 64 * h
                                last = t.matmul(ps[6 + u % 2][:, w * HD:(w + 1) * HD], PTp[:, u % 2, w, j * P:(j + 1) * P],
                                                kv[:, j, at:at + HD], start=(j == 0), stop=(j == i))
                        last.then_inc(S("p_pv"), 1)
            pe.wait_ge(S("o_dve"), 2)
            for f in range(4):
                for i in range(4):
                    t.transpose(ps[f][:, i * P:(i + 1) * P], oatt[:, i, f * P:(f + 1) * P], ident[:])
                t.transpose(ps[4 + f][:, 0:NSMP], oatt[0:NSMP, 4, f * P:(f + 1) * P],
                            ident[0:NSMP, 0:NSMP]).then_inc(S("o_turned"), 1)
            pe.wait_ge(S("o_mix"), 4)
            for m in range(KD):
                if m % 4 == 0:
                    pe.wait_ge(S(f"slab_in{m // 4}"), 48 + m // 4 * 16)
                if m >= 2:
                    pe.wait_ge(S("h_done"), m - 1)
                wt = ring[:, m // 4, :].rearrange("p (k n) -> p k n", k=KD)
                for k in range(KD):
                    w = wt[:, k, (m % 4) * P:(m % 4 + 1) * P]
                    t.matmul(ps[m % 2][:, 0:TA], w, xnT[:, k, 0:TA], start=(k == 0), stop=(k == KD - 1))
                    last = t.matmul(ps[2 + m % 2][:, 0:TB], w, xnT[:, k, TA:T], start=(k == 0), stop=(k == KD - 1))
                last.then_inc(S("h_mm"), 1)
                if m:
                    square_sum_pe(pe, 2, m - 1)
            square_sum_pe(pe, 2, KD - 1)
            pe.wait_ge(S("h_done"), KD)

            def up_pe(slot, sub, par, qn, norm=False):
                hi = whi[slot].rearrange("p (w k n) -> p w k n", w=2, k=KD)
                lo = ring_r[:, slot, :].rearrange("p (w k n) -> p w k n", w=2, k=KD)
                pe.wait_ge(S("u_pad"), qn + 1)
                pe.wait_ge(S("u_fc"), qn + 1)
                for w in range(2):
                    for k in range(KD):
                        if norm and w == 0:
                            pe.wait_ge(S("xn_lo"), k + 1)
                        if w == 0 and k == 1:
                            for z in range(2):
                                last = t.transpose(ps[6][:, 32 * z:32 * z + 19], fin[:, slot, z, sub * P:(sub + 1) * P],
                                                   ident[0:19, 0:19])
                            last.then_inc(S("u_ft"), 1)
                        c = slice(sub * P, (sub + 1) * P)
                        for n, (wk, x) in enumerate(((hi, xhi), (hi, xlo), (lo, xhi))):
                            on = dict(start=(k == 0 and n == 0), stop=(k == KD - 1 and n == 2))
                            first = dict(start=(k == 0 and n == 0 and w == 0), stop=(k == KD - 1 and n == 2))
                            t.matmul(ps[4 + par][:, w * UA:(w + 1) * UA], wk[:, w, k, c], x[:, k, 0:UA],
                                     skip_group_check=True, **first)
                            last = t.matmul(ps[2 * w + par][:, 0:UB], wk[:, w, k, c], x[:, k, UA:T], **on)
                last.then_inc(S("u_mm"), 1)

            def last_cols(qn):
                pe.wait_ge(S("u_l18"), qn + 1)
                pe.wait_ge(S("u_fo"), qn + 1)
                for w in range(2):
                    last = t.transpose(ps[7][0:18, w * P:(w + 1) * P], l18[:, w, :], ident[:])
                last.then_inc(S("u_lT"), 1)

            pe.wait_ge(S("u_lo"), 2)
            up_pe(0, 0, 0, 0, norm=True)
            with pe.Fori(0, 5) as it:
                for q in range(4):
                    if q % 2:
                        pe.wait_ge(S("u_lo"), it * 4 + (q + 3))
                    up_pe((q + 1) // 2 % 2, (q + 1) % 2, (q + 1) % 2, it * 4 + (q + 1))
                    last_cols(it * 4 + q)
            up_pe(0, 1, 1, 21)
            last_cols(20)
            def down_pe(s, mn, first=False):
                pe.wait_ge(S("d_lo"), mn + 1)
                if not first:
                    pe.wait_ge(S("d_add"), mn + 1)
                for k in range(NFF):
                    if first:
                        pe.wait_ge(S("a_lo"), k + 1)
                        if k == 8:
                            last_cols(21)
                    for n, (w, x) in enumerate(((dhi[s][k], ahi[k]), (dhi[s][k], alo[k]), (dlo[s][:, k, :], ahi[k]))):
                        on = dict(start=(k == 0 and n == 0), stop=(k == NFF - 1 and n == 2))
                        t.matmul(ps[s][:, 0:UA], w, x[:, 0:UA], **on)
                        last = t.matmul(ps[2 + s][:, 0:UB], w, x[:, UA:T], **on)
                last.then_inc(S("d_mm"), 1)

            def turn_y(s, mn):
                pe.wait_ge(S("d_add"), mn + 2)
                pe.wait_ge(S("d_out"), mn)
                for i in range(4):
                    t.transpose(ps[4 + s][:, i * P:(i + 1) * P], hst[:, s, i * P:(i + 1) * P], ident[:])
                t.transpose(ps[6 + s][0:NSMP, 0:P], hst[:, s, SEQ:T], ident[:]).then_inc(S("d_turned"), 1)

            pe.wait_ge(S("u_pad"), NFF + 2)
            down_pe(0, 0, first=True)
            pe.wait_ge(S("u_fo"), NFF + 1)
            with pe.Fori(0, 3) as it:
                for x in range(2):
                    down_pe((1 + x) % 2, it * 2 + (1 + x))
                    turn_y(x % 2, it * 2 + (1 + x))
            down_pe(1, 7)
            turn_y(0, 7)
            turn_y(1, 8)

        @block.vector
        def _(dve):
            v = nc.vector
            links = [0]

            def link(ins):
                links[0] += 1
                ins.then_inc(S("v_link"), 1)
                dve.wait_ge(S("v_link"), links[0])

            dve.wait_ge(S("pool_step"), 2)
            dve.wait_ge(S("idx_in"), NB * 16)
            part = b1["part"].bitcast(I32)
            link(v.tensor_scalar(part[:, 1:2], part[:, 0:1], 7, None, ALU.bitwise_and))
            link(v.tensor_copy(small[:, 1:2], part[:, 1:2]))
            v.tensor_scalar(idx[:], idx[:], 8.0, small[:, 1:2], ALU.mult, ALU.add).then_inc(S("setup_dve"), 1)
            v.tensor_scalar(winmask[:], b1["wrow"].bitcast(I32), small[:, 1:2], NEG, ALU.is_le, ALU.mult)
            v.tensor_scalar(newmask[:], b1["newk"].bitcast(I32), small[:, 1:2], NEG, ALU.is_gt, ALU.mult)
            dve.wait_ge(S("pool_step"), 4)
            v.scalar_tensor_tensor(out=gsum[:], in0=b1["mod"].bitcast(I32), scalar=small[:, 1:2], in1=gsum[:],
                                   op0=ALU.is_equal, op1=ALU.mult)
            for k in range(KD):
                dve.wait_ge(S("x_turned"), k + 1)
                v.tensor_copy(xT[:, k, 0:SEQ], ps[1 + k % 4][:, :]).then_inc(S("x_dve"), 1)
            v.tensor_copy(xT[:, :, SEQ:T], ps[5][:, :].rearrange("p (k t) -> p k t", k=KD)).then_inc(S("x_dve"), 1)
            dve.wait_ge(S("x_stat"), 2)
            link(v.reciprocal(ss[:, 1, :], ss[:, 1, :]))
            for i in range(NTILE):
                rows = TROWS[i]
                last = v.tensor_scalar(xs[0:rows, i, :], xtok[0:rows, i, :], ss[0:rows, 1, i:i + 1], None, ALU.mult)
            last.then_inc(S("x_scaled"), 1)
            dve.wait_ge(S("vec_turned"), 1)
            v.tensor_copy(vcol[:], ps[0][:, 0:V_COLS]).then_inc(S("setup_dve"), 1)
            dve.wait_ge(S("setup_dve"), 2)
            for k in range(0, KD, 2):
                dve.wait_ge(S("x_turned"), KD + k + 1)
                v.tensor_scalar(xnT[:, k, 0:SEQ], ps[1 + k % 4][:, :], vcol[:, V_GMIX + k:V_GMIX + k + 1], None,
                                ALU.mult).then_inc(S("xn_dve"), 1)
            dve.wait_ge(S("x_turned"), 2 * KD)
            v.tensor_tensor(xnT[:, :, SEQ:T], ps[6][:, :].rearrange("p (k t) -> p k t", k=KD),
                            vcol[:, V_GMIX:V_GMIX + KD].unsqueeze(2).to_broadcast([P, KD, NSMP]), ALU.mult).then_inc(S("xn_dve"), 1)

            def convolve(k):
                if k >= 2:
                    dve.wait_ge(S("m_uc"), k - 1)
                wc = V_WCONV + k
                cv = conv[:, k % 2, :]
                link(v.tensor_scalar(cv, uT[:, k, 0:CVW], vcol[:, wc:wc + 1], None, ALU.mult))
                for j in range(1, 4):
                    ins = v.scalar_tensor_tensor(out=cv, in0=uT[:, k, j:j + CVW], scalar=vcol[:, wc + 4 * j:wc + 4 * j + 1],
                                                 in1=cv, op0=ALU.mult, op1=ALU.add)
                    if j < 3:
                        link(ins)
                ins.then_inc(S("m_conv"), 1)

            def conv_state():
                for k in range(MH):
                    v.tensor_copy(mcg[:, k, 0:3], uT[:, k, SEQ:SEQ + 3])
                    last = v.tensor_copy(mcg[:, k, 3:27].rearrange("p (b j) -> p b j", b=NB),
                                         uT[:, k, 3 + SEQ:UPW].rearrange("p (b t) -> p b t", b=NB)[:, :, TS:TS + 3])
                last.then_inc(S("m_mcg"), 1)
                dve.wait_ge(S("m_mcg"), 1)

            starts = slice(SEQ, T, TS)

            def gate_rows():
                v.memset(restart, 1.0)
                link(v.memset(down, 0.0))
                v.memset(restart[:, starts], 0.0)
                v.memset(down[:, starts], NEG)
                link(v.tensor_scalar(frow, frow, gb[:, 1:2], None, ALU.add))
                v.scalar_tensor_tensor(out=r0, in0=frow, scalar=-1.0, in1=frow, op0=ALU.mult, op1=ALU.max).then_inc(S("gates_dve"), 1)

            def gate_maxima():
                dve.wait_ge(S("m_ln"), 2)
                link(v.scalar_tensor_tensor(out=frow, in0=frow, scalar=0.0, in1=r0, op0=ALU.min, op1=ALU.subtract))
                link(v.tensor_tensor_scan(r1, restart, frow, 0.0, ALU.mult, ALU.add))
                link(v.tensor_tensor(irow, irow, r1, ALU.subtract))
                link(v.tensor_copy(r0, irow))
                link(v.tensor_tensor(r0[:, starts], r0[:, starts], m0[:, :], ALU.max))
                link(v.tensor_tensor_scan(r2, down, r0, 0.0, ALU.add, ALU.max))
                link(v.tensor_tensor(r3, r1, r2, ALU.add))
                link(v.tensor_scalar(r1, r2, -1.0, None, ALU.mult))
                negm = r1[:, SEQ:T].rearrange("p (b t) -> p b t", b=NB)
                v.tensor_scalar(r0[:, 0:SEQ], irow[:, 0:SEQ], r1[:, SEQ - 1:SEQ], None, ALU.add)
                v.tensor_tensor(r0[:, SEQ:T].rearrange("p (b t) -> p b t", b=NB),
                                irow[:, SEQ:T].rearrange("p (b t) -> p b t", b=NB),
                                negm[:, :, TS - 1:TS].to_broadcast([MH, NB, TS]), ALU.add)
                v.tensor_tensor(r2[:, 0:NSMP].rearrange("p (b t) -> p b t", b=NB), negm,
                                m0[:, :].unsqueeze(2).to_broadcast([MH, NB, TS]), ALU.add).then_inc(S("gates_dve"), 1)

            dve.wait_ge(S("pool_step"), 3)
            for n, (_, kind, i) in enumerate(jobs):
                bank, smp = ps[n % 3], ps[3 + n % 2]
                rows = TROWS[i]
                if kind in ("q", "mu", "gates") or (kind in ("kvA", "mv") and i % 2 == 0):
                    dve.wait_ge(S("job"), n + 1)
                if kind == "q":
                    sv = smp[:, TB - NSMP:TB]
                    v.tensor_copy(qT[:, i, TA:T], smp[:, 0:TB])
                    for h in range(KVH):
                        last = v.tensor_copy(Qbd[64 * h:64 * h + 64, :, h * 32 + i * TS:h * 32 + i * TS + TS],
                                             sv[64 * h:64 * h + 64, :].rearrange("p (b t) -> p b t", b=NB))
                    last.then_inc(S("ev_dve"), 1)
                elif kind == "mu":
                    uv = uT[:, i, 3 + SEQ:UPW].rearrange("p (b t) -> p b t", b=NB)
                    v.tensor_copy(uv[:, :, 0:3],
                                  vcol[:, V_MCS + 24 * i:V_MCS + 24 * i + 24].rearrange("p (b j) -> p b j", b=NB))
                    v.tensor_copy(uT[:, i, 3 + TA:3 + SEQ], smp[:, 0:SEQ - TA])
                    v.tensor_copy(uv[:, :, 3:3 + TS],
                                  smp[:, TB - NSMP:TB].rearrange("p (b t) -> p b t", b=NB)).then_inc(S("ev_dve"), 1)
                elif kind == "gates":
                    v.tensor_scalar(irow[:, 0:TA], bank[0:MH, 0:TA], gb[:, 0:1], None, ALU.add)
                    v.tensor_scalar(irow[:, TA:T], smp[0:MH, 0:TB], gb[:, 0:1], None, ALU.add)
                    v.tensor_copy(frow[:, 0:TA], bank[32:32 + MH, 0:TA])
                    v.tensor_copy(frow[:, TA:T], smp[32:32 + MH, 0:TB]).then_inc(S("ev_dve"), 1)
                elif kind == "kvA" and i % 2 == 0:
                    v.tensor_copy(kv[0:rows, i, 0:512], bank[0:rows, :]).then_inc(S("ev_dve"), 1)
                elif kind == "mv" and i % 2 == 0:
                    v.tensor_copy(mv[0:rows, i, :, 0:P],
                                  bank[0:rows, :].rearrange("p (h e) -> p h e", h=MH)).then_inc(S("ev_dve"), 1)
                if CONV_JOB <= n < CONV_JOB + MH:
                    at = jobs.index((1, "mu", n - CONV_JOB))
                    dve.wait_ge(S("ev_act"), evac[at][0])
                    dve.wait_ge(S("ev_dve"), evac[at][1])
                    convolve(n - CONV_JOB)
                if n == CONV_JOB + MH:
                    conv_state()
                if n == GATE_JOB:
                    gate_rows()
                if n == GATE_JOB + 1:
                    gate_maxima()
            dve.sem_inc(S("c_xd"), 2)
            dve.sem_inc(S("c_kcd"), 2)

            def pack(b, slot, kvi, rows):
                src = ring[0:rows, slot, :].rearrange("p (j k h d) -> p j k h d", j=16, k=2, h=2)
                dst = packed[0:rows, kvi, :].rearrange("p (h j d) -> p h j d", h=2, j=16)
                dve.wait_ge(S("c_turned"), b * 8 + 4 * (kvi + 1))
                v.tensor_copy(dst, src[:, :, kvi, :, :].rearrange("p j h d -> p h j d")).then_inc(S("c_packed"), 1)

            def compress_dve(b, s, w, kdst, vdst, follow):
                nb = w // 2
                for kvi in range(2):
                    for f in (0, 2):
                        n = b * 8 + (4 * kvi + f)
                        dve.wait_ge(S("c_turned"), n + 9)
                        dve.wait_ge(S("c_mm"), n + 1)
                        v.tensor_copy(XT[:, f, 0:4 * w], ps[f][:, 0:4 * w]).then_inc(S("c_xd"), 1)
                    follow(kvi)
                dve.wait_ge(S("c_kc"), b * 2 + 5)
                v.tensor_copy(kdst, ps[6][:, 0:nb]).then_inc(S("c_kcd"), 1)
                dve.wait_ge(S("c_kc"), b * 2 + 6)
                v.tensor_copy(vdst, ps[7][64 * s:64 * s + nb, 0:P]).then_inc(S("c_kcd"), 1)

            def past(it, s, follow):
                compress_dve(it * 2 + s, s, P, kcT_s[:, bass.ds(it, 1), 64 * s:64 * s + 64],
                             vc_s[64 * s:64 * s + 64, bass.ds(it, 1), :], follow)

            def next_batch(it, s):
                def follow(kvi):
                    if kvi == 0:
                        dve.wait_ge(S(f"rows_in{1 - s}"), (it + 1 + s) * 16)
                    pack(it * 2 + (s + 1), 1 - s, kvi, P)
                return follow

            def own_rows(kvi):
                if kvi == 0:
                    dve.wait_ge(S("own_in"), 4 * 16)
                pack(NB, 0, kvi, 32)

            dve.wait_ge(S("job"), len(jobs))
            dve.wait_ge(S("rows_in0"), 16)
            pack(0, 0, 0, P)
            pack(0, 0, 1, P)
            with dve.Fori(0, NB // 2 - 1) as it:
                for s in range(2):
                    past(it, s, next_batch(it, s))
            past(NB // 2 - 1, 0, next_batch(NB // 2 - 1, 0))
            past(NB // 2 - 1, 1, own_rows)
            compress_dve(NB, 0, 32, kcT_p[:, :], vc_p[:, :], lambda kvi: None)

            v.memset(Qm, 0.0)
            v.memset(a4["rcol"], 0.0)
            v.memset(s2, 1.0)
            link(v.memset(hs[64:128, 4, :, :], 1.0))
            dve.wait_ge(S("m_mco"), 1)
            v.tensor_copy(mco, ps[5][0:27, :]).then_inc(S("m_mcod"), 1)

            def projected(h):
                dve.wait_ge(S("m_proj"), h + 1)
                v.tensor_copy(mqT[:, SEQ:T], ps[1][:, 0:NSMP])
                v.tensor_scalar(mkT[:, SEQ:T], ps[1][:, NSMP:2 * NSMP], KSCALE, None, ALU.mult)
                v.tensor_scalar(mk[0:NSMP, 4, :], ps[1][0:NSMP, P:2 * P], KSCALE, None, ALU.mult)
                if h:
                    dve.wait_ge(S("m_p7"), 5 * h)
                v.tensor_scalar(mk[:, 0:4, :], ps[4][:, :].rearrange("p (i d) -> p i d", i=4), KSCALE, None,
                                ALU.mult).then_inc(S("m_projd"), 1)

            projected(0)
            dve.wait_ge(S("m_cols"), 1)
            kinds = ps[3][:, 0:60].rearrange("p (k i h) -> p k i h", k=3, i=NTILE)
            v.tensor_copy(rcol[:, :, 0:4, :], kinds[:, :, 0:4, :])
            v.tensor_copy(rcol[0:NSMP, :, 4, :], kinds[0:NSMP, :, 4, :])
            v.tensor_copy(slcol, ps[3][0:NB, 60:64]).then_inc(S("m_rcol"), 1)
            dve.wait_ge(S("m_rcol"), 1)
            dve.wait_ge(S("wqk_in"), 48)
            bmask = smask[0:NSMP, TS - 1:NSMP:TS]
            for h in range(MH):
                if h:
                    projected(h)
                dve.wait_ge(S("m_spread"), h + 1)
                qd = Qm[:, 0, 0:1]
                dst = bass.AP(qd.tensor, qd.offset, [list(qd.ap[0]), [NSMP + TS, NB], [1, TS]])
                v.tensor_tensor(dst, mqT[:, SEQ:T].rearrange("p (b t) -> p b t", b=NB),
                                ps[1][:, NSMP:2 * NSMP].rearrange("p (b t) -> p b t", b=NB), ALU.mult)
                v.tensor_copy(slc, ps[1][:, 2 * NSMP:2 * NSMP + NB])
                for j in range(4):
                    v.scalar_tensor_tensor(out=E[:, EOFF[j]:EOFF[j] + P], in0=ps[3][:, j * P:(j + 1) * P],
                                           scalar=rcol[:, 0, j, h:h + 1], in1=causalT[:], op0=ALU.add, op1=ALU.add)
                v.scalar_tensor_tensor(out=E[0:NSMP, EW:EW + NSMP], in0=ps[1][0:NSMP, 0:NSMP],
                                       scalar=rcol[0:NSMP, 0, 4, h:h + 1], in1=smask[0:NSMP, :], op0=ALU.add,
                                       op1=ALU.add).then_inc(S("m_e"), 1)
                v.tensor_copy(CT[:, :, P], vcol[:, V_N + h:V_N + 32:MH])
                for x in range(2):
                    dve.wait_ge(S("m_p7"), 5 * h + x + 1)
                    v.tensor_copy(CT[:, 4 * x:4 * x + 4, 0:P],
                                  ps[7][:, :].rearrange("p (b e) -> p b e", b=4)).then_inc(S("m_p7d"), 1)
                dve.wait_ge(S("m_x"), h + 1)
                dve.wait_ge(S("m_qk"), h + 1)
                if h:
                    dve.wait_ge(S("m_sq"), h)
                v.tensor_tensor(W[:, 0:512], E[:, 0:512], ps[0][:, :], ALU.mult)
                v.tensor_tensor(W[:, 512:896], E[:, 512:896], ps[2][:, 0:384], ALU.mult)
                v.tensor_tensor(W[:, 896:EW], E[:, 896:EW], ps[4][:, 0:384], ALU.mult)
                v.tensor_tensor(W[0:NSMP, EW:EW + NSMP], E[0:NSMP, EW:EW + NSMP], ps[4][0:NSMP, 384:384 + NSMP],
                                ALU.mult).then_inc(S("m_w"), 1)
                v.tensor_tensor(vw[:, 0:4, :], mv[:, 0:4, h, 0:P],
                                rcol[:, 2, 0:4, h:h + 1].to_broadcast([P, 4, P]), ALU.mult)
                v.tensor_scalar(vw[0:NSMP, 4, :], mv[0:NSMP, 4, h, 0:P], rcol[0:NSMP, 2, 4, h:h + 1], None, ALU.mult)
                v.tensor_scalar(wlb[0:NSMP, :], bmask, 0.0, rcol[0:NSMP, 2, 4, h:h + 1], ALU.is_equal, ALU.mult)
                v.scalar_tensor_tensor(out=kbd[0:NSMP, :, :], in0=bmask.unsqueeze(2).to_broadcast([NSMP, NB, P]), scalar=0.0,
                                       in1=mk[0:NSMP, 4:5, :].to_broadcast([NSMP, NB, P]), op0=ALU.is_equal,
                                       op1=ALU.mult).then_inc(S("m_upd"), 1)
                dve.wait_ge(S("m_num"), h + 1)
                v.tensor_copy(hs[:, 0:3, h, :], ps[5][:, 0:3 * (P + 1)].rearrange("p (i e) -> p i e", i=3))
                v.tensor_copy(hs[:, 3, h, :], ps[6][:, 0:P + 1])
                v.tensor_copy(hs[0:NSMP, 4, h, :], ps[6][0:NSMP, P + 1:2 * (P + 1)]).then_inc(S("m_numd"), 1)
                for x in range(2):
                    dve.wait_ge(S("m_p7"), 5 * h + 3 + x)
                    for b in range(4):
                        last = v.scalar_tensor_tensor(out=Cst[:, 4 * x + b, :], in0=Cst[:, 4 * x + b, :],
                                                      scalar=slc[:, 4 * x + b:4 * x + b + 1], in1=ps[7][:, b * P:(b + 1) * P],
                                                      op0=ALU.mult, op1=ALU.add)
                    last.then_inc(S("m_p7d"), 1)
                dve.wait_ge(S("m_p7"), 5 * h + 5)
                v.tensor_copy(cpo[:, h, :], ps[7][:, 0:P])
                v.tensor_copy(npo[:, h * P:(h + 1) * P], ps[7][0:1, P:2 * P])
                v.scalar_tensor_tensor(out=nbh[:, h * P:(h + 1) * P], in0=nbh[:, h * P:(h + 1) * P],
                                       scalar=slcol[:, h:h + 1], in1=ps[7][0:NB, 2 * P:3 * P], op0=ALU.mult,
                                       op1=ALU.add).then_inc(S("m_p7d"), 1)
            den = hs[:, :, :, P]
            sh = lambda x: x.rearrange("p (i h) -> p i h", i=NTILE)
            dve.wait_ge(S("m_numd"), MH)
            link(v.tensor_scalar(sh(f1), den, -1.0, None, ALU.mult))
            link(v.tensor_tensor(sh(f1), sh(f1), den, ALU.max))
            link(v.tensor_tensor(sh(f1), sh(f1), rcol[:, 1, :, :], ALU.max))
            link(v.reciprocal(f1, f1))
            dve.wait_ge(S("m_sq"), MH)
            link(v.tensor_tensor(f3, f1, f1, ALU.mult))
            v.tensor_tensor(f2, f3, s2, ALU.mult).then_inc(S("heads_dve"), 1)
            dve.wait_ge(S("m_root"), 1)
            link(v.reciprocal(f3, f2))
            link(v.tensor_tensor(f1, f1, f3, ALU.mult))
            for i in range(NTILE):
                last = v.tensor_tensor(hs[:, i, :, 0:P], hs[:, i, :, 0:P],
                                       sh(f1)[:, i, :].unsqueeze(2).to_broadcast([P, MH, P]), ALU.mult)
            last.then_inc(S("heads_dve"), 1)
            for h in range(MH):
                last = v.tensor_scalar(ucT[:, h, :], ucT[:, h, :], vcol[:, V_SKIP + h:V_SKIP + h + 1], None, ALU.mult)
            link(last)
            dve.wait_ge(S("m_stored"), 6 * 16)
            for h in range(MH):
                dve.wait_ge(S("m_hT"), h + 1)
                gh = vcol[:, V_GHEAD + h:V_GHEAD + h + 1]
                v.scalar_tensor_tensor(out=xnT[:, h, 0:SEQ], in0=ps[h][:, :], scalar=gh, in1=ucT[:, h, 0:SEQ],
                                       op0=ALU.mult, op1=ALU.add)
                link(v.scalar_tensor_tensor(out=xnT[:, h, SEQ:T], in0=ps[4 + h][:, 0:NSMP], scalar=gh,
                                            in1=ucT[:, h, SEQ:T], op0=ALU.mult, op1=ALU.add))
                v.tensor_tensor(xnT[:, h, :], xnT[:, h, :], moT[:, h, :], ALU.mult).then_inc(S("m_mix"), 1)

            v.memset(Vbd, 0.0).then_inc(S("kv_dve"), 1)
            dve.wait_ge(S("k_turned"), 1)
            for w in range(2):
                v.tensor_copy(ktT[:, w, 0:SEQ], ps[2 * w])
                last = v.tensor_copy(ktT[:, w, SEQ:T], ps[2 * w + 1][:, 0:NSMP])
            last.then_inc(S("kv_dve"), 1)
            v.memset(pcd, 0.0)
            v.memset(col[:, 6:7], 1.0)
            link(v.memset(pri[:, 0, :], PRIORITY))
            dve.sem_inc(S("s_pt"), 1)
            dve.sem_inc(S("s_out"), 1)
            dve.wait_ge(S("m_cin"), (MH + NB) * 16)
            s_links = [0]

            def slink(ins, n=[0]):
                s_links[0] += 1
                ins.then_inc(S("v_link"), 1)
                dve.wait_ge(S("v_link"), base + s_links[0])

            PL = 12
            with dve.Fori(0, 2) as it:
                for x in range(2):
                    p10 = it * 20 + 10 * x
                    p1 = it * 2 + x
                    base = it * (2 * PL) + (PL * x + links[0])
                    s_links[0] = 0
                    v.tensor_copy(Qp.rearrange("p (b r) -> p b r", b=2), Qbd[:, bass.ds(it * 4 + 2 * x, 2), :])
                    v.tensor_copy(vcp.unsqueeze(1), vc_s[:, bass.ds(p1, 1), :])
                    v.tensor_copy(kcp.unsqueeze(1), kcT_s[:, bass.ds(p1, 1), :])
                    v.tensor_copy(ktn, ktT[:, :, bass.ds(it * 32 + (16 * x + SEQ), 2 * TS)])
                    v.tensor_copy(vnp, vnew[:, bass.ds(it * 4 + 2 * x, 2), :, :]).then_inc(S("s_stage"), 1)
                    dve.wait_ge(S("s_cmp"), p1 + 1)
                    v.tensor_tensor(Ss[:, PAST:PAST + TS], ps[7][:, 0:8], newmask[:], ALU.add)
                    v.tensor_tensor(Sw[:, WIN:WIN + TS], ps[7][:, 8:16], newmask[:], ALU.add)
                    slink(v.reduce_max(col[:, 0:1], ps[7][:, 16:80], AX.X))
                    v.tensor_scalar(col[:, 0:1], col[:, 0:1], -SCALE, None, ALU.mult).then_inc(S("s_cb"), 1)
                    dve.wait_ge(S("s_ce"), p1 + 1)
                    slink(v.reciprocal(col[:, 1:2], col[:, 1:2]))
                    v.tensor_scalar(pcd, pcd, col[:, 1:2], None, ALU.mult).then_inc(S("s_pn"), 1)
                    dve.wait_ge(S("s_sc"), p10 + 4)
                    slink(v.tensor_tensor(Sw[:, 0:WIN], ps[6], winmask[:], ALU.add))
                    slink(v.reduce_max(col[:, 2:3], Sw, AX.X))
                    v.tensor_scalar(col[:, 2:3], col[:, 2:3], -SCALE, None, ALU.mult).then_inc(S("s_wb"), 1)
                    dve.wait_ge(S("s_imp"), p1 + 1)
                    v.tensor_copy(PTc, ps[7][:, 2 * P:3 * P])
                    imp = ps[7][:, P:2 * P].rearrange("p (f j o) -> p j f o", f=2, o=2)
                    slink(v.tensor_reduce(pri[:, 0, 1:NSEL - 1],
                                          imp[:, 1:NSEL - 1], AX.XY, ALU.add))
                    v.memset(col[:, 10:11], 0.0)
                    slink(v.max(top[:, 0, :], pri[:, 0, :]))
                    v.memset(col[:, 11:12], 0.0)
                    slink(v.match_replace(pri[:, 1, :], top[:, 0, :], pri[:, 0, :], -1.0))
                    v.memset(col[:, 12:13], 0.0)
                    slink(v.max(top[:, 1, :], pri[:, 1, :]))
                    v.memset(col[:, 13:14], 0.0)
                    slink(v.match_replace(pri[:, 2, :], top[:, 1, :], pri[:, 1, :], -1.0))
                    v.tensor_scalar(add, pri[:, 2, :], 0.0, NEG, ALU.is_ge, ALU.mult).then_inc(S("s_pc"), 1)
                    dve.wait_ge(S("s_pc"), p1 + 1)
                    for f in range(4):
                        dve.wait_ge(S("s_sc"), p10 + (2 + 2 + 4 + f + 1))
                        out = Ss[:, f * 512:(f + 1) * 512].rearrange("p (j n o) -> p j n o", j=4, o=4)
                        last = v.tensor_tensor(out, ps[f].rearrange("p (j n o) -> p j n o", j=4, o=4),
                                               add[:, 0:NSEL].unsqueeze(1).unsqueeze(3).to_broadcast([P, 4, NSEL, 4]), ALU.add)
                    slink(last)
                    slink(v.reduce_max(col[:, 3:4], Ss, AX.X))
                    v.tensor_scalar(col[:, 3:4], col[:, 3:4], -SCALE, None, ALU.mult).then_inc(S("s_sb"), 1)
                    dve.wait_ge(S("s_wT"), p1 + 1)
                    v.tensor_copy(a5["PTw"], ps[6])
                    v.tensor_copy(PTn[:, 1, :], ps[7][0:TS, P:2 * P])
                    dve.wait_ge(S("s_sT"), p1 + 1)
                    for f in range(4):
                        v.tensor_copy(PT[:, 4 * f:4 * f + 4, :].rearrange("p j r -> p (j r)"), ps[f])
                    v.tensor_copy(PTn[:, 0, :], ps[5][0:TS, 0:P]).then_inc(S("s_pt"), 1)
                    slink(v.reciprocal(col[:, 8:10], col[:, 4:6]))
                    dve.wait_ge(S("s_pv"), p1 + 1)
                    dve.wait_ge(S("s_sto"), p1 * 16 + 16)
                    for q in range(4):
                        r, c0 = slice(32 * q, 32 * q + 32), 64 * q
                        v.tensor_tensor(orow[r, 0:2, :], banks[r, 0:2, c0:c0 + HD], col[r, 8:10].unsqueeze(2).to_broadcast([32, 2, HD]), ALU.mult)
                        last = v.tensor_copy(orow[r, 2, :], ps[2][r, HD * (q % 2):HD * (q % 2) + HD])
                    last.then_inc(S("s_out"), 1)
                    assert s_links[0] == PL
            links[0] += 4 * PL
            dve.wait_ge(S("s_pv"), 4)
            v.memset(qst, 0.0)
            dve.wait_ge(S("cmp_pe"), 1)
            dve.wait_ge(S("cmk_pool"), 2)
            pcv = Pc.rearrange("p (i h n) -> p i h n", i=4, n=16)
            pcu = Pc.rearrange("p (u n) -> p u n", n=16)
            for h in range(KVH):
                last = v.tensor_tensor(pcv[:, :, GRP * h:GRP * (h + 1), :],
                                       ps[h][:, 0:256].rearrange("p (i g n) -> p i g n", i=4, n=16),
                                       cmk.unsqueeze(2).to_broadcast([P, 4, GRP, 16]), ALU.add)
            link(last)
            link(v.tensor_reduce(cm[:, 0, :], pcu, AX.X, ALU.max))
            v.tensor_tensor(pcu, pcu, cm[:, 0, :].unsqueeze(2).to_broadcast([P, 32, 16]), ALU.subtract).then_inc(S("cmp_dve"), 1)
            dve.wait_ge(S("p_cexp"), 1)
            link(v.tensor_reduce(cm[:, 0, :], pcu, AX.X, ALU.add))
            link(v.reciprocal(cm[:, 1, :], cm[:, 0, :]))
            link(v.tensor_scalar(cm[:, 1, 0:HEADS], cm[:, 1, 0:HEADS], small[:, 4:5], None, ALU.mult))
            v.tensor_tensor(pcu, pcu, cm[:, 1, :].unsqueeze(2).to_broadcast([P, 32, 16]), ALU.mult).then_inc(S("cmp_dve"), 1)
            dve.wait_ge(S("cmp_pe"), 2)
            v.tensor_copy(b6["PcT"], ps[1]).then_inc(S("cmp_dve"), 1)
            dve.wait_ge(S("cmp_pe"), 3)
            gv = gsig[:, :, :].rearrange("p i (h w) -> p i h w", w=3)
            for i in range(4):
                last = v.tensor_tensor(oatt[:, i, :].rearrange("p (h d) -> p h d", h=HEADS),
                                       ps[2 + i].rearrange("p (h d) -> p h d", h=HEADS),
                                       gv[:, i, :, 0:1].to_broadcast([P, HEADS, HD]), ALU.mult)
            last.then_inc(S("cmp_dve"), 1)
            dve.wait_ge(S("cmp_dve"), 4)
            dve.sem_inc(S("p_ptd"), 1)
            dve.sem_inc(S("p_fin"), 2)
            g4 = gsig[:, 0:4, :].rearrange("p i (h g w) -> p i h g w", h=KVH, g=GRP)
            o4 = oatt[:, 0:4, :].rearrange("p i (h g d) -> p i h g d", h=KVH, g=GRP)
            GL = 8 * 6
            with dve.Fori(0, GRP) as g:
                done = [0]

                def glink(ins):
                    done[0] += 1
                    ins.then_inc(S("v_link"), 1)
                    dve.wait_ge(S("v_link"), g * GL + (links[0] + done[0]))

                for h in range(KVH):
                    r = slice(64 * h, 64 * h + 64)
                    v.tensor_copy(qst[r, h:h + 1, :], qT[r, bass.ds(g, 1), 0:SEQ])
                for h in range(KVH):
                    for i in range(4):
                        last = v.tensor_copy(gst[:, i, h, :].unsqueeze(1), g4[:, i, h, bass.ds(g, 1), 1:3])
                last.then_inc(S("p_stage"), 1)
                dve.wait_ge(S("p_stage"), g + 1)
                for step in range(10):
                    if step < 8:
                        u = step
                        i, h = UNITS[u]
                        both = banks[:, 2 * (u % 2):2 * (u % 2) + 2, :]
                        dve.wait_ge(S("p_sc"), g * 8 + (u + 1))
                        dg = both[:, :, i * P:(i + 1) * P]
                        glink(v.tensor_tensor(dg, dg, causal[:, :].unsqueeze(1).to_broadcast([P, 2, P]), ALU.add))
                        glink(v.tensor_reduce(cst[:, u % 2, 0, :], both[:, :, 0:(i + 1) * P], AX.X, ALU.max))
                        v.tensor_scalar(cst[:, u % 2, 1, :], cst[:, u % 2, 0, :], -SCALE, None, ALU.mult).then_inc(S("p_max"), 1)
                    if 1 <= step < 9:
                        u = step - 1
                        n = (UNITS[u][0] + 1) * P
                        dve.wait_ge(S("p_tr"), g * 8 + (u + 3))
                        dve.wait_ge(S("p_pv"), g * 8 + (u + 1))
                        v.tensor_copy(PTp[:, u % 2, 0, 0:n], ps[4][:, 0:n]).then_inc(S("p_ptd"), 1)
                        glink(v.reciprocal(cst[:, u % 2, 3, :], cst[:, u % 2, 2, :]))
                        i, h = UNITS[u]
                        glink(v.tensor_tensor(cst[:, u % 2, 3, :], cst[:, u % 2, 3, :], gst[:, i, h, :], ALU.mult))
                    if step >= 2:
                        u = step - 2
                        i, h = UNITS[u]
                        dve.wait_ge(S("p_pv"), g * 8 + (u + 3))
                        glink(v.tensor_tensor(tmp[:, u % 2, :, :], ps[6 + u % 2][:, 0:2 * HD].rearrange("p (w d) -> p w d", w=2),
                                              gfac(u % 2), ALU.mult))
                        dst = o4[:, i, h, bass.ds(g, 1), :]
                        glink(v.tensor_tensor(dst, dst, tmp[:, u % 2, 0:1, :], ALU.add))
                        v.tensor_tensor(dst, dst, tmp[:, u % 2, 1:2, :], ALU.add).then_inc(S("p_fin"), 1)
                assert done[0] == GL, done[0]
            links[0] += GRP * GL
            dve.wait_ge(S("s_sto"), (5 + 24) * 16)
            os8 = osm[0:NSMP, :, :].rearrange("p w (h d) -> p w h d", h=HEADS)
            for w, gi in ((0, 1), (1, 2), (2, 0)):
                last = v.tensor_tensor(os8[:, w], os8[:, w], gv[0:NSMP, 4, :, gi:gi + 1].to_broadcast([NSMP, HEADS, HD]), ALU.mult)
            link(last)
            link(v.tensor_tensor(osm[0:NSMP, 0, :], osm[0:NSMP, 0, :], osm[0:NSMP, 1, :], ALU.add))
            v.tensor_tensor(oatt[0:NSMP, 4, :], osm[0:NSMP, 0, :], osm[0:NSMP, 2, :], ALU.add)
            v.memset(nss, 1.0).then_inc(S("o_dve"), 1)
            dve.wait_ge(S("p_fin"), 2 + 32)
            dve.wait_ge(S("o_act"), 2)
            link(v.reciprocal(nss[:, 8:13], nss[:, 8:13]))
            for i in range(NTILE):
                rows = TROWS[i]
                last = v.tensor_scalar(oatt[0:rows, i, :], oatt[0:rows, i, :], nss[0:rows, 8 + i:9 + i], None, ALU.mult)
            last.then_inc(S("o_dve"), 1)
            for f in range(4):
                dve.wait_ge(S("o_turned"), f + 1)
                gn = vcol[:, V_GNSA + f:V_GNSA + f + 1]
                v.tensor_scalar(xnT[:, 4 + f, 0:SEQ], ps[f], gn, None, ALU.mult)
                v.tensor_scalar(xnT[:, 4 + f, SEQ:T], ps[4 + f][:, 0:NSMP], gn, None, ALU.mult).then_inc(S("o_mix"), 1)
            def split_up_dve(slot, n2):
                for w in range(2):
                    dve.wait_ge(S("u_hi"), n2 + (w + 1))
                    half = ring[:, slot, 2048 * w:2048 * (w + 1)]
                    v.tensor_tensor(ring_r[:, slot, 2048 * w:2048 * (w + 1)], half, whi[slot][:, 2048 * w:2048 * (w + 1)].bitcast(F32),
                                    ALU.subtract).then_inc(S("u_lo"), 1)

            for m in range(KD):
                if m == 6:
                    split_up_dve(0, 0)
                dve.wait_ge(S("h_mm"), m + 1)
                v.tensor_tensor(xT[:, m, 0:TA], xT[:, m, 0:TA], ps[m % 2][:, 0:TA], ALU.add)
                v.tensor_tensor(xT[:, m, TA:T], xT[:, m, TA:T], ps[2 + m % 2][:, 0:TB], ALU.add).then_inc(S("h_done"), 1)
            dve.wait_ge(S("h_done"), KD)
            dve.sem_inc(S("u_fc"), 1)
            dve.sem_inc(S("u_pad"), 2)
            norm_dve(dve, xT, V_GFFN)
            dve.wait_ge(S("xn_lo"), KD)
            v.memset(pad[:, :, :, 0:2], 0.0)
            v.memset(ssy[:], 1.0)
            dve.sem_inc(S("u_conv"), 2)
            UL = 4

            def up_dve(par, qn, split, before_conv=lambda: None):
                n = [0]

                def ulink(ins):
                    n[0] += 1
                    ins.then_inc(S("v_link"), 1)
                    dve.wait_ge(S("v_link"), qn * UL + (links[0] + n[0]))

                dve.wait_ge(S("u_ft"), qn + 1)
                v.tensor_copy(fcol[:, par, :, :], ps[6][:, 0:64].rearrange("p (w n) -> p w n", w=2)[:, :, 0:19]).then_inc(S("u_fc"), 1)
                dve.wait_ge(S("u_fc"), qn + 2)
                dve.wait_ge(S("u_conv"), qn + 1)
                for w in range(2):
                    pv = pad[:, par, w, 2 + SEQ:FPW].rearrange("p (b t) -> p b t", b=NB)
                    last = v.tensor_copy(pv[:, :, 0:2], fcol[:, par, w, 0:16].rearrange("p (b j) -> p b j", b=NB))
                last.then_inc(S("u_smp"), 1)
                dve.wait_ge(S("u_smp"), qn + 1)
                dve.wait_ge(S("u_pad"), qn + 3)
                dve.wait_ge(S("u_lT"), qn + 1)
                v.tensor_copy(l18[:, :, 0:2], pad[:, par, :, SEQ:SEQ + 2])
                for w in range(2):
                    pv = pad[:, par, w, 2 + SEQ:FPW].rearrange("p (b t) -> p b t", b=NB)
                    last = v.tensor_copy(l18[:, w, 2:18].rearrange("p (b j) -> p b j", b=NB), pv[:, :, TS:TS + 2])
                last.then_inc(S("u_l18"), 1)
                split()
                dve.wait_ge(S("u_act"), qn + 1)
                taps = [fcol[:, par, w, 16 + j:17 + j] for w in range(2) for j in range(3)]
                for w, c in ((1, cg), (0, ca)):
                    ulink(v.tensor_scalar(c, pad[:, par, w, 0:FVW], taps[3 * w], None, ALU.mult))
                    ulink(v.scalar_tensor_tensor(out=c, in0=pad[:, par, w, 1:1 + FVW], scalar=taps[3 * w + 1], in1=c,
                                                 op0=ALU.mult, op1=ALU.add))
                    v.scalar_tensor_tensor(out=c, in0=pad[:, par, w, 2:2 + FVW], scalar=taps[3 * w + 2], in1=c,
                                           op0=ALU.mult, op1=ALU.add).then_inc(S("u_cg" if w else "u_conv"), 1)
                dve.wait_ge(S("u_conv"), qn + 3)
                dve.wait_ge(S("u_silu"), qn + 1)
                v.tensor_tensor(actT[:, bass.ds(qn, 1), 0:SEQ], cg[:, 0:SEQ].unsqueeze(1), ca[:, 0:SEQ].unsqueeze(1), ALU.mult)
                v.tensor_tensor(actT[:, bass.ds(qn, 1), SEQ:T].rearrange("p k (b t) -> p (k b) t", b=NB), ffn_sample(cg),
                                ffn_sample(ca), ALU.mult).then_inc(S("u_act"), 1)
                dve.wait_ge(S("u_lT"), qn + 2)
                dve.wait_ge(S("u_fof"), qn + 1)
                v.tensor_copy(a7["fo"][0:18, :], ps[7][0:18, 0:256]).then_inc(S("u_fo"), 1)

            dve.sem_inc(S("u_lT"), 1)
            dve.sem_inc(S("u_act"), 1)
            dve.sem_inc(S("u_fo"), 1)
            with dve.Fori(0, 5) as it:
                for q in range(4):
                    if q % 2 == 0:
                        up_dve(0, it * 4 + q, lambda: split_up_dve(1 - q // 2, it * 4 + (q + 2)))
                    else:
                        up_dve(1, it * 4 + q, lambda: None)

            def split_down_dve(s, mn):
                dve.wait_ge(S("d_hi"), mn + 1)
                for k0, n, where in dhi_runs[s]:
                    last = v.tensor_tensor(dlo[s][:, k0:k0 + n, :].rearrange("p k n -> p (k n)"),
                                           draw[s][:, k0:k0 + n, :].rearrange("p k n -> p (k n)"), where.bitcast(F32),
                                           ALU.subtract)
                last.then_inc(S("d_lo"), 1)

            def act_lo(k):
                dve.wait_ge(S("a_hi"), k + 1)
                v.tensor_tensor(alo[k], actT[:, k, :], ahi[k].bitcast(F32), ALU.subtract).then_inc(S("a_lo"), 1)

            up_dve(0, 20, lambda: split_down_dve(0, 0))
            up_dve(1, 21, lambda: [act_lo(k) for k in range(12)])
            for k in range(12, NFF):
                act_lo(k)
            def down_dve(s, mn, split, turned):
                if split:
                    split_down_dve(1 - s, mn + 1)
                dve.wait_ge(S("d_mm"), mn + 1)
                dve.wait_ge(S("d_out"), mn + 1)
                x = xT[:, bass.ds(mn, 1), :]
                v.tensor_tensor(hst[:, s:s + 1, 0:UA], x[:, :, 0:UA], ps[s][:, 0:UA].unsqueeze(1), ALU.add)
                v.tensor_tensor(hst[:, s:s + 1, UA:T], x[:, :, UA:T], ps[2 + s][:, 0:UB].unsqueeze(1),
                                ALU.add).then_inc(S("d_add"), 1)
                if turned:
                    token_rows(1 - s, mn)

            def token_rows(s, mn):
                dve.wait_ge(S("d_sq"), mn + 1)
                dve.wait_ge(S("d_turned"), mn)
                g = gB[:, bass.ds((mn + (-1)) * P, P)]
                v.tensor_tensor(ytok[:, 0:4, bass.ds((mn + (-1)) * P, P)], ps[4 + s].rearrange("p (i n) -> p i n", i=4),
                                g.unsqueeze(1).to_broadcast([P, 4, P]), ALU.mult)
                v.tensor_tensor(ytok[0:NSMP, 4, bass.ds((mn + (-1)) * P, P)], ps[6 + s][0:NSMP, 0:P], g[0:NSMP, :],
                                ALU.mult).then_inc(S("d_out"), 1)

            dve.sem_inc(S("d_add"), 2)
            dve.sem_inc(S("d_out"), 2)
            down_dve(0, 0, True, False)
            dve.wait_ge(S("u_fof"), 1 + NFF)
            dve.wait_ge(S("g_in"), 16)
            with dve.Fori(0, 3) as it:
                for x in range(2):
                    down_dve((1 + x) % 2, it * 2 + (1 + x), True, True)
            down_dve(1, 7, False, True)
            token_rows(1, 8)
            dve.wait_ge(S("d_out"), KD + 2)
            v.tensor_reduce(yrt, ssy[:, :, :], AX.X, ALU.add).then_inc(S("y_sum"), 1)
            dve.wait_ge(S("y_root"), 1)
            v.reciprocal(yrt, yrt).then_inc(S("y_sum"), 1)
            dve.wait_ge(S("y_sum"), 2)
            for i in range(1, NTILE, 2):
                v.tensor_scalar(ytok[:, i, :], ytok[:, i, :], yrt[:, i:i + 1], None, ALU.mult).then_inc(S("y_dve"), 1)

        @block.sync
        def _(sp):
            for i in range(4):
                sp.dma_start(xtok[:, i, :], A["x_prompt"][0, i * P:(i + 1) * P, :]).then_inc(S("x_in"), 16)
            sp.dma_start(xtok[0:NSMP, 4, :], A["x_sample"].rearrange("b t f -> (b t) f")).then_inc(S("x_in"), 16)
            sp.dma_start(vrows[V_GMIX:V_GMIX + 8, :], A["g_mix"][0].rearrange("(k p) -> k p", p=P)).then_inc(S("vec_in"), 16)
            sp.dma_start(vrows[V_GFFN:V_GFFN + 8, :], A["g_ffn"][0].rearrange("(k p) -> k p", p=P)).then_inc(S("vec_in"), 16)
            sp.dma_start(vrows[V_GNSA:V_GNSA + 4, :], A["g_nsa"][0].rearrange("(k p) -> k p", p=P)).then_inc(S("vec_in"), 16)
            sp.dma_start(vrows[V_SKIP:V_SKIP + 4, :], A["m_skip"][0].rearrange("(k p) -> k p", p=P)).then_inc(S("vec_in"), 16)
            sp.dma_start(vrows[V_GHEAD:V_GHEAD + 4, :], A["g_mhead"][0]).then_inc(S("vec_in"), 16)
            sp.dma_start(vrows[V_BCONV:V_BCONV + 4, :], A["b_mconv"][0].rearrange("(k p) -> k p", p=P)).then_inc(S("vec_in"), 16)
            sp.dma_start(vrows[V_WCONV:V_WCONV + 16, :], A["w_mconv"][0].rearrange("j (k p) -> (j k) p", p=P)).then_inc(S("vec_in"), 16)
            sp.dma_start(vrows[V_PE:V_PE + 32, :], A["pe_cmp"][0].rearrange("k (c two) d -> (k c) (two d)", two=2)).then_inc(S("vec_in"), 16)
            sp.dma_start(vrows[V_GFIN:V_GFIN + 8, :], A["g_final"].rearrange("(k p) -> k p", p=P)).then_inc(S("vec_in"), 16)
            sp.dma_start(mcs[0:24, :], A["state_mlstm_conv"][0].rearrange("b j f -> (b j) f")).then_inc(S("vec_in"), 16)
            sp.dma_start(nrows[0:32, :], A["state_mlstm_n"][0].rearrange("b h d -> (b h) d")).then_inc(S("vec_in"), 16)
            sp.dma_start(gb[:, 0:1], A["b_ig"].rearrange("a h -> h a"), allow_slow_non_contiguous=True).then_inc(S("vec_in"), 16)
            sp.dma_start(gb[:, 1:2], A["b_fg"].rearrange("a h -> h a"), allow_slow_non_contiguous=True).then_inc(S("vec_in"), 16)
            sp.dma_start(m0[:, :], A["state_mlstm_m"][0].rearrange("b h -> h b"), allow_slow_non_contiguous=True).then_inc(S("vec_in"), 16)

            def slab(n):
                c0, w = SLABS[n]
                if n == 0:
                    dq = ring[:, 0, :].rearrange("p (k g h d) -> p k g h d", k=KD, g=GRP, h=KVH)
                    for h in range(KVH):
                        for g in range(GRP):
                            at = (h * GRP + g) * HD
                            sp.dma_start(dq[:, :, g, h, :], w_in[:, :, at:at + HD]).then_inc(S("q_in"), 16)
                    return
                dst = ring[:, n % 2, :].rearrange("p (k n) -> p k n", k=KD)[:, :, 0:w]
                sp.dma_start(dst, w_in[:, :, c0:c0 + w]).then_inc(S(f"slab_in{n % 2}"), 16)

            slab(0)
            slab(1)
            sp.wait_ge(S("filled"), 1)
            sp.dma_start(wg[:, :, 0:MH], w_in[:, :, 2840:2844]).then_inc(S("wg_in"), 16)
            sp.dma_start(wg[:, :, 32:32 + MH], w_in[:, :, 2844:2848]).then_inc(S("wg_in"), 16)
            sp.wait_ge(S("setup_dve"), 2)
            for k in range(2):
                sp.dma_start(w1c[:, k, :, :], A["w_cmp1"][0, k].rearrange("(c p) n -> p c n", p=P)).then_inc(S("w1_in"), 16)
                sp.dma_start(w2c[:, k, :], A["w_cmp2"][0, k]).then_inc(S("w1_in"), 16)
            for n in range(2, 6):
                sp.wait_ge(S("job"), slab_last[n - 2] + 1)
                slab(n)
            for w, name in enumerate(("w_mq", "w_mk")):
                sp.dma_start(wqk[:, w, :, :], A[name][0].rearrange("h d e -> d h e")).then_inc(S("wqk_in"), 16)
            sp.wait_ge(S("c_kc"), 4 + 2 * 9)
            for b in range(NB):
                sp.dma_start(vnew[:, b, :, :],
                             kv[b * TS:(b + 1) * TS, 4, 256:768].rearrange("t (w k f) -> t w k f", w=2, k=2)[:, :, 1, :])\
                    .then_inc(S("m_cin"), 16)
            sp.dma_start(nbh.rearrange("b (h d) -> b h d", h=MH), A["state_mlstm_n"][0]).then_inc(S("wqk_in"), 16)
            for h in range(MH):
                if h:
                    sp.wait_ge(S("m_cout"), 16 * h)
                sp.dma_start(Cst[:, :, :], A["state_mlstm_C"][0, :, h].rearrange("b e d -> e b d")).then_inc(S("m_cin"), 16)
            sp.wait_ge(S("m_mix"), MH)

            def window(p):
                for b2 in range(2):
                    b = 2 * p + b2
                    sp.dma_start(wkv[:, 2 * (p % 2) + b2, :],
                                 A["state_win"][0, b].rearrange("(p j) k h d -> p (j k h d)", p=P)).then_inc(S(f"win_in{p % 2}"), 16)

            window(0)
            window(1)
            sp.wait_ge(S("kv_dve"), 1)
            for hd in range(HEADS):
                sp.dma_start(Vbd[hd * 16:hd * 16 + 16, hd * HD:(hd + 1) * HD],
                             vc_p[:, (hd // GRP) * HD:(hd // GRP + 1) * HD]).then_inc(S("vbd_in"), 16)
            sp.sem_inc(S("s_sto"), 16)
            for p in range(4):
                sp.wait_ge(S("s_out"), p + 2)
                sp.dma_start(osc[:, p * P:(p + 1) * P, :].rearrange("w r d -> r w d"), orow).then_inc(S("s_sto"), 16)
                if p < 2:
                    window(p + 2)
            sp.dma_start(ring[:, 0, :].rearrange("p (k n) -> p k n", k=KD),
                         A["w_out"][0].rearrange("(k p) n -> p k n", p=P)[:, :, 0:512]).then_inc(S("slab_in0"), 16)
            sp.dma_start(ring[:, 1, :].rearrange("p (k n) -> p k n", k=KD),
                         A["w_out"][0].rearrange("(k p) n -> p k n", p=P)[:, :, 512:D]).then_inc(S("slab_in1"), 16)
            sp.wait_ge(S("s_sto"), 5 * 16)
            for b in range(NB):
                for w in range(3):
                    sp.dma_start(osm[b * TS:(b + 1) * TS, w, :].rearrange("t (h d) -> t h d", h=HEADS),
                                 osc[w, b * 64:(b + 1) * 64, :].rearrange("(h t) d -> t h d", h=HEADS)).then_inc(S("s_sto"), 16)
            w_up = A["w_up"][0].rearrange("(k p) (w n) -> p w k n", p=P, w=2)
            w_dn = A["w_down"][0].rearrange("(k p) n -> p k n", p=P)
            f_st = A["state_ffn_conv"][0].rearrange("b j (w n) -> (b j) w n", w=2)
            f_wt = A["w_fconv"][0].rearrange("j (w n) -> j w n", w=2)

            def up_slab(n):
                s = n % 2
                dst = ring[:, s, :].rearrange("p (w k n) -> p w k n", w=2, k=KD)
                for w in range(2):
                    sp.dma_start(dst[:, w], w_up[:, w, :, n * 256:(n + 1) * 256]).then_inc(S(f"slab_in{s}"), 16)
                sp.dma_start(fin[0:16, s, :, :], f_st[:, :, n * 256:(n + 1) * 256]).then_inc(S(f"slab_in{s}"), 16)
                sp.dma_start(fin[16:19, s, :, :], f_wt[:, :, n * 256:(n + 1) * 256]).then_inc(S(f"slab_in{s}"), 16)

            sp.wait_ge(S("o_dve"), 2)
            for n in range(2):
                sp.wait_ge(S("h_mm"), 4 * (n + 1))
                up_slab(n)
            for n in range(2, 11):
                sp.wait_ge(S("u_mm"), 2 * (n - 1))
                up_slab(n)
            def down_tile(m):
                sp.dma_start(draw[m % 2], w_dn[:, :, m * P:(m + 1) * P]).then_inc(S(f"dn_in{m % 2}"), 16)

            sp.wait_ge(S("u_mm"), 20)
            down_tile(0)
            sp.dma_start(gB, bass.AP(A["g_final"].tensor, A["g_final"].offset, [[0, P], [1, D]])).then_inc(S("g_in"), 16)
            sp.wait_ge(S("u_mm"), 22)
            down_tile(1)
            for m in range(2, KD):
                sp.wait_ge(S("d_mm"), m - 1)
                down_tile(m)
            for i in range(NTILE):
                sp.wait_ge(S("y_dve" if i % 2 else "y_act"), i // 2 + 1)
                dst = O["y_p"][0, i * P:(i + 1) * P, :] if i < 4 else O["y_s"].rearrange("b t f -> (b t) f")
                sp.dma_start(dst, ytok[0:TROWS[i], i, :]).then_inc(S("y_stored"), 16)
            sp.wait_ge(S("y_stored"), NTILE * 16)
            sp.wait_ge(S("stored"), outs[0])



_INS = ['x_prompt', 'x_sample', 'cache_cmp', 'cache_sel', 'state_win', 'state_mlstm_C', 'state_mlstm_n',
        'state_mlstm_m', 'state_mlstm_conv', 'state_ffn_conv', 'page_table',
        'g_mix', 'w_in', 'w_out', 'w_mconv', 'b_mconv', 'w_mq', 'w_mk', 'b_ig', 'b_fg', 'g_mhead', 'm_skip',
        'pe_cmp', 'w_cmp1', 'w_cmp2', 'g_nsa', 'g_ffn', 'w_up', 'w_fconv', 'w_down', 'g_final']
_OUTS = [('y_p', (1, 512, 1024)), ('y_s', (8, 8, 1024)),
         ('cmp_p', (1, 1, 512, 2, 2, 64)), ('cmp_s', (1, 8, 8, 2, 2, 64)),
         ('sel_p', (1, 1, 512, 2, 2, 64)), ('sel_s', (1, 8, 8, 2, 2, 64)),
         ('win_p', (1, 1, 512, 2, 2, 64)), ('win_s', (1, 8, 512, 2, 2, 64)),
         ('C_p', (1, 1, 4, 128, 128)), ('C_s', (1, 8, 4, 128, 128)),
         ('n_p', (1, 1, 4, 128)), ('n_s', (1, 8, 4, 128)),
         ('m_p', (1, 1, 4)), ('m_s', (1, 8, 4)),
         ('mconv_p', (1, 1, 3, 512)), ('mconv_s', (1, 8, 3, 512)),
         ('fconv_p', (1, 1, 2, 5632)), ('fconv_s', (1, 8, 2, 5632))]


def kernel(**inputs):
    import numpy as _np
    import concourse.bacc as _bacc
    from concourse import mybir as _mybir
    from concourse.bass_utils import run_bass_kernel_spmd as _run

    nc = _bacc.Bacc("TRN2", target_bir_lowering=False, num_devices=1)
    arrays, ins, outs = {}, {}, {}
    for name in _INS:
        a = _np.ascontiguousarray(inputs[name])
        arrays[f"in_{name}_dram"] = a
        ins[name] = nc.dram_tensor(f"in_{name}_dram", a.shape, _mybir.dt.from_np(a.dtype), kind="ExternalInput").ap()
    for name, shape in _OUTS:
        outs[name] = nc.dram_tensor(f"out_{name}_dram", shape, _mybir.dt.float32, kind="ExternalOutput").ap()
    hybrid_decoder_layer(nc, ins, outs)
    r = _run(nc, [arrays], core_ids=[0])
    return tuple(r.results[0][f"out_{name}_dram"] for name, _ in _OUTS)
```

```python
import concourse.bass as bass
from concourse import mybir
from contextlib import ExitStack

F32 = mybir.dt.float32
I32 = mybir.dt.int32
F32R = mybir.dt.float32r
ALU = mybir.AluOpType
ACT = mybir.ActivationFunctionType
AX = mybir.AxisListType


P = 128
D = 1024
KD = D // P
SEQ = 512
NB, TS = 8, 8
NSMP = NB * TS
T = SEQ + NSMP
TA, TB = 384, 192
UA, UB = 256, 320
SBUF_END = 229375
NTILE = 5
TROWS = [P] * 4 + [NSMP]
PAST, PAGE = 2048, 128
HD, KVH, GRP = 64, 2, 4
HEADS = KVH * GRP
MH = 4
DFF = 2816
NFF = DFF // P
WIN = 512
NIN = 2848
EPS = 1e-6
NEG = -1e30
SCALE = HD ** -0.5
KSCALE = P ** -0.5
NSEL = PAST // 64
PRIORITY = 1e4
ROWF = 4096
UPW = 3 + SEQ + NB * (3 + TS)
CVW = UPW - 3
FPW = 2 + SEQ + NB * (2 + TS)
FVW = FPW - 2

V_GMIX, V_GFFN, V_GNSA, V_SKIP, V_GHEAD, V_BCONV, V_WCONV, V_PE, V_GFIN = 0, 8, 16, 20, 24, 28, 32, 48, 80
V_ROWS = 88
V_MCS = 88
V_N = V_MCS + 4 * 24
V_COLS = V_N + NB * MH


def hybrid_decoder_layer(nc, A, O):
    ctx = ExitStack()
    with ctx:
        def sb(name, shape, dt=F32):
            return ctx.enter_context(nc.sbuf_tensor(name, shape, dt))

        def sb2(name, shape):
            at = (SBUF_END - nc.sbuf_bytes_remaining) // 32 * 32
            return sb(name, shape), nc.alloc_sbuf_tensor_at(name + "_r", shape, F32R, offset=at)

        made = {}

        def S(name):
            if name not in made:
                made[name] = ctx.enter_context(nc.semaphore(name))
            return made[name]

        banks = ctx.enter_context(nc.psum_tensor("banks", [P, 8, 512], F32))
        ps = [banks[:, i, :] for i in range(8)]

        def carve(region, sizes):
            at, out = 0, {}
            for name, n in sizes:
                out[name] = region[:, at:at + n]
                at += n
            assert at <= region.shape[1], (at, region.shape)
            return out

        ident = sb("ident", [P, P])
        ones = sb("ones", [P, P])
        causal = sb("causal", [P, P])
        causalT = sb("causalT", [P, P])
        smask = sb("smask", [P, NSMP])
        winmask = sb("winmask", [P, WIN])
        newmask = sb("newmask", [P, TS])
        gsum = sb("gsum", [P, P])
        selh = sb("selh", [MH, MH, P])
        small = sb("small", [P, 8])
        vcol = sb("vcol", [P, V_COLS])
        idx = sb("idx", [P, NB], I32)
        xT = sb("xT", [P, KD, T])
        xnT, xnT_r = sb2("xnT", [P, KD, T])
        ring, ring_r = sb2("ring", [P, 2, ROWF])
        RA = sb("RA", [P, 5248])
        RB, RB_r = sb2("RB", [P, 8192])
        RC, RC_r = sb2("RC", [P, 17412])
        ktT = sb("ktT", [P, 2, T])
        kcT_s = sb("kcT_s", [P, 4, P])
        vc_s = sb("vc_s", [P, 4, P])
        kcT_p = sb("kcT_p", [P, 16])
        vc_p = sb("vc_p", [16, P])
        gsig = sb("gsig", [P, NTILE, HEADS * 3])
        gb = sb("gb", [MH, 2])
        m0 = sb("m0", [MH, NB])
        hb = sb("hb", [P, 2])

        c = carve(RC, [("qT", GRP * T), ("Qbd", NB * 64), ("uT", MH * UPW + 152), ("kv", NTILE * 768),
                       ("ucT", MH * T), ("moT", MH * T), ("mv", NTILE * MH * (P + 1))])
        ring2 = RC[:, 9220:9220 + 2 * ROWF].rearrange("p (s n) -> p s n", s=2)
        qT = c["qT"].rearrange("p (g t) -> p g t", g=GRP)
        Qbd = c["Qbd"].rearrange("p (b r) -> p b r", b=NB)
        uT = c["uT"][:, 0:MH * UPW].rearrange("p (k t) -> p k t", k=MH)
        oatt = c["uT"][:, 0:NTILE * 512].rearrange("p (i f) -> p i f", i=NTILE)
        ucT = c["ucT"].rearrange("p (k t) -> p k t", k=MH)
        moT = c["moT"].rearrange("p (k t) -> p k t", k=MH)
        kv = c["kv"].rearrange("p (i f) -> p i f", i=NTILE)
        mv = c["mv"].rearrange("p (i h e) -> p i h e", i=NTILE, h=MH)

        a1 = carve(RA, [("xtok", NTILE * D)])
        xtok = a1["xtok"].rearrange("p (i f) -> p i f", i=NTILE)
        xs = RC[:, 5380:5380 + NTILE * D].rearrange("p (i f) -> p i f", i=NTILE)
        ss = sb("ss", [P, 2, NTILE])
        b1 = carve(RB, [("", 4 * T), ("vrows", P), ("mcs", MH * P), ("nrows", P),
                        ("wrow", WIN), ("mod", P), ("part", 8), ("newk", 8)])
        vrows, nrows = b1["vrows"], b1["nrows"]
        mcs = b1["mcs"]
        packed = xnT[:, :, :].rearrange("p k t -> p (k t)")[:, 0:4096].rearrange("p (k n) -> p k n", k=2)
        a3 = carve(RA, [("XT", 4 * 512), ("hid", 2 * 2 * P), ("", 1536), ("irow", T), ("frow", T)])
        XT = a3["XT"].rearrange("p (s n) -> p s n", s=4)
        hid = a3["hid"].rearrange("p (s k n) -> p s k n", s=2, k=2)
        hsum = RA[:, 2608:2608 + 2 * P].rearrange("p (k n) -> p k n", k=2)
        irow, frow = a3["irow"][0:MH, :], a3["frow"][0:MH, :]
        b3 = carve(RB, [("w1c", 2 * 16 * P), ("w2c", 2 * HD), ("wg", KD * 36)])
        w1c = b3["w1c"].rearrange("p (k c n) -> p k c n", k=2, c=16)
        w2c = b3["w2c"].rearrange("p (k n) -> p k n", k=2)
        wg = b3["wg"].rearrange("p (k n) -> p k n", k=KD)

        a4 = carve(RA, [("hs", NTILE * MH * (P + 1)), ("vw", NTILE * P), ("rcol", 64), ("s2", 20), ("f1", 20), ("f2", 20),
                        ("f3", 20), ("slc", NB), ("wlb", NB), ("mcg", MH * 27), ("cpo", MH * P)])
        hs = a4["hs"].rearrange("p (i h e) -> p i h e", i=NTILE, h=MH)
        vw = a4["vw"].rearrange("p (i e) -> p i e", i=NTILE)
        rcol = a4["rcol"][:, 0:60].rearrange("p (k i h) -> p k i h", k=3, i=NTILE)
        slcol = a4["rcol"][0:NB, 60:64]
        s2, f1, f2, f3 = a4["s2"], a4["f1"], a4["f2"], a4["f3"]
        slc, wlb = a4["slc"], a4["wlb"]
        mcg = a4["mcg"].rearrange("p (k n) -> p k n", k=MH)
        cpo = a4["cpo"].rearrange("p (h d) -> p h d", h=MH)
        EW = 1280
        b4 = carve(RB, [("E", EW + NSMP), ("W", EW + NSMP), ("mqT", T), ("mkT", T), ("mk", NTILE * P), ("Cst", NB * P),
                        ("CT", NB * (P + 1)), ("kbd", NB * P), ("Qm", NB * NSMP)])
        E, W, mqT, mkT = b4["E"], b4["W"], b4["mqT"], b4["mkT"]
        conv = RA[:, 0:2 * CVW].rearrange("p (s t) -> p s t", s=2)
        mk = b4["mk"].rearrange("p (i d) -> p i d", i=NTILE)
        Cst = b4["Cst"].rearrange("p (b d) -> p b d", b=NB)
        CT = b4["CT"].rearrange("p (b e) -> p b e", b=NB)
        kbd = b4["kbd"].rearrange("p (b d) -> p b d", b=NB)
        Qm = b4["Qm"].rearrange("p (b t) -> p b t", b=NB)
        EOFF = [0, 512, 896, 1152]
        xrows = xnT[:, :, :].rearrange("p k t -> p (k t)")
        nbh, npo, mco = xrows[0:NB, 0:512], xrows[0:1, 512:1024], xrows[0:27, 1024:1536]
        r0, r1, r2, r3 = (c["uT"][0:MH, n * T:(n + 1) * T] for n in range(4))
        restart, down = RA[0:MH, 2 * CVW:2 * CVW + T], RA[0:MH, 2 * CVW + T:2 * (CVW + T)]
        wqk = ktT[:, :, :].rearrange("p s t -> p (s t)")[:, 0:2 * MH * P].rearrange("p (w h e) -> p w h e", w=2, h=MH)

        a5 = carve(RA, [("S", PAST + TS), ("Sw", WIN + TS), ("PTw", 4 * P), ("PTn", 2 * P), ("PTc", P), ("Qp", P), ("vcp", P),
                        ("pcd", P), ("mx", 8), ("orow", 3 * HD), ("col", 16), ("pri", 3 * 40), ("top", 16), ("add", 40),
                        ("vnp", 4 * P)])
        Ss, Sw, PTc, Qp, vcp, pcd = a5["S"], a5["Sw"], a5["PTc"], a5["Qp"], a5["vcp"], a5["pcd"]
        PTw = a5["PTw"].rearrange("p (j r) -> p j r", j=4)
        PTn = a5["PTn"][0:TS, :].rearrange("p (w r) -> p w r", w=2)
        mx = a5["mx"]
        orow = a5["orow"].rearrange("p (w d) -> p w d", w=3)
        col = a5["col"]
        pri = a5["pri"].rearrange("p (s j) -> p s j", s=3)[:, :, 0:NSEL + 1]
        top = a5["top"].rearrange("p (s j) -> p s j", s=2)
        add = a5["add"][:, 0:NSEL + 1]
        vnp = a5["vnp"][0:TS, :].rearrange("p (b w d) -> p b w d", b=2, w=2)
        b5 = carve(RB, [("PT", 16 * P), ("KTb", 2 * 512), ("wkv", 4 * 4 * 256), ("kcp", P), ("ktn", 32)])
        kcp, ktn = b5["kcp"], b5["ktn"].rearrange("p (w n) -> p w n", w=2)
        PT = b5["PT"].rearrange("p (j r) -> p j r", j=16)
        KTb = b5["KTb"].rearrange("p (s n) -> p s n", s=2)
        wkv = b5["wkv"].rearrange("p (s n) -> p s n", s=4)
        vnew = xnT[0:TS, 4:8, :].rearrange("p k t -> p (k t)")[:, 0:NB * 2 * P].rearrange("p (b w d) -> p b w d", b=NB, w=2)
        osc = nc.dram_tensor("osc", (3, NB * 64, HD), F32, kind="Internal").ap()
        slots = [ring[:, 0, :], ring[:, 1, :], ring2[:, 0, :], ring2[:, 1, :]]
        b6 = carve(RB, [("qst", KVH * SEQ), ("gst", 4 * 2 * 2), ("Pb", 2 * 2 * SEQ), ("PTp", 2 * 2 * SEQ), ("cst", 16), ("tmp", 2 * P),
                        ("Pc", SEQ), ("PcT", SEQ), ("cmk", 4 * 16), ("cm", 2 * 32)])
        qst = b6["qst"].rearrange("p (h t) -> p h t", h=KVH)
        gst = b6["gst"].rearrange("p (i h w) -> p i h w", i=4, h=2)
        Pb = b6["Pb"].rearrange("p (s w n) -> p s w n", s=2, w=2)
        PTp = b6["PTp"].rearrange("p (s w n) -> p s w n", s=2, w=2)
        cst = b6["cst"].rearrange("p (s k w) -> p s k w", s=2, k=4)
        tmp = b6["tmp"].rearrange("p (s w d) -> p s w d", s=2, w=2)
        Pc, PcT, Vbd = b6["Pc"], b6["PcT"].rearrange("p (i t) -> p i t", i=4), c["uT"][:, 0:SEQ]
        cmk = b6["cmk"].rearrange("p (i n) -> p i n", i=4)
        cm = b6["cm"].rearrange("p (s n) -> p s n", s=2)
        a6 = carve(RA, [("osm", 3 * 512), ("nss", 16)])
        osm = a6["osm"].rearrange("p (w f) -> p w f", w=3)
        nss = a6["nss"]
        sqo = RA[:, 1552:1552 + NTILE * 512].rearrange("p (i f) -> p i f", i=NTILE)
        wraw = ring[:, :, :].rearrange("p s n -> p (s n)")
        wlo = ring_r[:, :, :].rearrange("p s n -> p (s n)")
        wohi = RC_r[:, 9220:9220 + 2 * ROWF]
        mhi = [RC_r[:, T * k:T * (k + 1)] for k in range(KD)]
        mlo = [RC_r[:, at:at + T] for at in (5380, 5956, 6532, 7108, 4608, 7684, 8260)] + [RB_r[:, 4096:4096 + T]]
        a7 = carve(RA, [("pad", 2 * 2 * FPW), ("ca", FVW), ("cg", FVW), ("fin", 2 * 512), ("fcol", 2 * 2 * 19), ("l18", 2 * 18),
                        ("fo", 256)])
        pad = a7["pad"].rearrange("p (s w t) -> p s w t", s=2, w=2)
        ca, cg = a7["ca"], a7["cg"]
        fin = a7["fin"][0:19, :].rearrange("p (s w n) -> p s w n", s=2, w=2)
        fcol = a7["fcol"].rearrange("p (s w n) -> p s w n", s=2, w=2)
        l18 = a7["l18"].rearrange("p (w n) -> p w n", w=2)
        fo = a7["fo"][0:18, :].rearrange("p (w n) -> p w n", w=2)
        an = carve(RA, [("sq", 2 * T), ("rms", T), ("rstd", T), ("xn", 2 * T)])
        assert 6 * T <= 2 * 2 * FPW + 2 * FVW
        sq = an["sq"].rearrange("p (s t) -> p s t", s=2)
        xn = an["xn"].rearrange("p (s t) -> p s t", s=2)
        rms, rstd = an["rms"], an["rstd"]
        actT = RC[:, 0:NFF * T].rearrange("p (k t) -> p k t", k=NFF)
        xhi = xnT_r[:, :, :]
        xlo = RC_r[:, NFF * T:(NFF + KD) * T].rearrange("p (k t) -> p k t", k=KD)
        whi = [RB_r[:, 4096 * s:4096 * (s + 1)] for s in range(2)]
        draw = [ring[:, 1 - s, 0:NFF * P].rearrange("p (k n) -> p k n", k=NFF) for s in range(2)]
        dlo = [ring_r[:, 1 - s, 0:NFF * P].rearrange("p (k n) -> p k n", k=NFF) for s in range(2)]
        dhi_runs = [[(0, 22, RB_r[:, 4096:6912])], [(0, 10, RB_r[:, 6912:8192]), (10, 5, RB_r[:, 3456:4096]),
                                                    (15, 7, ring_r[:, 0, 2816:3712])]]
        dhi = [[where[:, P * k:P * (k + 1)] for _, n, where in runs for k in range(n)] for runs in dhi_runs]
        ahi = [xhi[:, k, :] for k in range(8)] + [xlo[:, k, :] for k in range(8)] + \
              [RB_r[:, T * k:T * (k + 1)] for k in range(6)]
        alo = [RC_r[:, T * k:T * (k + 1)] for k in range(NFF)]
        assert len(ahi) == NFF and 6 * T == 3456
        hst = ring[:, 1, 2816:2816 + 2 * T].rearrange("p (s t) -> p s t", s=2)
        gB = ktT[:, :, :].rearrange("p s t -> p (s t)")[:, 0:D]
        sqs = kcT_s
        ssy = sb("ssy", [P, NTILE, KD])
        yrt = ss[:, 0, :]
        ytok = RA[:, 0:NTILE * D].rearrange("p (i f) -> p i f", i=NTILE)

        def gfac(slot):
            return cst[:, slot, 3, :].unsqueeze(2).to_broadcast([P, 2, HD])

        UNITS = [(i, h) for i in range(4) for h in range(KVH)]

        w_in = A["w_in"][0].rearrange("(k p) n -> p k n", p=P)
        SLABS = [(0, 512), (1304, 512), (512, 512), (1024, 280), (1816, 512), (2328, 512)]
        jobs = [(0, "q", i) for i in range(4)] + [(0, "gates", 0)] + [(1, "mu", i) for i in range(4)]
        jobs += [(2, "kvA", i) for i in range(5)] + [(3, "kvB", i) for i in range(5)]
        jobs += [(4, "mv", i) for i in range(5)] + [(5, "mo", i) for i in range(4)]
        slab_last = [max(n for n, j in enumerate(jobs) if j[0] == s) for s in range(6)]
        evac, na, nv = [], 0, 0
        for _, kind, i in jobs:
            if kind in ("q", "mu"):
                na, nv = na + 1, nv + 1
            elif kind in ("mo", "kvB"):
                na += 1
            elif kind == "gates":
                nv += 1
            elif i % 2:
                na += 1
            else:
                nv += 1
            evac.append((na, nv))

        CONV_JOB = jobs.index((2, "kvA", 0))
        GATE_JOB = jobs.index((3, "kvB", 0))

        pool_cmp = A["cache_cmp"][0].rearrange("n (c j) k h d -> (n c) (j k h d)", j=16)
        pool_sel = A["cache_sel"][0].rearrange("n (c j) k h d -> (n c) (j k h d)", j=16)

        outs = [0]

        def out_dma(eng, dst, src, slow=False):
            outs[0] += 16
            return eng.dma_start(dst, src, allow_slow_non_contiguous=slow).then_inc(S("stored"), 16)

        def conv_sample(k):
            cv = conv[:, k % 2, SEQ + 3:CVW]
            full = bass.AP(cv.tensor, cv.offset, [list(cv.ap[0]), [3 + TS, NB], [1, TS]])
            return full

        def ffn_sample(cv):
            at = cv[:, SEQ + 2:FVW]
            return bass.AP(at.tensor, at.offset, [list(at.ap[0]), [2 + TS, NB], [1, TS]])

        block = ctx.enter_context(nc.Block())

        @block.gpsimd
        def _(pool):
            g = nc.gpsimd
            wrow = b1["wrow"].bitcast(I32).rearrange("p (j q) -> p j q", j=4)
            mod = b1["mod"].bitcast(I32).rearrange("p (q g t) -> p q g t", q=4, g=GRP)
            src = A["page_table"]
            for b in range(NB):
                pool.dma_start(idx[:, b:b + 1], bass.AP(src.tensor, src.offset + 16 * b, [[1, 16], [0, 8], [1, 1]]),
                               allow_slow_non_contiguous=True).then_inc(S("idx_in"), 16)
            g.memset(ident[:], 0.0)
            g.memset(wg, 0.0)
            g.memset(small[:, 0:1], EPS)
            g.memset(small[:, 2:3], 0.0)
            g.memset(ss[:], 1.0)
            g.memset(small[:, 3:5], 1.0)
            g.memset(ones[:], 1.0).then_inc(S("filled"), 1)
            pool.wait_ge(S("filled"), 1)
            g.affine_select(out=ident[:], in_=ident[:], compare_op=ALU.not_equal, fill=1.0, base=0,
                            pattern=[[-1, P]], channel_multiplier=1).then_inc(S("pool_step"), 1)
            g.iota(b1["part"].bitcast(I32)[:, 0:1], [[0, 1]], base=0, channel_multiplier=1)
            g.iota(b1["newk"].bitcast(I32), [[1, TS]], base=0, channel_multiplier=0)
            g.iota(mod, [[0, 4], [0, GRP], [1, TS]], base=0, channel_multiplier=0)
            g.iota(wrow, [[1, 4], [4, P]], base=0, channel_multiplier=0).then_inc(S("pool_step"), 1)
            g.memset(uT, 0.0)
            g.memset(mv[:, :, :, P:P + 1], 1.0)
            g.memset(Qbd, 0.0).then_inc(S("pool_step"), 1)
            g.memset(causal[:], 0.0)
            g.memset(causalT[:], 0.0)
            g.memset(smask[:], 0.0)
            g.memset(gsum[:], 1.0)
            g.memset(selh[:], 1.0).then_inc(S("filled"), 1)
            pool.wait_ge(S("filled"), 2)
            g.affine_select(out=causal[:], in_=causal[:], compare_op=ALU.is_ge, fill=NEG, base=0,
                            pattern=[[-1, P]], channel_multiplier=1)
            g.affine_select(out=causalT[:], in_=causalT[:], compare_op=ALU.is_ge, fill=NEG, base=0,
                            pattern=[[1, P]], channel_multiplier=-1)
            g.affine_select(out=small[:, 4:5], in_=small[:, 4:5], compare_op=ALU.is_ge, fill=0.0, base=-31,
                            pattern=[[0, 1]], channel_multiplier=1)
            g.affine_select(out=selh[:], in_=selh[:], compare_op=ALU.is_equal, fill=0.0, base=0,
                            pattern=[[-1, MH], [0, P]], channel_multiplier=1)
            sv = smask[0:NSMP, :].rearrange("p (b t) -> p b t", b=NB)
            g.affine_select(out=sv, in_=sv, compare_op=ALU.is_ge, fill=NEG, base=0,
                            pattern=[[-TS, NB], [0, TS]], channel_multiplier=1)
            gv = gsum[:, :].rearrange("p (q r) -> p q r", q=4)
            g.affine_select(out=gv, in_=gv, compare_op=ALU.is_ge, fill=0.0, base=0,
                            pattern=[[-32, 4], [0, 32]], channel_multiplier=1).then_inc(S("filled"), 1)
            pool.wait_ge(S("filled"), 3)
            g.affine_select(out=sv, in_=sv, compare_op=ALU.is_ge, fill=NEG, base=0,
                            pattern=[[TS, NB], [1, TS]], channel_multiplier=-1)
            g.affine_select(out=gv, in_=gv, compare_op=ALU.is_ge, fill=0.0, base=31,
                            pattern=[[32, 4], [0, 32]], channel_multiplier=-1).then_inc(S("pool_step"), 1)
            kv_job = [n for n, j in enumerate(jobs) if j[1] == "kvB"][-1]
            pool.wait_ge(S("ev_act"), evac[kv_job][0])
            pool.wait_ge(S("ev_dve"), evac[kv_job][1])
            for br, (op, os) in enumerate((("cmp_p", "cmp_s"), ("sel_p", "sel_s"), ("win_p", None))):
                out_dma(pool, O[op][0, 0].rearrange("(i p) k h d -> p i (k h d)", p=P), kv[:, 0:4, br * 256:br * 256 + 256])
                if os:
                    out_dma(pool, O[os][0].rearrange("b t k h d -> (b t) (k h d)"), kv[0:NSMP, 4, br * 256:br * 256 + 256])
            for b in range(NB):
                out_dma(pool, O["win_s"][0, b, WIN - TS:WIN].rearrange("t k h d -> t (k h d)"),
                        kv[b * TS:(b + 1) * TS, 4, 512:768])
            out_dma(pool, O["win_s"][0, :, 0:WIN - TS].rearrange("b r k h d -> b (r k h d)"),
                    A["state_win"][0, :, TS:WIN].rearrange("b r k h d -> b (r k h d)"))
            pool.wait_ge(S("setup_dve"), 1)

            def gather(pool_rows, slot, col):
                g.indirect_dma_start(ring[:, slot, :], None, pool_rows,
                                     bass.IndirectOffsetOnAxis(ap=col, axis=0)).then_inc(S(f"rows_in{slot}"), 16)

            for b in range(2):
                pool.wait_ge(S("job"), slab_last[4 + b] + 1)
                gather(pool_cmp, b, idx[:, b:b + 1])
            for b in range(2, NB):
                pool.wait_ge(S("c_packed"), 2 * (b - 1))
                gather(pool_cmp, b % 2, idx[:, b:b + 1])
            pool.wait_ge(S("c_packed"), 2 * 7)
            for i in range(4):
                pool.dma_start(ring[8 * i:8 * i + 8, 0, :].rearrange("r (j n) -> r j n", j=16),
                               kv[:, i, 0:256]).then_inc(S("own_in"), 16)
            pool.wait_ge(S("c_packed"), 2 * 9)
            for b in range(2):
                g.indirect_dma_start(slots[b], None, pool_sel,
                                     bass.IndirectOffsetOnAxis(ap=idx[:, b:b + 1], axis=0)).then_inc(S(f"sel_in{b}"), 16)
            pool.wait_ge(S("m_mcod"), 1)
            pool.dma_start(O["mconv_p"][0, 0], mco[0:3, :]).then_inc(S("m_stored"), 16)
            pool.dma_start(O["mconv_s"][0].rearrange("b j f -> (b j) f"), mco[3:27, :]).then_inc(S("m_stored"), 16)
            pool.wait_ge(S("gates_dve"), 2)
            pool.dma_start(O["m_p"][0].rearrange("a h -> h a"), r3[:, SEQ - 1:SEQ],
                           allow_slow_non_contiguous=True).then_inc(S("m_stored"), 16)
            pool.dma_start(O["m_s"][0].rearrange("b h -> h b"), r3[:, SEQ + TS - 1:T:TS],
                           allow_slow_non_contiguous=True).then_inc(S("m_stored"), 16)
            for h in range(MH):
                pool.wait_ge(S("m_p7d"), 5 * h + 4)
                pool.dma_start(O["C_s"][0, :, h].rearrange("b e d -> e b d"), Cst[:, :, :]).then_inc(S("m_cout"), 16)
                pool.wait_ge(S("m_p7d"), 5 * h + 5)
                out_dma(pool, O["C_p"][0, 0, h], cpo[:, h, :])
            pool.dma_start(O["n_p"][0].rearrange("a h d -> a (h d)"), npo).then_inc(S("m_stored"), 16)
            pool.dma_start(O["n_s"][0].rearrange("b h d -> b (h d)"), nbh).then_inc(S("m_stored"), 16)
            pool.wait_ge(S("m_stored"), 6 * 16)
            pool.wait_ge(S("m_cout"), 4 * 16)
            pool.wait_ge(S("m_mix"), MH)
            for b in range(2, NB):
                if b >= 4:
                    pool.wait_ge(S("s_pv"), b // 2 - 1)
                g.indirect_dma_start(slots[b % 4], None, pool_sel,
                                     bass.IndirectOffsetOnAxis(ap=idx[:, b:b + 1], axis=0)).then_inc(S(f"sel_in{b % 4}"), 16)
            pool.wait_ge(S("s_pv"), 4)
            g.memset(cmk, 0.0).then_inc(S("p_pool"), 1)
            pool.wait_ge(S("p_pool"), 1)
            g.affine_select(out=cmk, in_=cmk, compare_op=ALU.is_ge, fill=NEG, base=-31,
                            pattern=[[P, 4], [-32, 16]], channel_multiplier=1).then_inc(S("p_pool"), 1)
            pool.wait_ge(S("s_sto"), (5 + 24) * 16)
            gv = gsig[:, :, :].rearrange("p i (h w) -> p i h w", w=3)
            os8 = osm[0:NSMP, :, :].rearrange("p w (h d) -> p w h d", h=HEADS)
            for w, gi in ((0, 1), (1, 2), (2, 0)):
                last = g.tensor_tensor(os8[:, w], os8[:, w], gv[0:NSMP, 4, :, gi:gi + 1].to_broadcast([NSMP, HEADS, HD]), ALU.mult)
            last.then_inc(S("p_pool"), 1)
            pool.wait_ge(S("p_pool"), 3)
            g.tensor_tensor(osm[0:NSMP, 0, :], osm[0:NSMP, 0, :], osm[0:NSMP, 1, :], ALU.add).then_inc(S("p_pool"), 1)
            pool.wait_ge(S("p_pool"), 4)
            g.tensor_tensor(oatt[0:NSMP, 4, :], osm[0:NSMP, 0, :], osm[0:NSMP, 2, :], ALU.add)
            g.memset(nss, 1.0).then_inc(S("p_pool"), 1)
            pool.wait_ge(S("cmp_dve"), 4)
            pool.sem_inc(S("p_added"), 2)
            o4 = oatt[:, 0:4, :].rearrange("p i (h g d) -> p i h g d", h=KVH, g=GRP)
            with pool.Fori(0, GRP) as q:
                for u, (i, h) in enumerate(UNITS):
                    pool.wait_ge(S("p_fin"), q * 8 + (u + 3))
                    dst = o4[:, i, h, bass.ds(q, 1), :]
                    g.tensor_tensor(tmp[:, u % 2, 0:1, :], tmp[:, u % 2, 0:1, :], tmp[:, u % 2, 1:2, :], ALU.add)\
                        .then_inc(S("p_pair"), 1)
                    pool.wait_ge(S("p_pair"), q * 8 + (u + 1))
                    g.tensor_tensor(dst, dst, tmp[:, u % 2, 0:1, :], ALU.add).then_inc(S("p_added"), 1)
                for n in range(2):
                    pool.wait_ge(S("wo_hi"), q * 2 + (n + 1))
                    at = q * 2048 + n * 1024
                    g.tensor_tensor(wlo[:, bass.ds(at, 1024)], wraw[:, bass.ds(at, 1024)],
                                    wohi[:, bass.ds(at, 1024)].bitcast(F32), ALU.subtract).then_inc(S("wo_lo"), 1)
            for k in range(4):
                pool.wait_ge(S("wo_hi"), 8 + k + 1)
                g.tensor_tensor(mlo[k], xnT[:, k, :], mhi[k].bitcast(F32), ALU.subtract).then_inc(S("wo_lo"), 1)
            pool.sem_inc(S("u_fof"), 1)
            for q in range(NFF):
                pool.wait_ge(S("u_fo"), q + 2)
                cols = slice(q * P, (q + 1) * P)
                pool.dma_start(O["fconv_p"][0, 0].rearrange("j (w n) -> j w n", w=2)[:, :, cols], fo[0:2]).then_inc(S("u_fos"), 16)
                pool.dma_start(O["fconv_s"][0].rearrange("b j (w n) -> (b j) w n", w=2)[:, :, cols], fo[2:18])\
                    .then_inc(S("u_fos"), 16)
                pool.wait_ge(S("u_fos"), 32 * (q + 1))
                pool.sem_inc(S("u_fof"), 1)

        def square_sum_act(act, n, ready, src):
            for k in range(KD):
                ready(act, k)
                if k >= 2:
                    act.wait_ge(S("norm_summed"), KD * (n - 2) + k - 1)
                nc.scalar.activation(sq[:, k % 2, :], src[:, k, :], ACT.Square).then_inc(S("norm_sq"), 1)
            act.wait_ge(S("norm_summed"), KD * (n - 1))
            nc.scalar.activation(rms[:, 0:TA], ps[6][:, 0:TA], ACT.Sqrt, bias=small[:, 0:1], scale=1.0 / D)
            nc.scalar.activation(rms[:, TA:T], ps[7][:, 0:TB], ACT.Sqrt, bias=small[:, 0:1],
                                 scale=1.0 / D).then_inc(S("norm_root"), 1)

        def square_sum_pe(pe, n, k):
            pe.wait_ge(S("norm_sq"), KD * (n - 2) + k + 1)
            nc.tensor.matmul(ps[6][:, 0:TA], ones[:], sq[:, k % 2, 0:TA], start=(k == 0), stop=(k == KD - 1))
            nc.tensor.matmul(ps[7][:, 0:TB], ones[:], sq[:, k % 2, TA:T], start=(k == 0),
                             stop=(k == KD - 1)).then_inc(S("norm_summed"), 1)

        def norm_dve(dve, src, gain):
            dve.wait_ge(S("norm_root"), 1)
            nc.vector.reciprocal(rstd, rms).then_inc(S("o_dve"), 1)
            dve.wait_ge(S("o_dve"), 2)
            for k in range(KD + 1):
                if k < KD:
                    if k >= 2:
                        dve.wait_ge(S("xn_lo"), k - 1)
                    nc.vector.scalar_tensor_tensor(out=xn[:, k % 2, :], in0=src[:, k, :], scalar=vcol[:, gain + k:gain + k + 1],
                                                   in1=rstd, op0=ALU.mult, op1=ALU.mult).then_inc(S("normed"), 1)
                if k:
                    dve.wait_ge(S("normed"), k)
                    dve.wait_ge(S("xn_hi"), k)
                    nc.vector.tensor_tensor(xlo[:, k - 1, :], xn[:, (k - 1) % 2, :], xhi[:, k - 1, :].bitcast(F32),
                                            ALU.subtract).then_inc(S("xn_lo"), 1)

        @block.scalar
        def _(act):
            a = nc.scalar
            act.wait_ge(S("filled"), 1)
            act.wait_ge(S("x_in"), 5 * 16)
            for i in range(NTILE):
                last = a.activation(xs[0:TROWS[i], i, :], xtok[0:TROWS[i], i, :], ACT.Square, accum_out=ss[0:TROWS[i], 0, i:i + 1])
            last.then_inc(S("x_stat"), 1)
            act.wait_ge(S("x_stat"), 1)
            a.activation(ss[:, 1, :], ss[:, 0, :], ACT.Sqrt, bias=small[:, 0:1], scale=1.0 / D).then_inc(S("x_stat"), 1)
            act.wait_ge(S("setup_dve"), 2)
            for k in range(1, KD, 2):
                act.wait_ge(S("x_turned"), KD + k + 1)
                a.activation(xnT[:, k, 0:SEQ], ps[1 + k % 4][:, :], ACT.Copy,
                             scale=vcol[:, V_GMIX + k:V_GMIX + k + 1]).then_inc(S("xn_act"), 1)
            act.wait_ge(S("pool_step"), 3)
            for n, (_, kind, i) in enumerate(jobs):
                bank, rest = ps[n % 3][:, 0:TA], ps[3 + n % 2][:, 0:TB]
                rows = TROWS[i]
                if kind in ("q", "mu", "mo") or kind == "kvB" or (kind in ("kvA", "mv") and i % 2):
                    act.wait_ge(S("job"), n + 1)
                if kind == "q":
                    a.activation(qT[:, i, 0:TA], bank, ACT.Copy).then_inc(S("ev_act"), 1)
                elif kind == "mu":
                    a.activation(uT[:, i, 3:3 + TA], bank, ACT.Copy).then_inc(S("ev_act"), 1)
                elif kind == "mo":
                    a.activation(moT[:, i, 0:TA], bank, ACT.Sigmoid)
                    a.activation(moT[:, i, TA:T], rest, ACT.Sigmoid).then_inc(S("ev_act"), 1)
                elif kind == "kvB":
                    a.activation(kv[0:rows, i, 512:768], ps[n % 3][0:rows, 0:256], ACT.Copy)
                    a.activation(gsig[0:rows, i, :], ps[n % 3][0:rows, 256:280], ACT.Sigmoid).then_inc(S("ev_act"), 1)
                elif kind == "kvA" and i % 2:
                    a.activation(kv[0:rows, i, 0:512], ps[n % 3][0:rows, :], ACT.Copy).then_inc(S("ev_act"), 1)
                elif kind == "mv" and i % 2:
                    a.activation(mv[0:rows, i, :, 0:P], ps[n % 3][0:rows, :].rearrange("p (h e) -> p h e", h=MH),
                                 ACT.Copy).then_inc(S("ev_act"), 1)
                if CONV_JOB + 1 <= n < CONV_JOB + 1 + MH:
                    k = n - CONV_JOB - 1
                    act.wait_ge(S("m_conv"), k + 1)
                    a.activation(ucT[:, k, 0:SEQ], conv[:, k % 2, 0:SEQ], ACT.Silu, bias=vcol[:, V_BCONV + k:V_BCONV + k + 1])
                    a.activation(ucT[:, k, SEQ:T].rearrange("p (b t) -> p b t", b=NB),
                                 conv_sample(k), ACT.Silu,
                                 bias=vcol[:, V_BCONV + k:V_BCONV + k + 1]).then_inc(S("m_uc"), 1)
                if n == GATE_JOB:
                    act.wait_ge(S("gates_dve"), 1)
                    a.activation(r0, r0, ACT.Exp, scale=-1.0).then_inc(S("m_ln"), 1)
                    act.wait_ge(S("m_ln"), 1)
                    a.activation(r0, r0, ACT.Ln, bias=small[0:MH, 3:4]).then_inc(S("m_ln"), 1)
                if n == GATE_JOB + 3:
                    act.wait_ge(S("gates_dve"), 2)
                    a.activation(frow, r3, ACT.Exp, scale=-1.0)
                    a.activation(r0, r0, ACT.Exp)
                    a.activation(r2[:, 0:NSMP], r2[:, 0:NSMP], ACT.Exp).then_inc(S("m_rows"), 1)
            act.sem_inc(S("c_xa"), 2)
            act.wait_ge(S("hb_made"), 1)
            a.activation(hb[:, 0:1], ps[5][:, 0:1], ACT.Copy)
            a.activation(hb[:, 1:2], ps[5][:, 1:2], ACT.Copy).then_inc(S("c_hid"), 2)
            act.wait_ge(S("c_hid"), 2)

            def compress_act(b, s, w):
                for kvi in range(2):
                    for f in (1, 3):
                        n = b * 8 + (4 * kvi + f)
                        act.wait_ge(S("c_turned"), n + 9)
                        act.wait_ge(S("c_mm"), n + 1)
                        a.activation(XT[:, f, 0:4 * w], ps[f][:, 0:4 * w], ACT.Copy).then_inc(S("c_xa"), 1)
                    act.wait_ge(S("c_mm"), b * 8 + (4 * kvi + 4 + 4))
                    act.wait_ge(S("c_kc"), b * 2 + (kvi + 1))
                    a.activation(hid[:, s, kvi, 0:w], ps[4 + kvi][:, 0:w], ACT.Silu,
                                 bias=hb[:, kvi:kvi + 1]).then_inc(S("c_hid"), 1)

            with act.Fori(0, NB // 2) as it:
                for s in range(2):
                    compress_act(it * 2 + s, s, P)
            compress_act(NB, 0, 32)

            for h in range(MH):
                act.wait_ge(S("m_proj"), h + 1)
                a.activation(mqT[:, 0:SEQ], ps[0][:, :], ACT.Copy)
                a.activation(mkT[:, 0:SEQ], ps[2][:, :], ACT.Copy, scale=KSCALE).then_inc(S("m_proja"), 1)
                act.wait_ge(S("m_e"), h + 1)
                for j in range(4):
                    dg = E[:, EOFF[j]:EOFF[j] + P]
                    a.activation(dg, dg, ACT.Exp)
                    if j < 3:
                        a.activation(E[:, EOFF[j] + P:EOFF[j + 1]], ps[3][:, (j + 1) * P:SEQ], ACT.Exp,
                                     bias=rcol[:, 0, j, h:h + 1])
                a.activation(E[0:NSMP, EW:EW + NSMP], E[0:NSMP, EW:EW + NSMP], ACT.Exp).then_inc(S("m_x"), 1)
                act.wait_ge(S("m_numd"), h + 1)
                for i in range(NTILE):
                    rows = TROWS[i]
                    last = a.activation(W[0:rows, i * P:(i + 1) * P], hs[0:rows, i, h, 0:P], ACT.Square,
                                        accum_out=s2[0:rows, 4 * i + h:4 * i + h + 1])
                last.then_inc(S("m_sq"), 1)
            act.wait_ge(S("heads_dve"), 1)
            a.activation(f2, f2, ACT.Sqrt, bias=small[:, 0:1], scale=1.0 / P).then_inc(S("m_root"), 1)

            act.sem_inc(S("s_kt"), 1)
            with act.Fori(0, 2) as it:
                for x in range(2):
                    p10 = it * 20 + 10 * x
                    p1 = it * 2 + x

                    def keys(n):
                        act.wait_ge(S("s_t"), p10 + (n + 1))
                        act.wait_ge(S("s_sc"), p10 + (n + 1))
                        a.activation(KTb[:, n % 2, :], ps[4 + n % 2], ACT.Copy).then_inc(S("s_kt"), 1)

                    keys(0)
                    keys(1)
                    act.wait_ge(S("s_cb"), p1 + 1)
                    for b2 in range(2):
                        r = slice(64 * b2, 64 * b2 + 64)
                        last = a.activation(pcd[r, r], ps[7][r, 16:80], ACT.Exp, bias=col[r, 0:1], scale=SCALE,
                                            accum_out=col[r, 1:2])
                    last.then_inc(S("s_ce"), 1)
                    for n in range(2, 7):
                        keys(n)
                    act.wait_ge(S("s_wb"), p1 + 1)
                    a.activation(Sw, Sw, ACT.Exp, bias=col[:, 2:3], scale=SCALE, accum_out=col[:, 5:6]).then_inc(S("s_we"), 1)
                    for n in range(7, 10):
                        keys(n)
                    act.wait_ge(S("s_sb"), p1 + 1)
                    for n, (c0, c1) in enumerate(((0, 1024), (1024, PAST + TS))):
                        a.activation(Ss[:, c0:c1], Ss[:, c0:c1], ACT.Exp, bias=col[:, 3:4], scale=SCALE,
                                     accum_out=col[:, 6 + n:7 + n]).then_inc(S("s_se"), 1)
            act.sem_inc(S("p_exp"), 2)
            act.sem_inc(S("p_pta"), 1)
            act.wait_ge(S("cmp_dve"), 1)
            a.activation(Pc, Pc, ACT.Exp, scale=SCALE).then_inc(S("p_cexp"), 1)

            def exp_act(g, s):
                u = s % 8
                n = (UNITS[u][0] + 1) * P
                act.wait_ge(S("p_max"), g * 8 + (s + 1))
                act.wait_ge(S("p_tr"), g * 8 + (s + 1))
                for w in range(2):
                    last = a.activation(Pb[:, u % 2, w, 0:n], ps[2 * (u % 2) + w][:, 0:n], ACT.Exp,
                                        bias=cst[:, u % 2, 1, w:w + 1], scale=SCALE, accum_out=cst[:, u % 2, 2, w:w + 1])
                last.then_inc(S("p_exp"), 1)

            def turned_act(g, s):
                u = s % 8
                n = (UNITS[u][0] + 1) * P
                act.wait_ge(S("p_tr"), g * 8 + (s + 3))
                act.wait_ge(S("p_pv"), g * 8 + (s + 1))
                a.activation(PTp[:, u % 2, :, 0:n], banks[:, 4:6, 0:n], ACT.Copy).then_inc(S("p_pta"), 1)

            def unit_act(g, s, more=True):
                if s < 9 or more:
                    turned_act(g, s - 1)
                if s < 8 or more:
                    exp_act(g, s)

            def square_out(i):
                if i == NTILE - 1:
                    act.wait_ge(S("p_pool"), 5)
                else:
                    act.wait_ge(S("p_added"), 24 + 2 * (i + 1) + 2)
                rows = TROWS[i]
                return a.activation(sqo[0:rows, i, :], oatt[0:rows, i, :], ACT.Square, accum_out=nss[0:rows, i:i + 1])

            def out_weights_act(at):
                a.activation(wohi[:, bass.ds(at, 1024)], wraw[:, bass.ds(at, 1024)], ACT.Copy).then_inc(S("wo_hi"), 1)

            exp_act(0, 0)
            unit_act(0, 1)
            act.wait_ge(S("slab_in0"), 48)
            act.wait_ge(S("slab_in1"), 64)
            with act.Fori(0, GRP - 1) as g:
                for s in range(2, 10):
                    unit_act(g, s)
                    if s % 4 == 3:
                        out_weights_act(g * 2048 + s // 4 * 1024)
            for s in range(2, 10):
                unit_act(GRP - 1, s, more=False)
                if s % 2:
                    last = square_out(max((s - 5) // 2, 0) if s > 3 else NTILE - 1)
                if s % 4 == 3:
                    out_weights_act((GRP - 1) * 2048 + s // 4 * 1024)
            last = square_out(3)
            last.then_inc(S("o_act"), 1)
            act.wait_ge(S("o_act"), 1)
            a.activation(nss[:, 8:13], nss[:, 0:5], ACT.Sqrt, bias=small[:, 0:1], scale=1.0 / 512).then_inc(S("o_act"), 1)
            for k in range(KD):
                if k >= 4:
                    act.wait_ge(S("o_turned"), 4)
                    act.wait_ge(S("o_mix"), k - 3)
                a.activation(mhi[k], xnT[:, k, :], ACT.Copy).then_inc(S("wo_hi"), 1)
            def split_up_act(slot, arrived):
                act.wait_ge(S(f"slab_in{slot}"), arrived)
                for w in range(2):
                    a.activation(whi[slot][:, 2048 * w:2048 * (w + 1)], ring[:, slot, 2048 * w:2048 * (w + 1)],
                                 ACT.Copy).then_inc(S("u_hi"), 1)

            def h_ready(act, k):
                if k == 6:
                    split_up_act(0, 48 + 64)
                act.wait_ge(S("h_done"), k + 1)

            square_sum_act(act, 2, h_ready, xT)
            for k in range(KD):
                act.wait_ge(S("normed"), k + 1)
                a.activation(xhi[:, k, :], xn[:, k % 2, :], ACT.Copy).then_inc(S("xn_hi"), 1)

            def up_act(par, qn, split):
                act.wait_ge(S("u_mm"), qn + 1)
                act.wait_ge(S("u_conv"), qn + 1)
                a.activation(pad[:, par, :, 2:2 + UA], ps[4 + par].rearrange("p (w t) -> p w t", w=2), ACT.Copy)
                for w in range(2):
                    a.activation(pad[:, par, w, 2 + UA:2 + SEQ], ps[2 * w + par][:, 0:SEQ - UA], ACT.Copy)
                    last = a.activation(pad[:, par, w, 2 + SEQ:FPW].rearrange("p (b t) -> p b t", b=NB)[:, :, 2:2 + TS],
                                        ps[2 * w + par][:, SEQ - UA:UB].rearrange("p (b t) -> p b t", b=NB), ACT.Copy)
                last.then_inc(S("u_pad"), 1)
                split()
                act.wait_ge(S("u_cg"), qn + 1)
                a.activation(cg, cg, ACT.Silu).then_inc(S("u_silu"), 1)

            with act.Fori(0, 5) as it:
                for q in range(4):
                    if q == 0:
                        up_act(0, it * 4, lambda: split_up_act(1, it * 64 + (64 + 64)))
                    elif q == 2:
                        up_act(0, it * 4 + 2, lambda: split_up_act(0, it * 64 + (48 + 128)))
                    else:
                        up_act(1, it * 4 + q, lambda: None)

            def split_down_act(s, first):
                act.wait_ge(S(f"dn_in{s}"), first)
                for k0, n, where in dhi_runs[s]:
                    last = a.activation(where, draw[s][:, k0:k0 + n, :].rearrange("p k n -> p (k n)"), ACT.Copy)
                last.then_inc(S("d_hi"), 1)

            def act_hi(k):
                act.wait_ge(S("u_act"), k + 2)
                a.activation(ahi[k], actT[:, k, :], ACT.Copy).then_inc(S("a_hi"), 1)

            up_act(0, 20, lambda: split_down_act(0, 16))
            up_act(1, 21, lambda: [act_hi(k) for k in range(12)])
            for k in range(12, NFF):
                act_hi(k)

            def down_act(s, mn, first, split, turned):
                if split:
                    split_down_act(1 - s, first)
                if turned:
                    squares(1 - s, mn)

            def squares(s, mn):
                act.wait_ge(S("d_turned"), mn)
                act.wait_ge(S("d_sq"), mn)
                for i in range(NTILE):
                    rows = TROWS[i]
                    src = ps[4 + s][:, i * P:(i + 1) * P] if i < 4 else ps[6 + s][0:rows, 0:P]
                    dst = sqs[:, i, :] if i < 4 else vc_s[0:rows, 0, :]
                    m1 = mn + (-1)
                    last = a.activation(dst, src, ACT.Square, accum_out=ssy[0:rows, i, bass.ds(m1, 1)])
                last.then_inc(S("d_sq"), 1)

            act.sem_inc(S("d_sq"), 1)
            down_act(0, 0, 16, True, False)
            with act.Fori(0, 3) as it:
                for x in range(2):
                    down_act((1 + x) % 2, it * 2 + (1 + x), it * 16 + 32, True, True)
            down_act(1, 7, 0, False, True)
            squares(1, 8)
            act.wait_ge(S("y_sum"), 1)
            a.activation(yrt, yrt, ACT.Sqrt, bias=small[:, 0:1], scale=1.0 / D).then_inc(S("y_root"), 1)
            act.wait_ge(S("y_sum"), 2)
            for i in range(0, NTILE, 2):
                rows = TROWS[i]
                a.activation(ytok[0:rows, i, :], ytok[0:rows, i, :], ACT.Copy, scale=yrt[0:rows, i:i + 1]).then_inc(S("y_act"), 1)


        @block.tensor
        def _(pe):
            t = nc.tensor
            pe.wait_ge(S("pool_step"), 1)
            pe.wait_ge(S("x_in"), 5 * 16)

            def turn_tokens(src, k, smp):
                for i in range(4):
                    t.transpose(ps[1 + k % 4][:, i * P:(i + 1) * P], src[:, i, k * P:(k + 1) * P], ident[:])
                return t.transpose(smp[:, k * NSMP:(k + 1) * NSMP], src[0:NSMP, 4, k * P:(k + 1) * P], ident[0:NSMP, 0:NSMP])

            for k in range(KD):
                if k >= 4:
                    pe.wait_ge(S("x_dve"), k - 3)
                turn_tokens(xtok, k, ps[5]).then_inc(S("x_turned"), 1)
            pe.wait_ge(S("vec_in"), 14 * 16)
            t.transpose(ps[0][:, 0:V_ROWS], vrows[0:V_ROWS, :], ident[0:V_ROWS, 0:V_ROWS])
            for k in range(MH):
                t.transpose(ps[0][:, V_MCS + 24 * k:V_MCS + 24 * k + 24], mcs[0:24, k * P:(k + 1) * P], ident[0:24, 0:24])
            t.transpose(ps[0][:, V_N:V_N + 32], nrows[0:32, :], ident[0:32, 0:32]).then_inc(S("vec_turned"), 1)
            pe.wait_ge(S("x_dve"), KD + 1)
            pe.wait_ge(S("x_scaled"), 1)
            for k in range(KD):
                if k >= 4:
                    pe.wait_ge(S("xn_act" if k % 2 else "xn_dve"), k // 2 - 1)
                turn_tokens(xs, k, ps[6]).then_inc(S("x_turned"), 1)
            pe.wait_ge(S("setup_dve"), 2)
            arrived = 0
            for n, (sl, kind, i) in enumerate(jobs):
                if n == 0:
                    pe.wait_ge(S("xn_act"), 4)
                    pe.wait_ge(S("xn_dve"), 5)
                if n >= 2 and evac[n - 2][0]:
                    pe.wait_ge(S("ev_act"), evac[n - 2][0])
                if n >= 2 and evac[n - 2][1]:
                    pe.wait_ge(S("ev_dve"), evac[n - 2][1])
                if kind == "gates":
                    pe.wait_ge(S("wg_in"), 32)
                elif n == 0:
                    pe.wait_ge(S("q_in"), 8 * 16)
                elif sl != jobs[n - 1][0]:
                    pe.wait_ge(S(f"slab_in{sl % 2}"), 16 * (sl // 2 + sl % 2))
                wt = ring[:, sl % 2, :].rearrange("p (k n) -> p k n", k=KD)
                bank, smp = ps[n % 3], ps[3 + n % 2]
                for k in range(KD):
                    on = dict(start=(k == 0), stop=(k == KD - 1))
                    if kind in ("q", "mu", "mo", "gates"):
                        if kind == "gates":
                            w = wg[:, k, :]
                        else:
                            w = wt[:, k, i * P:(i + 1) * P]
                        m = 36 if kind == "gates" else P
                        t.matmul(bank[0:m, 0:TA], w, xnT[:, k, 0:TA], **on)
                        last = t.matmul(smp[0:m, 0:TB], w, xnT[:, k, TA:T], **on)
                    else:
                        w = SLABS[sl][1]
                        last = t.matmul(bank[0:TROWS[i], 0:w], xnT[:, k, i * P:i * P + TROWS[i]], wt[:, k, 0:w], **on)
                last.then_inc(S("job"), 1)
            pe.wait_ge(S("ev_act"), evac[-1][0])
            pe.wait_ge(S("ev_dve"), evac[-1][1])
            pe.wait_ge(S("w1_in"), 4 * 16)
            pe.wait_ge(S("setup_dve"), 3)
            pe.sem_inc(S("c_turned"), 8)
            for kvi in range(2):
                last = t.matmul(ps[5][:, kvi:kvi + 1], hsum[:, kvi, :], ones[:, 0:1], start=True, stop=True)
            last.then_inc(S("hb_made"), 1)
            pe.sem_inc(S("c_mm"), 4)
            pe.sem_inc(S("c_kc"), 4)

            def turn(b, s, n, rows):
                kvi, f = n // 4, n % 4
                ct = packed[0:rows, kvi, :].rearrange("p (h j d) -> p h j d", h=2, j=16)
                if f == 0:
                    pe.wait_ge(S("c_packed"), b * 2 + (kvi + 1))
                if f % 2:
                    pe.wait_ge(S("c_xa"), b * 4 + (n // 2 + 1))
                else:
                    pe.wait_ge(S("c_xd"), b * 4 + (n // 2 + 1))
                for c2 in range(2):
                    for h in range(2):
                        j = 2 * (2 * f + c2)
                        at = (2 * c2 + h) * rows
                        last = t.transpose(ps[f][:, at:at + rows], ct[:, h, j:j + 2, :], ident[0:rows, 0:rows])
                last.then_inc(S("c_turned"), 1)

            def hidden(b, s, n, rows):
                kvi, f = n // 4, n % 4
                if f == 0:
                    pe.wait_ge(S("c_hid"), b * 2 + (kvi + 1))
                if f % 2:
                    pe.wait_ge(S("c_xa"), b * 4 + (n // 2 + 3))
                else:
                    pe.wait_ge(S("c_xd"), b * 4 + (n // 2 + 3))
                nb = rows // 2
                for c2 in range(2):
                    for half in range(2):
                        x = XT[:, f, 2 * c2 * rows:2 * (c2 + 1) * rows].rearrange("p (h n f) -> p h n f", h=2, f=2)[:, :, :, half]
                        last = t.matmul(ps[4 + kvi][:, 0:rows], w1c[:, kvi, half * 8 + 2 * f + c2, :], x,
                                        start=(f == 0 and c2 == 0 and half == 0), stop=(f == 3 and c2 == 1 and half == 1))
                last.then_inc(S("c_mm"), 1)

            def second(b, s, kvi, rows):
                pe.wait_ge(S("c_hid"), b * 2 + (kvi + 3))
                pe.wait_ge(S("c_kcd"), b * 2 + (kvi + 1))
                nb = rows // 2
                for h in range(2):
                    hv = hid[:, s, kvi, h * nb:(h + 1) * nb]
                    if kvi == 0:
                        last = t.matmul(ps[6][64 * h:64 * h + 64, 0:nb], w2c[:, 0, :], hv, start=True, stop=True)
                    else:
                        last = t.matmul(ps[7][64 * s:64 * s + nb, 64 * h:64 * h + 64], hv, w2c[:, 1, :],
                                        start=True, stop=True)
                last.then_inc(S("c_kc"), 1)

            def compress_pe(b, s, rows):
                turn(b, s, 0, rows)
                for n in range(8):
                    if n < 7:
                        turn(b, s, n + 1, rows)
                    hidden(b, s, n, rows)
                    if n == 5:
                        second(b, s, 0, rows)
                second(b, s, 1, rows)

            with pe.Fori(0, NB // 2) as it:
                for s in range(2):
                    compress_pe(it * 2 + s, s, P)
            compress_pe(NB, 0, 32)

            pe.wait_ge(S("c_xa"), 2 + 4 * 9)
            pe.wait_ge(S("c_xd"), 2 + 4 * 9)
            pe.wait_ge(S("c_hid"), 2 + 2 * 9)
            pe.wait_ge(S("c_kcd"), 2 + 2 * 9)
            pe.wait_ge(S("m_mcg"), 1)
            for k in range(MH):
                last = t.transpose(ps[5][0:27, k * P:(k + 1) * P], mcg[:, k, :], ident[:])
            last.then_inc(S("m_mco"), 1)
            pe.wait_ge(S("wqk_in"), 48)

            def project(h):
                if h:
                    pe.wait_ge(S("m_w"), h)
                    pe.wait_ge(S("m_e"), h)
                pe.wait_ge(S("m_uc"), h + 1)
                for w, b in ((0, 0), (1, 2)):
                    t.matmul(ps[b][:, :], wqk[:, w, h, :], ucT[:, h, 0:SEQ], start=True, stop=True)
                    t.matmul(ps[1][:, NSMP * w:NSMP * (w + 1)], wqk[:, w, h, :], ucT[:, h, SEQ:T], start=True, stop=True)
                for i in range(4):
                    t.matmul(ps[4][:, i * P:(i + 1) * P], ucT[:, h, i * P:(i + 1) * P], wqk[:, 1, h, :], start=True, stop=True)
                t.matmul(ps[1][0:NSMP, P:2 * P], ucT[:, h, SEQ:T], wqk[:, 1, h, :], start=True,
                         stop=True).then_inc(S("m_proj"), 1)

            def turn_states(h, x):
                pe.wait_ge(S("m_cin"), 16 * (NB + h + 1))
                if 5 * h + x:
                    pe.wait_ge(S("m_p7d"), 5 * h + x)
                for b in range(4):
                    last = t.transpose(ps[7][:, b * P:(b + 1) * P], Cst[:, 4 * x + b, :], ident[:])
                last.then_inc(S("m_p7"), 1)

            project(0)
            pe.wait_ge(S("m_rows"), 1)
            for kind, row in enumerate((irow, frow, r0)):
                for i in range(NTILE):
                    at = (kind * NTILE + i) * MH
                    t.transpose(ps[3][0:TROWS[i], at:at + MH], row[:, i * P:i * P + TROWS[i]], ident[0:MH, 0:MH])
            t.transpose(ps[3][0:NB, 60:64], r2[:, TS - 1:NSMP:TS], ident[0:MH, 0:MH]).then_inc(S("m_cols"), 1)
            pe.wait_ge(S("m_rcol"), 1)
            for h in range(MH):
                if h:
                    project(h)
                pe.wait_ge(S("m_projd"), h + 1)
                pe.wait_ge(S("m_rows"), 1)
                if h:
                    pe.wait_ge(S("m_p7d"), 5 * h - 1)
                t.matmul(ps[3][:, :], selh[:, h, :], r1[:, 0:SEQ], start=True, stop=True)
                t.matmul(ps[1][0:NSMP, 0:NSMP], selh[:, h, 0:NSMP], r1[:, SEQ:T], start=True, stop=True)
                t.matmul(ps[1][:, NSMP:2 * NSMP], selh[:, h, :], r2[:, 0:NSMP], start=True, stop=True)
                t.matmul(ps[1][:, 2 * NSMP:2 * NSMP + NB], selh[:, h, :], r2[:, TS - 1:NSMP:TS], start=True,
                         stop=True).then_inc(S("m_spread"), 1)
                turn_states(h, 0)
                pe.wait_ge(S("m_proja"), h + 1)
                for j in range(4):
                    out = (ps[0][:, :], ps[2][:, 0:384], ps[4][:, 0:256], ps[4][:, 256:384])[j]
                    t.matmul(out, mkT[:, j * P:(j + 1) * P], mqT[:, j * P:SEQ], start=True, stop=True)
                t.matmul(ps[4][0:NSMP, 384:384 + NSMP], mkT[:, SEQ:T], mqT[:, SEQ:T], start=True,
                         stop=True).then_inc(S("m_qk"), 1)
                turn_states(h, 1)
                pe.wait_ge(S("m_w"), h + 1)
                pe.wait_ge(S("m_p7d"), 5 * h + 2)
                if h:
                    pe.wait_ge(S("m_numd"), h)
                else:
                    pe.wait_ge(S("m_mcod"), 1)
                for i in range(4):
                    out = ps[5][:, i * (P + 1):(i + 1) * (P + 1)] if i < 3 else ps[6][:, 0:P + 1]
                    for j in range(i + 1):
                        at = EOFF[j] + (i - j) * P
                        t.matmul(out, W[:, at:at + P], mv[:, j, h, :], start=(j == 0), stop=(j == i))
                out = ps[6][0:NSMP, P + 1:2 * (P + 1)]
                t.matmul(out, W[0:NSMP, EW:EW + NSMP], mv[0:NSMP, 4, h, :], start=True, stop=False)
                for b in range(NB):
                    last = t.matmul(out, Qm[:, b, :], CT[:, b, :], start=False, stop=(b == NB - 1))
                last.then_inc(S("m_num"), 1)
                pe.wait_ge(S("m_upd"), h + 1)
                for x in range(2):
                    if x:
                        pe.wait_ge(S("m_x"), h + 1)
                    t.matmul(ps[3 if x else 7][:, :], vw[0:NSMP, 4, :],
                             kbd[0:NSMP, 4 * x:4 * x + 4, :].rearrange("p b d -> p (b d)"),
                             start=True, stop=True).then_inc(S("m_p7"), 1)
                pe.wait_ge(S("m_p7d"), 5 * h + 3)
                for i in range(4):
                    t.matmul(ps[7][:, 0:P], vw[:, i, :], mk[:, i, :], start=(i == 0), stop=(i == 3))
                for i in range(4):
                    t.matmul(ps[7][0:1, P:2 * P], rcol[:, 2, i, h:h + 1], mk[:, i, :], start=(i == 0), stop=(i == 3))
                t.matmul(ps[7][0:NB, 2 * P:3 * P], wlb[0:NSMP, :], mk[0:NSMP, 4, :], start=True,
                         stop=True).then_inc(S("m_p7"), 1)
            pe.wait_ge(S("heads_dve"), 2)
            pe.wait_ge(S("m_w"), MH)
            pe.wait_ge(S("m_p7d"), 5 * MH)
            for h in range(MH):
                for i in range(4):
                    t.transpose(ps[h][:, i * P:(i + 1) * P], hs[:, i, h, 0:P], ident[:])
                t.transpose(ps[4 + h][:, 0:NSMP], hs[0:NSMP, 4, h, 0:P],
                            ident[0:NSMP, 0:NSMP]).then_inc(S("m_hT"), 1)

            pe.wait_ge(S("m_mix"), MH)
            for w in range(2):
                for i in range(NTILE):
                    rows = TROWS[i]
                    out = ps[2 * w][:, i * P:(i + 1) * P] if i < 4 else ps[2 * w + 1][:, 0:NSMP]
                    last = t.transpose(out, kv[0:rows, i, 256 + 256 * w:384 + 256 * w], ident[0:rows, 0:rows])
            last.then_inc(S("k_turned"), 1)
            pe.wait_ge(S("kv_dve"), 2)
            pe.sem_inc(S("s_sc"), 2)
            with pe.Fori(0, 2) as it:
                for x in range(2):
                    p10 = it * 20 + 10 * x
                    p1 = it * 2 + x
                    kvs = [slots[2 * x], slots[2 * x + 1]]
                    kvw = [wkv[:, 2 * x, :], wkv[:, 2 * x + 1, :]]
                    def turn_keys(n):
                        if n == 0:
                            pe.wait_ge(S(f"win_in{x}"), it * 32 + 32)
                        if n == 2:
                            pe.wait_ge(S(f"sel_in{2 * x}"), it * 16 + 16)
                        if n == 6:
                            pe.wait_ge(S(f"sel_in{2 * x + 1}"), it * 16 + 16)
                        if n < 2:
                            src, j0 = kvw[n], 0
                            pe.wait_ge(S("s_kt"), p10 + (n + 0 if n else 1))
                        else:
                            src, j0 = kvs[(n - 2) // 4], 4 * ((n - 2) % 4)
                            pe.wait_ge(S("s_kt"), p10 + n)
                        for j in range(4):
                            last = t.transpose(ps[4 + n % 2][:, j * P:(j + 1) * P],
                                               src[:, (j0 + j) * 256:(j0 + j) * 256 + P], ident[:])
                        last.then_inc(S("s_t"), 1)

                    def score(n):
                        pe.wait_ge(S("s_kt"), p10 + (n + 2))
                        b2 = n if n < 2 else (n - 2) // 4
                        bank = ps[6] if n < 2 else ps[(n - 2) % 4]
                        t.matmul(bank[64 * b2:64 * b2 + 64, :], Qp[:, 64 * b2:64 * b2 + 64], KTb[:, n % 2, :], start=True,
                                 stop=True).then_inc(S("s_sc"), 1)

                    turn_keys(0)
                    turn_keys(1)
                    pe.wait_ge(S("s_stage"), p1 + 1)
                    for b2 in range(2):
                        r = slice(64 * b2, 64 * b2 + 64)
                        q = Qp[:, 64 * b2:64 * b2 + 64]
                        for w in range(2):
                            t.matmul(ps[7][r, 8 * w:8 * w + 8], q, ktn[:, w, b2 * TS:(b2 + 1) * TS], start=True, stop=True)
                        last = t.matmul(ps[7][r, 16:80], q, kcp[:, 64 * b2:64 * b2 + 64], start=True, stop=True)
                    last.then_inc(S("s_cmp"), 1)
                    pe.wait_ge(S("s_out"), p1 + 1)
                    for n in range(10):
                        if 1 <= n < 9:
                            turn_keys(n + 1)
                        score(n)
                        if n == 4:
                            pe.wait_ge(S("s_pn"), p1 + 1)
                            t.matmul(ps[7][:, P:2 * P], gsum[:], pcd, start=True, stop=True)
                            t.transpose(ps[7][:, 2 * P:3 * P], pcd, ident[:]).then_inc(S("s_imp"), 1)
                    pe.wait_ge(S("s_we"), p1 + 1)
                    for j in range(4):
                        t.transpose(ps[6][:, j * P:(j + 1) * P], Sw[:, j * P:(j + 1) * P], ident[:])
                    pe.wait_ge(S("s_pc"), p1 + 1)
                    t.transpose(ps[7][0:TS, P:2 * P], Sw[:, WIN:WIN + TS], ident[:]).then_inc(S("s_wT"), 1)
                    pe.wait_ge(S("s_ptw"), p1 + 1)
                    both = (ring if x == 0 else ring2)[:, :, :].rearrange("p s (j k n) -> p s j k n", j=16, k=2)
                    wins = wkv[:, 2 * x:2 * x + 2, :].rearrange("p s (j k n) -> p s j k n", j=4, k=2)
                    for j in range(4):
                        t.matmul(ps[6][:, 0:256], PTw[:, j, :], wins[:, :, j, 1, :], start=(j == 0), stop=False)
                    t.matmul(ps[6][:, 0:256], PTn[:, 1, :], vnp[:, :, 1, :], start=False, stop=True)
                    t.matmul(ps[6][:, 256:384], PTc, vcp, start=True, stop=True)
                    p2 = it * 4 + 2 * x
                    p4 = it * 8 + 4 * x
                    for f in range(4):
                        if f % 2 == 0:
                            pe.wait_ge(S("s_se"), p2 + (f // 2 + 1))
                        for j in range(4 * f, 4 * f + 4):
                            last = t.transpose(ps[f][:, (j % 4) * P:(j % 4 + 1) * P], Ss[:, j * P:(j + 1) * P], ident[:])
                        if f == 3:
                            last = t.transpose(ps[5][0:TS, 0:P], Ss[:, PAST:PAST + TS], ident[:])
                        last.then_inc(S("s_sT"), 1)
                    for j in range(16):
                        if j % 4 == 0:
                            pe.wait_ge(S("s_pt"), p4 + (j // 4 + 1))
                        t.matmul(ps[0][:, 0:256], PT[:, j, :], both[:, :, j, 1, :], start=(j == 0), stop=False)
                    t.matmul(ps[0][:, 0:256], PTn[:, 0, :], vnp[:, :, 0, :], start=False, stop=True).then_inc(S("s_pv"), 1)
            pe.wait_ge(S("s_out"), 5)
            for i in range(4):
                for hd in range(HEADS):
                    h, g = hd // GRP, hd % GRP
                    at = (i * GRP + g) * 16
                    last = t.matmul(ps[h][:, at:at + 16], qT[64 * h:64 * h + 64, g, i * P:(i + 1) * P], kcT_p[64 * h:64 * h + 64, :],
                                    start=True, stop=True)
            last.then_inc(S("cmp_pe"), 1)
            pe.wait_ge(S("cmp_dve"), 2)
            for i in range(4):
                last = t.transpose(ps[1][:, i * P:(i + 1) * P], Pc[:, i * P:(i + 1) * P], ident[:])
            last.then_inc(S("cmp_pe"), 1)
            pe.wait_ge(S("cmp_dve"), 3)
            pe.wait_ge(S("vbd_in"), HEADS * 16)
            for i in range(4):
                last = t.matmul(ps[2 + i], PcT[:, i, :], Vbd, start=True, stop=True)
            last.then_inc(S("cmp_pe"), 1)
            pe.wait_ge(S("cmp_dve"), 4)
            pe.sem_inc(S("p_tr"), 2)
            pe.sem_inc(S("p_pv"), 2)

            def score_unit(g, s):
                i, h = UNITS[s % 8]
                if s % 8 == 0:
                    pe.wait_ge(S("p_stage"), g + (s // 8 + 1))
                pe.wait_ge(S("p_exp"), g * 8 + (s + 1))
                for w in range(2):
                    last = t.matmul(ps[2 * (s % 2) + w][:, 0:(i + 1) * P], qst[:, h, i * P:(i + 1) * P],
                                    ktT[:, w, 0:(i + 1) * P], start=True, stop=True)
                last.then_inc(S("p_sc"), 1)

            def turn_unit(g, s):
                i = UNITS[s % 8][0]
                pe.wait_ge(S("p_exp"), g * 8 + (s + 3))
                pe.wait_ge(S("p_pta"), g * 8 + (s + 1))
                for w in range(2):
                    for j in range(i + 1):
                        last = t.transpose(ps[4 + w][:, j * P:(j + 1) * P], Pb[:, s % 2, w, j * P:(j + 1) * P], ident[:])
                last.then_inc(S("p_tr"), 1)

            def value_unit(g, s):
                i, h = UNITS[s % 8]
                pe.wait_ge(S("p_pta"), g * 8 + (s + 2))
                pe.wait_ge(S("p_fin"), g * 8 + (s + 1))
                for w in range(2):
                    for j in range(i + 1):
                        at = 384 + 256 * w + 64 * h
                        last = t.matmul(ps[6 + s % 2][:, w * HD:(w + 1) * HD], PTp[:, s % 2, w, j * P:(j + 1) * P],
                                        kv[:, j, at:at + HD], start=(j == 0), stop=(j == i))
                last.then_inc(S("p_pv"), 1)

            def unit_pe(g, s, more=True):
                if s < 8:
                    score_unit(g, s)
                if s < 9 or more:
                    turn_unit(g, s - 1)
                if s >= 2:
                    value_unit(g, s - 2)
                if s >= 8 and more:
                    score_unit(g, s)

            score_unit(0, 0)
            unit_pe(0, 1)
            with pe.Fori(0, GRP - 1) as g:
                for s in range(2, 10):
                    unit_pe(g, s)
            for s in range(2, 10):
                unit_pe(GRP - 1, s, more=False)
            pe.wait_ge(S("o_dve"), 1)
            for f in range(4):
                for i in range(4):
                    t.transpose(ps[f][:, i * P:(i + 1) * P], oatt[:, i, f * P:(f + 1) * P], ident[:])
                t.transpose(ps[4 + f][:, 0:NSMP], oatt[0:NSMP, 4, f * P:(f + 1) * P],
                            ident[0:NSMP, 0:NSMP]).then_inc(S("o_turned"), 1)
            pe.wait_ge(S("o_mix"), 4)
            for m in range(KD):
                if m % 4 == 0:
                    pe.wait_ge(S("wo_lo"), m + 4)
                if m >= 2:
                    pe.wait_ge(S("h_done"), m - 1)
                hi = wohi.rearrange("p (s k n) -> p s k n", s=2, k=KD)
                lo = wlo.rearrange("p (s k n) -> p s k n", s=2, k=KD)
                for k in range(KD):
                    if m == 0:
                        pe.wait_ge(S("wo_lo" if k < 4 else "o_mix"), 8 + k + 1 if k < 4 else k + 1)
                    c = slice((m % 4) * P, (m % 4 + 1) * P)
                    for n, (w, x) in enumerate(((hi, mhi[k]), (hi, mlo[k]), (lo, mhi[k]))):
                        on = dict(start=(k == 0 and n == 0), stop=(k == KD - 1 and n == 2))
                        t.matmul(ps[m % 2][:, 0:UA], w[:, m // 4, k, c], x[:, 0:UA], **on)
                        last = t.matmul(ps[2 + m % 2][:, 0:UB], w[:, m // 4, k, c], x[:, UA:T], **on)
                last.then_inc(S("h_mm"), 1)
                if m:
                    square_sum_pe(pe, 2, m - 1)
            square_sum_pe(pe, 2, KD - 1)
            pe.wait_ge(S("h_done"), KD)

            def up_pe(slot, sub, par, qn, norm=False):
                hi = whi[slot].rearrange("p (w k n) -> p w k n", w=2, k=KD)
                lo = ring_r[:, slot, :].rearrange("p (w k n) -> p w k n", w=2, k=KD)
                pe.wait_ge(S("u_pad"), qn + 1)
                pe.wait_ge(S("u_fc"), qn + 1)
                for w in range(2):
                    for k in range(KD):
                        if norm and w == 0:
                            pe.wait_ge(S("xn_lo"), k + 1)
                        if w == 0 and k == 1:
                            for z in range(2):
                                last = t.transpose(ps[6][:, 32 * z:32 * z + 19], fin[:, slot, z, sub * P:(sub + 1) * P],
                                                   ident[0:19, 0:19])
                            last.then_inc(S("u_ft"), 1)
                        c = slice(sub * P, (sub + 1) * P)
                        for n, (wk, x) in enumerate(((hi, xhi), (hi, xlo), (lo, xhi))):
                            on = dict(start=(k == 0 and n == 0), stop=(k == KD - 1 and n == 2))
                            first = dict(start=(k == 0 and n == 0 and w == 0), stop=(k == KD - 1 and n == 2))
                            t.matmul(ps[4 + par][:, w * UA:(w + 1) * UA], wk[:, w, k, c], x[:, k, 0:UA],
                                     skip_group_check=True, **first)
                            last = t.matmul(ps[2 * w + par][:, 0:UB], wk[:, w, k, c], x[:, k, UA:T], **on)
                last.then_inc(S("u_mm"), 1)

            def last_cols(qn):
                pe.wait_ge(S("u_l18"), qn + 1)
                pe.wait_ge(S("u_fo"), qn + 1)
                for w in range(2):
                    last = t.transpose(ps[7][0:18, w * P:(w + 1) * P], l18[:, w, :], ident[:])
                last.then_inc(S("u_lT"), 1)

            pe.wait_ge(S("u_lo"), 2)
            up_pe(0, 0, 0, 0, norm=True)
            with pe.Fori(0, 5) as it:
                for q in range(4):
                    if q % 2:
                        pe.wait_ge(S("u_lo"), it * 4 + (q + 3))
                    up_pe((q + 1) // 2 % 2, (q + 1) % 2, (q + 1) % 2, it * 4 + (q + 1))
                    last_cols(it * 4 + q)
            up_pe(0, 1, 1, 21)
            last_cols(20)
            def down_pe(s, mn, first=False):
                pe.wait_ge(S("d_lo"), mn + 1)
                if not first:
                    pe.wait_ge(S("d_add"), mn + 1)
                for k in range(NFF):
                    if first:
                        pe.wait_ge(S("a_lo"), k + 1)
                        if k == 8:
                            last_cols(21)
                    for n, (w, x) in enumerate(((dhi[s][k], ahi[k]), (dhi[s][k], alo[k]), (dlo[s][:, k, :], ahi[k]))):
                        on = dict(start=(k == 0 and n == 0), stop=(k == NFF - 1 and n == 2))
                        t.matmul(ps[s][:, 0:UA], w, x[:, 0:UA], **on)
                        last = t.matmul(ps[2 + s][:, 0:UB], w, x[:, UA:T], **on)
                last.then_inc(S("d_mm"), 1)

            def turn_y(s, mn):
                pe.wait_ge(S("d_add"), mn + 2)
                pe.wait_ge(S("d_out"), mn)
                for i in range(4):
                    t.transpose(ps[4 + s][:, i * P:(i + 1) * P], hst[:, s, i * P:(i + 1) * P], ident[:])
                t.transpose(ps[6 + s][0:NSMP, 0:P], hst[:, s, SEQ:T], ident[:]).then_inc(S("d_turned"), 1)

            pe.wait_ge(S("u_pad"), NFF + 2)
            down_pe(0, 0, first=True)
            pe.wait_ge(S("u_fo"), NFF + 1)
            with pe.Fori(0, 3) as it:
                for x in range(2):
                    down_pe((1 + x) % 2, it * 2 + (1 + x))
                    turn_y(x % 2, it * 2 + (1 + x))
            down_pe(1, 7)
            turn_y(0, 7)
            turn_y(1, 8)

        @block.vector
        def _(dve):
            v = nc.vector
            links = [0]

            def link(ins):
                links[0] += 1
                ins.then_inc(S("v_link"), 1)
                dve.wait_ge(S("v_link"), links[0])

            dve.wait_ge(S("pool_step"), 2)
            dve.wait_ge(S("idx_in"), NB * 16)
            part = b1["part"].bitcast(I32)
            link(v.tensor_scalar(part[:, 1:2], part[:, 0:1], 7, None, ALU.bitwise_and))
            link(v.tensor_copy(small[:, 1:2], part[:, 1:2]))
            v.tensor_scalar(idx[:], idx[:], 8.0, small[:, 1:2], ALU.mult, ALU.add).then_inc(S("setup_dve"), 1)
            v.tensor_scalar(winmask[:], b1["wrow"].bitcast(I32), small[:, 1:2], NEG, ALU.is_le, ALU.mult)
            v.tensor_scalar(newmask[:], b1["newk"].bitcast(I32), small[:, 1:2], NEG, ALU.is_gt, ALU.mult)
            for k in range(KD):
                dve.wait_ge(S("x_turned"), k + 1)
                v.tensor_copy(xT[:, k, 0:SEQ], ps[1 + k % 4][:, :]).then_inc(S("x_dve"), 1)
            v.tensor_copy(xT[:, :, SEQ:T], ps[5][:, :].rearrange("p (k t) -> p k t", k=KD)).then_inc(S("x_dve"), 1)
            dve.wait_ge(S("x_stat"), 2)
            link(v.reciprocal(ss[:, 1, :], ss[:, 1, :]))
            for i in range(NTILE):
                rows = TROWS[i]
                last = v.tensor_scalar(xs[0:rows, i, :], xtok[0:rows, i, :], ss[0:rows, 1, i:i + 1], None, ALU.mult)
            last.then_inc(S("x_scaled"), 1)
            dve.wait_ge(S("pool_step"), 4)
            v.scalar_tensor_tensor(out=gsum[:], in0=b1["mod"].bitcast(I32), scalar=small[:, 1:2], in1=gsum[:],
                                   op0=ALU.is_equal, op1=ALU.mult)
            dve.wait_ge(S("vec_turned"), 1)
            v.tensor_copy(vcol[:], ps[0][:, 0:V_COLS]).then_inc(S("setup_dve"), 1)
            dve.wait_ge(S("setup_dve"), 2)
            for k in range(0, KD, 2):
                dve.wait_ge(S("x_turned"), KD + k + 1)
                v.tensor_scalar(xnT[:, k, 0:SEQ], ps[1 + k % 4][:, :], vcol[:, V_GMIX + k:V_GMIX + k + 1], None,
                                ALU.mult).then_inc(S("xn_dve"), 1)
            dve.wait_ge(S("x_turned"), 2 * KD)
            v.tensor_tensor(xnT[:, :, SEQ:T], ps[6][:, :].rearrange("p (k t) -> p k t", k=KD),
                            vcol[:, V_GMIX:V_GMIX + KD].unsqueeze(2).to_broadcast([P, KD, NSMP]), ALU.mult).then_inc(S("xn_dve"), 1)

            def convolve(k):
                if k >= 2:
                    dve.wait_ge(S("m_uc"), k - 1)
                wc = V_WCONV + k
                cv = conv[:, k % 2, :]
                link(v.tensor_scalar(cv, uT[:, k, 0:CVW], vcol[:, wc:wc + 1], None, ALU.mult))
                for j in range(1, 4):
                    ins = v.scalar_tensor_tensor(out=cv, in0=uT[:, k, j:j + CVW], scalar=vcol[:, wc + 4 * j:wc + 4 * j + 1],
                                                 in1=cv, op0=ALU.mult, op1=ALU.add)
                    if j < 3:
                        link(ins)
                ins.then_inc(S("m_conv"), 1)

            def conv_state():
                for k in range(MH):
                    v.tensor_copy(mcg[:, k, 0:3], uT[:, k, SEQ:SEQ + 3])
                    last = v.tensor_copy(mcg[:, k, 3:27].rearrange("p (b j) -> p b j", b=NB),
                                         uT[:, k, 3 + SEQ:UPW].rearrange("p (b t) -> p b t", b=NB)[:, :, TS:TS + 3])
                last.then_inc(S("m_mcg"), 1)
                dve.wait_ge(S("m_mcg"), 1)

            starts = slice(SEQ, T, TS)

            def gate_rows():
                v.memset(restart, 1.0)
                link(v.memset(down, 0.0))
                v.memset(restart[:, starts], 0.0)
                v.memset(down[:, starts], NEG)
                link(v.tensor_scalar(frow, frow, gb[:, 1:2], None, ALU.add))
                v.scalar_tensor_tensor(out=r0, in0=frow, scalar=-1.0, in1=frow, op0=ALU.mult, op1=ALU.max).then_inc(S("gates_dve"), 1)

            def gate_maxima():
                dve.wait_ge(S("m_ln"), 2)
                link(v.scalar_tensor_tensor(out=frow, in0=frow, scalar=0.0, in1=r0, op0=ALU.min, op1=ALU.subtract))
                link(v.tensor_tensor_scan(r1, restart, frow, 0.0, ALU.mult, ALU.add))
                link(v.tensor_tensor(irow, irow, r1, ALU.subtract))
                link(v.tensor_copy(r0, irow))
                link(v.tensor_tensor(r0[:, starts], r0[:, starts], m0[:, :], ALU.max))
                link(v.tensor_tensor_scan(r2, down, r0, 0.0, ALU.add, ALU.max))
                link(v.tensor_tensor(r3, r1, r2, ALU.add))
                link(v.tensor_scalar(r1, r2, -1.0, None, ALU.mult))
                negm = r1[:, SEQ:T].rearrange("p (b t) -> p b t", b=NB)
                v.tensor_scalar(r0[:, 0:SEQ], irow[:, 0:SEQ], r1[:, SEQ - 1:SEQ], None, ALU.add)
                v.tensor_tensor(r0[:, SEQ:T].rearrange("p (b t) -> p b t", b=NB),
                                irow[:, SEQ:T].rearrange("p (b t) -> p b t", b=NB),
                                negm[:, :, TS - 1:TS].to_broadcast([MH, NB, TS]), ALU.add)
                v.tensor_tensor(r2[:, 0:NSMP].rearrange("p (b t) -> p b t", b=NB), negm,
                                m0[:, :].unsqueeze(2).to_broadcast([MH, NB, TS]), ALU.add).then_inc(S("gates_dve"), 1)

            dve.wait_ge(S("pool_step"), 3)
            for n, (_, kind, i) in enumerate(jobs):
                bank, smp = ps[n % 3], ps[3 + n % 2]
                rows = TROWS[i]
                if kind in ("q", "mu", "gates") or (kind in ("kvA", "mv") and i % 2 == 0):
                    dve.wait_ge(S("job"), n + 1)
                if kind == "q":
                    sv = smp[:, TB - NSMP:TB]
                    v.tensor_copy(qT[:, i, TA:T], smp[:, 0:TB])
                    for h in range(KVH):
                        last = v.tensor_copy(Qbd[64 * h:64 * h + 64, :, h * 32 + i * TS:h * 32 + i * TS + TS],
                                             sv[64 * h:64 * h + 64, :].rearrange("p (b t) -> p b t", b=NB))
                    last.then_inc(S("ev_dve"), 1)
                elif kind == "mu":
                    uv = uT[:, i, 3 + SEQ:UPW].rearrange("p (b t) -> p b t", b=NB)
                    v.tensor_copy(uv[:, :, 0:3],
                                  vcol[:, V_MCS + 24 * i:V_MCS + 24 * i + 24].rearrange("p (b j) -> p b j", b=NB))
                    v.tensor_copy(uT[:, i, 3 + TA:3 + SEQ], smp[:, 0:SEQ - TA])
                    v.tensor_copy(uv[:, :, 3:3 + TS],
                                  smp[:, TB - NSMP:TB].rearrange("p (b t) -> p b t", b=NB)).then_inc(S("ev_dve"), 1)
                elif kind == "gates":
                    v.tensor_scalar(irow[:, 0:TA], bank[0:MH, 0:TA], gb[:, 0:1], None, ALU.add)
                    v.tensor_scalar(irow[:, TA:T], smp[0:MH, 0:TB], gb[:, 0:1], None, ALU.add)
                    v.tensor_copy(frow[:, 0:TA], bank[32:32 + MH, 0:TA])
                    v.tensor_copy(frow[:, TA:T], smp[32:32 + MH, 0:TB]).then_inc(S("ev_dve"), 1)
                elif kind == "kvA" and i % 2 == 0:
                    v.tensor_copy(kv[0:rows, i, 0:512], bank[0:rows, :]).then_inc(S("ev_dve"), 1)
                elif kind == "mv" and i % 2 == 0:
                    v.tensor_copy(mv[0:rows, i, :, 0:P],
                                  bank[0:rows, :].rearrange("p (h e) -> p h e", h=MH)).then_inc(S("ev_dve"), 1)
                if CONV_JOB <= n < CONV_JOB + MH:
                    at = jobs.index((1, "mu", n - CONV_JOB))
                    dve.wait_ge(S("ev_act"), evac[at][0])
                    dve.wait_ge(S("ev_dve"), evac[at][1])
                    convolve(n - CONV_JOB)
                if n == CONV_JOB + MH:
                    conv_state()
                if n == GATE_JOB:
                    gate_rows()
                if n == GATE_JOB + 1:
                    gate_maxima()
            dve.wait_ge(S("w1_in"), 4 * 16)
            for cc in range(16):
                for kvi in range(2):
                    pe_col = vcol[:, V_PE + 16 * kvi + cc:V_PE + 16 * kvi + cc + 1]
                    if cc == 0:
                        last = v.tensor_scalar(hsum[:, kvi, :], w1c[:, kvi, cc, :], pe_col, None, ALU.mult)
                    else:
                        last = v.scalar_tensor_tensor(out=hsum[:, kvi, :], in0=w1c[:, kvi, cc, :], scalar=pe_col,
                                                      in1=hsum[:, kvi, :], op0=ALU.mult, op1=ALU.add)
                if cc < 15:
                    link(last)
            last.then_inc(S("setup_dve"), 1)
            dve.sem_inc(S("c_xd"), 2)
            dve.sem_inc(S("c_kcd"), 2)

            def pack(b, slot, kvi, rows):
                src = ring[0:rows, slot, :].rearrange("p (j k h d) -> p j k h d", j=16, k=2, h=2)
                dst = packed[0:rows, kvi, :].rearrange("p (h j d) -> p h j d", h=2, j=16)
                dve.wait_ge(S("c_turned"), b * 8 + 4 * (kvi + 1))
                v.tensor_copy(dst, src[:, :, kvi, :, :].rearrange("p j h d -> p h j d")).then_inc(S("c_packed"), 1)

            def compress_dve(b, s, w, kdst, vdst, follow):
                nb = w // 2
                for kvi in range(2):
                    for f in (0, 2):
                        n = b * 8 + (4 * kvi + f)
                        dve.wait_ge(S("c_turned"), n + 9)
                        dve.wait_ge(S("c_mm"), n + 1)
                        v.tensor_copy(XT[:, f, 0:4 * w], ps[f][:, 0:4 * w]).then_inc(S("c_xd"), 1)
                    follow(kvi)
                dve.wait_ge(S("c_kc"), b * 2 + 5)
                v.tensor_copy(kdst, ps[6][:, 0:nb]).then_inc(S("c_kcd"), 1)
                dve.wait_ge(S("c_kc"), b * 2 + 6)
                v.tensor_copy(vdst, ps[7][64 * s:64 * s + nb, 0:P]).then_inc(S("c_kcd"), 1)

            def past(it, s, follow):
                compress_dve(it * 2 + s, s, P, kcT_s[:, bass.ds(it, 1), 64 * s:64 * s + 64],
                             vc_s[64 * s:64 * s + 64, bass.ds(it, 1), :], follow)

            def next_batch(it, s):
                def follow(kvi):
                    if kvi == 0:
                        dve.wait_ge(S(f"rows_in{1 - s}"), (it + 1 + s) * 16)
                    pack(it * 2 + (s + 1), 1 - s, kvi, P)
                return follow

            def own_rows(kvi):
                if kvi == 0:
                    dve.wait_ge(S("own_in"), 4 * 16)
                pack(NB, 0, kvi, 32)

            dve.wait_ge(S("job"), len(jobs))
            dve.wait_ge(S("rows_in0"), 16)
            pack(0, 0, 0, P)
            pack(0, 0, 1, P)
            with dve.Fori(0, NB // 2 - 1) as it:
                for s in range(2):
                    past(it, s, next_batch(it, s))
            past(NB // 2 - 1, 0, next_batch(NB // 2 - 1, 0))
            past(NB // 2 - 1, 1, own_rows)
            compress_dve(NB, 0, 32, kcT_p[:, :], vc_p[:, :], lambda kvi: None)

            v.memset(Qm, 0.0)
            v.memset(a4["rcol"], 0.0)
            v.memset(s2, 1.0)
            link(v.memset(hs[64:128, 4, :, :], 1.0))
            dve.wait_ge(S("m_mco"), 1)
            v.tensor_copy(mco, ps[5][0:27, :]).then_inc(S("m_mcod"), 1)

            def projected(h):
                dve.wait_ge(S("m_proj"), h + 1)
                v.tensor_copy(mqT[:, SEQ:T], ps[1][:, 0:NSMP])
                v.tensor_scalar(mkT[:, SEQ:T], ps[1][:, NSMP:2 * NSMP], KSCALE, None, ALU.mult)
                v.tensor_scalar(mk[0:NSMP, 4, :], ps[1][0:NSMP, P:2 * P], KSCALE, None, ALU.mult)
                if h:
                    dve.wait_ge(S("m_p7"), 5 * h)
                v.tensor_scalar(mk[:, 0:4, :], ps[4][:, :].rearrange("p (i d) -> p i d", i=4), KSCALE, None,
                                ALU.mult).then_inc(S("m_projd"), 1)

            projected(0)
            dve.wait_ge(S("m_cols"), 1)
            kinds = ps[3][:, 0:60].rearrange("p (k i h) -> p k i h", k=3, i=NTILE)
            v.tensor_copy(rcol[:, :, 0:4, :], kinds[:, :, 0:4, :])
            v.tensor_copy(rcol[0:NSMP, :, 4, :], kinds[0:NSMP, :, 4, :])
            v.tensor_copy(slcol, ps[3][0:NB, 60:64]).then_inc(S("m_rcol"), 1)
            dve.wait_ge(S("m_rcol"), 1)
            dve.wait_ge(S("wqk_in"), 48)
            bmask = smask[0:NSMP, TS - 1:NSMP:TS]
            for h in range(MH):
                if h:
                    projected(h)
                dve.wait_ge(S("m_spread"), h + 1)
                qd = Qm[:, 0, 0:1]
                dst = bass.AP(qd.tensor, qd.offset, [list(qd.ap[0]), [NSMP + TS, NB], [1, TS]])
                v.tensor_tensor(dst, mqT[:, SEQ:T].rearrange("p (b t) -> p b t", b=NB),
                                ps[1][:, NSMP:2 * NSMP].rearrange("p (b t) -> p b t", b=NB), ALU.mult)
                v.tensor_copy(slc, ps[1][:, 2 * NSMP:2 * NSMP + NB])
                for j in range(4):
                    v.scalar_tensor_tensor(out=E[:, EOFF[j]:EOFF[j] + P], in0=ps[3][:, j * P:(j + 1) * P],
                                           scalar=rcol[:, 0, j, h:h + 1], in1=causalT[:], op0=ALU.add, op1=ALU.add)
                v.scalar_tensor_tensor(out=E[0:NSMP, EW:EW + NSMP], in0=ps[1][0:NSMP, 0:NSMP],
                                       scalar=rcol[0:NSMP, 0, 4, h:h + 1], in1=smask[0:NSMP, :], op0=ALU.add,
                                       op1=ALU.add).then_inc(S("m_e"), 1)
                v.tensor_copy(CT[:, :, P], vcol[:, V_N + h:V_N + 32:MH])
                for x in range(2):
                    dve.wait_ge(S("m_p7"), 5 * h + x + 1)
                    v.tensor_copy(CT[:, 4 * x:4 * x + 4, 0:P],
                                  ps[7][:, :].rearrange("p (b e) -> p b e", b=4)).then_inc(S("m_p7d"), 1)
                dve.wait_ge(S("m_x"), h + 1)
                dve.wait_ge(S("m_qk"), h + 1)
                if h:
                    dve.wait_ge(S("m_sq"), h)
                v.tensor_tensor(W[:, 0:512], E[:, 0:512], ps[0][:, :], ALU.mult)
                v.tensor_tensor(W[:, 512:896], E[:, 512:896], ps[2][:, 0:384], ALU.mult)
                v.tensor_tensor(W[:, 896:EW], E[:, 896:EW], ps[4][:, 0:384], ALU.mult)
                v.tensor_tensor(W[0:NSMP, EW:EW + NSMP], E[0:NSMP, EW:EW + NSMP], ps[4][0:NSMP, 384:384 + NSMP],
                                ALU.mult).then_inc(S("m_w"), 1)
                v.tensor_tensor(vw[:, 0:4, :], mv[:, 0:4, h, 0:P],
                                rcol[:, 2, 0:4, h:h + 1].to_broadcast([P, 4, P]), ALU.mult)
                v.tensor_scalar(vw[0:NSMP, 4, :], mv[0:NSMP, 4, h, 0:P], rcol[0:NSMP, 2, 4, h:h + 1], None, ALU.mult)
                v.tensor_scalar(wlb[0:NSMP, :], bmask, 0.0, rcol[0:NSMP, 2, 4, h:h + 1], ALU.is_equal, ALU.mult)
                v.scalar_tensor_tensor(out=kbd[0:NSMP, :, :], in0=bmask.unsqueeze(2).to_broadcast([NSMP, NB, P]), scalar=0.0,
                                       in1=mk[0:NSMP, 4:5, :].to_broadcast([NSMP, NB, P]), op0=ALU.is_equal,
                                       op1=ALU.mult).then_inc(S("m_upd"), 1)
                dve.wait_ge(S("m_num"), h + 1)
                v.tensor_copy(hs[:, 0:3, h, :], ps[5][:, 0:3 * (P + 1)].rearrange("p (i e) -> p i e", i=3))
                v.tensor_copy(hs[:, 3, h, :], ps[6][:, 0:P + 1])
                v.tensor_copy(hs[0:NSMP, 4, h, :], ps[6][0:NSMP, P + 1:2 * (P + 1)]).then_inc(S("m_numd"), 1)
                for x in range(2):
                    dve.wait_ge(S("m_p7"), 5 * h + 3 + x)
                    for b in range(4):
                        last = v.scalar_tensor_tensor(out=Cst[:, 4 * x + b, :], in0=Cst[:, 4 * x + b, :],
                                                      scalar=slc[:, 4 * x + b:4 * x + b + 1], in1=ps[3 if x else 7][:, b * P:(b + 1) * P],
                                                      op0=ALU.mult, op1=ALU.add)
                    last.then_inc(S("m_p7d"), 1)
                dve.wait_ge(S("m_p7"), 5 * h + 5)
                v.tensor_copy(cpo[:, h, :], ps[7][:, 0:P])
                v.tensor_copy(npo[:, h * P:(h + 1) * P], ps[7][0:1, P:2 * P])
                v.scalar_tensor_tensor(out=nbh[:, h * P:(h + 1) * P], in0=nbh[:, h * P:(h + 1) * P],
                                       scalar=slcol[:, h:h + 1], in1=ps[7][0:NB, 2 * P:3 * P], op0=ALU.mult,
                                       op1=ALU.add).then_inc(S("m_p7d"), 1)
            den = hs[:, :, :, P]
            sh = lambda x: x.rearrange("p (i h) -> p i h", i=NTILE)
            dve.wait_ge(S("m_numd"), MH)
            link(v.tensor_scalar(sh(f1), den, -1.0, None, ALU.mult))
            link(v.tensor_tensor(sh(f1), sh(f1), den, ALU.max))
            link(v.tensor_tensor(sh(f1), sh(f1), rcol[:, 1, :, :], ALU.max))
            link(v.reciprocal(f1, f1))
            dve.wait_ge(S("m_sq"), MH)
            link(v.tensor_tensor(f3, f1, f1, ALU.mult))
            v.tensor_tensor(f2, f3, s2, ALU.mult).then_inc(S("heads_dve"), 1)
            dve.wait_ge(S("m_root"), 1)
            link(v.reciprocal(f3, f2))
            link(v.tensor_tensor(f1, f1, f3, ALU.mult))
            for i in range(NTILE):
                last = v.tensor_tensor(hs[:, i, :, 0:P], hs[:, i, :, 0:P],
                                       sh(f1)[:, i, :].unsqueeze(2).to_broadcast([P, MH, P]), ALU.mult)
            last.then_inc(S("heads_dve"), 1)
            for h in range(MH):
                last = v.tensor_scalar(ucT[:, h, :], ucT[:, h, :], vcol[:, V_SKIP + h:V_SKIP + h + 1], None, ALU.mult)
            link(last)
            dve.wait_ge(S("m_stored"), 6 * 16)
            for h in range(MH):
                dve.wait_ge(S("m_hT"), h + 1)
                gh = vcol[:, V_GHEAD + h:V_GHEAD + h + 1]
                v.scalar_tensor_tensor(out=xnT[:, h, 0:SEQ], in0=ps[h][:, :], scalar=gh, in1=ucT[:, h, 0:SEQ],
                                       op0=ALU.mult, op1=ALU.add)
                link(v.scalar_tensor_tensor(out=xnT[:, h, SEQ:T], in0=ps[4 + h][:, 0:NSMP], scalar=gh,
                                            in1=ucT[:, h, SEQ:T], op0=ALU.mult, op1=ALU.add))
                v.tensor_tensor(xnT[:, h, :], xnT[:, h, :], moT[:, h, :], ALU.mult).then_inc(S("m_mix"), 1)

            v.memset(Vbd, 0.0).then_inc(S("kv_dve"), 1)
            dve.wait_ge(S("k_turned"), 1)
            for w in range(2):
                v.tensor_copy(ktT[:, w, 0:SEQ], ps[2 * w])
                last = v.tensor_copy(ktT[:, w, SEQ:T], ps[2 * w + 1][:, 0:NSMP])
            last.then_inc(S("kv_dve"), 1)
            v.memset(pcd, 0.0)
            link(v.memset(pri[:, 0, :], PRIORITY))
            dve.sem_inc(S("s_out"), 1)
            dve.wait_ge(S("m_cin"), (MH + NB) * 16)
            s_links = [0]

            def slink(ins):
                s_links[0] += 1
                ins.then_inc(S("v_link"), 1)
                dve.wait_ge(S("v_link"), base + s_links[0])

            PL = 17
            with dve.Fori(0, 2) as it:
                for x in range(2):
                    p10 = it * 20 + 10 * x
                    p1 = it * 2 + x
                    base = it * (2 * PL) + (PL * x + links[0])
                    s_links[0] = 0
                    v.tensor_copy(Qp.rearrange("p (b r) -> p b r", b=2), Qbd[:, bass.ds(it * 4 + 2 * x, 2), :])
                    v.tensor_copy(vcp.unsqueeze(1), vc_s[:, bass.ds(p1, 1), :])
                    v.tensor_copy(kcp.unsqueeze(1), kcT_s[:, bass.ds(p1, 1), :])
                    v.tensor_copy(ktn, ktT[:, :, bass.ds(it * 32 + (16 * x + SEQ), 2 * TS)])
                    v.tensor_copy(vnp, vnew[:, bass.ds(it * 4 + 2 * x, 2), :, :]).then_inc(S("s_stage"), 1)
                    dve.wait_ge(S("s_cmp"), p1 + 1)
                    v.tensor_tensor(Ss[:, PAST:PAST + TS], ps[7][:, 0:8], newmask[:], ALU.add)
                    v.tensor_tensor(Sw[:, WIN:WIN + TS], ps[7][:, 8:16], newmask[:], ALU.add)
                    slink(v.reduce_max(col[:, 0:1], ps[7][:, 16:80], AX.X))
                    v.tensor_scalar(col[:, 0:1], col[:, 0:1], -SCALE, None, ALU.mult).then_inc(S("s_cb"), 1)
                    dve.wait_ge(S("s_ce"), p1 + 1)
                    slink(v.reciprocal(col[:, 1:2], col[:, 1:2]))
                    v.tensor_scalar(pcd, pcd, col[:, 1:2], None, ALU.mult).then_inc(S("s_pn"), 1)
                    dve.wait_ge(S("s_sc"), p10 + 4)
                    slink(v.tensor_tensor(Sw[:, 0:WIN], ps[6], winmask[:], ALU.add))
                    slink(v.reduce_max(col[:, 2:3], Sw, AX.X))
                    v.tensor_scalar(col[:, 2:3], col[:, 2:3], -SCALE, None, ALU.mult).then_inc(S("s_wb"), 1)
                    dve.wait_ge(S("s_imp"), p1 + 1)
                    v.tensor_copy(PTc, ps[7][:, 2 * P:3 * P])
                    imp = ps[7][:, P:2 * P].rearrange("p (f j o) -> p j f o", f=2, o=2)
                    slink(v.tensor_reduce(pri[:, 0, 1:NSEL - 1],
                                          imp[:, 1:NSEL - 1], AX.XY, ALU.add))
                    v.memset(col[:, 10:11], 0.0)
                    slink(v.max(top[:, 0, :], pri[:, 0, :]))
                    v.memset(col[:, 11:12], 0.0)
                    slink(v.match_replace(pri[:, 1, :], top[:, 0, :], pri[:, 0, :], -1.0))
                    v.memset(col[:, 12:13], 0.0)
                    slink(v.max(top[:, 1, :], pri[:, 1, :]))
                    v.memset(col[:, 13:14], 0.0)
                    slink(v.match_replace(pri[:, 2, :], top[:, 1, :], pri[:, 1, :], -1.0))
                    v.tensor_scalar(add, pri[:, 2, :], 0.0, NEG, ALU.is_ge, ALU.mult).then_inc(S("s_pc"), 1)
                    dve.wait_ge(S("s_pc"), p1 + 1)
                    for f in range(4):
                        dve.wait_ge(S("s_sc"), p10 + (2 + 2 + 4 + f + 1))
                        out = Ss[:, f * 512:(f + 1) * 512].rearrange("p (j n o) -> p j n o", j=4, o=4)
                        slink(v.tensor_tensor(out, ps[f].rearrange("p (j n o) -> p j n o", j=4, o=4),
                                              add[:, 0:NSEL].unsqueeze(1).unsqueeze(3).to_broadcast([P, 4, NSEL, 4]), ALU.add))
                        end = (f + 1) * 512 if f < 3 else PAST + TS
                        last = v.reduce_max(mx[:, f:f + 1], Ss[:, f * 512:end], AX.X)
                    slink(last)
                    slink(v.reduce_max(col[:, 3:4], mx[:, 0:4], AX.X))
                    v.tensor_scalar(col[:, 3:4], col[:, 3:4], -SCALE, None, ALU.mult).then_inc(S("s_sb"), 1)
                    dve.wait_ge(S("s_wT"), p1 + 1)
                    v.tensor_copy(a5["PTw"], ps[6])
                    v.tensor_copy(PTn[:, 1, :], ps[7][0:TS, P:2 * P]).then_inc(S("s_ptw"), 1)
                    p4 = it * 8 + 4 * x
                    for f in range(4):
                        dve.wait_ge(S("s_sT"), p4 + (f + 1))
                        last = v.tensor_copy(PT[:, 4 * f:4 * f + 4, :].rearrange("p j r -> p (j r)"), ps[f])
                        if f == 3:
                            last = v.tensor_copy(PTn[:, 0, :], ps[5][0:TS, 0:P])
                        last.then_inc(S("s_pt"), 1)
                    slink(v.tensor_tensor(col[:, 4:5], col[:, 6:7], col[:, 7:8], ALU.add))
                    slink(v.reciprocal(col[:, 8:10], col[:, 4:6]))
                    dve.wait_ge(S("s_pv"), p1 + 1)
                    dve.wait_ge(S("s_sto"), p1 * 16 + 16)
                    for q in range(4):
                        r, c0 = slice(32 * q, 32 * q + 32), 64 * q
                        v.tensor_scalar(orow[r, 0, :], ps[0][r, c0:c0 + HD], col[r, 8:9], None, ALU.mult)
                        v.tensor_scalar(orow[r, 1, :], ps[6][r, c0:c0 + HD], col[r, 9:10], None, ALU.mult)
                        last = v.tensor_copy(orow[r, 2, :], ps[6][r, 256 + HD * (q % 2):256 + HD * (q % 2) + HD])
                    last.then_inc(S("s_out"), 1)
                    assert s_links[0] == PL
            links[0] += 4 * PL
            dve.wait_ge(S("s_pv"), 4)
            v.memset(qst, 0.0)
            dve.wait_ge(S("cmp_pe"), 1)
            dve.wait_ge(S("p_pool"), 2)
            pcv = Pc.rearrange("p (i h n) -> p i h n", i=4, n=16)
            pcu = Pc.rearrange("p (u n) -> p u n", n=16)
            for h in range(KVH):
                last = v.tensor_tensor(pcv[:, :, GRP * h:GRP * (h + 1), :],
                                       ps[h][:, 0:256].rearrange("p (i g n) -> p i g n", i=4, n=16),
                                       cmk.unsqueeze(2).to_broadcast([P, 4, GRP, 16]), ALU.add)
            link(last)
            link(v.tensor_reduce(cm[:, 0, :], pcu, AX.X, ALU.max))
            v.tensor_tensor(pcu, pcu, cm[:, 0, :].unsqueeze(2).to_broadcast([P, 32, 16]), ALU.subtract).then_inc(S("cmp_dve"), 1)
            dve.wait_ge(S("p_cexp"), 1)
            link(v.tensor_reduce(cm[:, 0, :], pcu, AX.X, ALU.add))
            link(v.reciprocal(cm[:, 1, :], cm[:, 0, :]))
            link(v.tensor_scalar(cm[:, 1, 0:HEADS], cm[:, 1, 0:HEADS], small[:, 4:5], None, ALU.mult))
            v.tensor_tensor(pcu, pcu, cm[:, 1, :].unsqueeze(2).to_broadcast([P, 32, 16]), ALU.mult).then_inc(S("cmp_dve"), 1)
            dve.wait_ge(S("cmp_pe"), 2)
            v.tensor_copy(b6["PcT"], ps[1]).then_inc(S("cmp_dve"), 1)
            dve.wait_ge(S("cmp_pe"), 3)
            gv = gsig[:, :, :].rearrange("p i (h w) -> p i h w", w=3)
            for i in range(4):
                last = v.tensor_tensor(oatt[:, i, :].rearrange("p (h d) -> p h d", h=HEADS),
                                       ps[2 + i].rearrange("p (h d) -> p h d", h=HEADS),
                                       gv[:, i, :, 0:1].to_broadcast([P, HEADS, HD]), ALU.mult)
            last.then_inc(S("cmp_dve"), 1)
            dve.wait_ge(S("cmp_dve"), 4)
            dve.sem_inc(S("p_fin"), 2)
            g4 = gsig[:, 0:4, :].rearrange("p i (h g w) -> p i h g w", h=KVH, g=GRP)
            o4 = oatt[:, 0:4, :].rearrange("p i (h g d) -> p i h g d", h=KVH, g=GRP)
            done = [0]

            def stage_queries(q):
                for h in range(KVH):
                    r = slice(64 * h, 64 * h + 64)
                    last = v.tensor_copy(qst[r, h:h + 1, :], qT[r, bass.ds(q, 1), 0:SEQ])
                last.then_inc(S("p_stage"), 1)

            def stage_gates(q, glink):
                for h in range(KVH):
                    for i in range(4):
                        last = v.tensor_copy(gst[:, i, h, :].unsqueeze(1), g4[:, i, h, bass.ds(q, 1), 1:3])
                glink(last)

            def max_unit(g, s, glink):
                i = UNITS[s % 8][0]
                both = banks[:, 2 * (s % 2):2 * (s % 2) + 2, :]
                dve.wait_ge(S("p_sc"), g * 8 + (s + 1))
                dg = both[:, :, i * P:(i + 1) * P]
                glink(v.tensor_tensor(dg, dg, causal[:, :].unsqueeze(1).to_broadcast([P, 2, P]), ALU.add))
                glink(v.tensor_reduce(cst[:, s % 2, 0, :], both[:, :, 0:(i + 1) * P], AX.X, ALU.max))
                v.tensor_scalar(cst[:, s % 2, 1, :], cst[:, s % 2, 0, :], -SCALE, None, ALU.mult).then_inc(S("p_max"), 1)

            def turned_unit(g, s, glink):
                i, h = UNITS[s % 8]
                dve.wait_ge(S("p_exp"), g * 8 + (s + 3))
                dve.wait_ge(S("p_fin"), g * 8 + (s + 1))
                glink(v.reciprocal(cst[:, s % 2, 3, :], cst[:, s % 2, 2, :]))
                glink(v.tensor_tensor(cst[:, s % 2, 3, :], cst[:, s % 2, 3, :], gst[:, i, h, :], ALU.mult))

            def scale_unit(g, s):
                i, h = UNITS[s % 8]
                dve.wait_ge(S("p_pv"), g * 8 + (s + 3))
                dve.wait_ge(S("p_added"), g * 8 + (s + 1))
                v.tensor_tensor(tmp[:, s % 2, :, :], ps[6 + s % 2][:, 0:2 * HD].rearrange("p (w d) -> p w d", w=2),
                                gfac(s % 2), ALU.mult).then_inc(S("p_fin"), 1)

            def unit_dve(g, s, glink, more=True):
                if s < 8:
                    max_unit(g, s, glink)
                if s == 8 and more:
                    dve.wait_ge(S("p_sc"), g * 8 + 8)
                    stage_queries(g + 1)
                if s < 9 or more:
                    turned_unit(g, s - 1, glink)
                if s == 8 and more:
                    stage_gates(g + 1, glink)
                if s >= 2:
                    scale_unit(g, s - 2)
                if s >= 8 and more:
                    max_unit(g, s, glink)

            stage_queries(0)
            stage_gates(0, link)
            max_unit(0, 0, link)
            unit_dve(0, 1, link)
            GL = 8 * 4 + 1
            with dve.Fori(0, GRP - 1) as g:

                def glink(ins):
                    done[0] += 1
                    ins.then_inc(S("v_link"), 1)
                    dve.wait_ge(S("v_link"), g * GL + (links[0] + done[0]))

                for s in range(2, 10):
                    unit_dve(g, s, glink)
                assert done[0] == GL, done[0]
            links[0] += (GRP - 1) * GL
            for s in range(2, 10):
                unit_dve(GRP - 1, s, link, more=False)
            dve.wait_ge(S("p_added"), 2 + 32)
            dve.wait_ge(S("o_act"), 2)
            link(v.reciprocal(nss[:, 8:13], nss[:, 8:13]))
            for i in range(NTILE):
                rows = TROWS[i]
                last = v.tensor_scalar(oatt[0:rows, i, :], oatt[0:rows, i, :], nss[0:rows, 8 + i:9 + i], None, ALU.mult)
            last.then_inc(S("o_dve"), 1)
            for f in range(4):
                dve.wait_ge(S("o_turned"), f + 1)
                gn = vcol[:, V_GNSA + f:V_GNSA + f + 1]
                v.tensor_scalar(xnT[:, 4 + f, 0:SEQ], ps[f], gn, None, ALU.mult)
                v.tensor_scalar(xnT[:, 4 + f, SEQ:T], ps[4 + f][:, 0:NSMP], gn, None, ALU.mult).then_inc(S("o_mix"), 1)
            for k in range(4, KD):
                dve.wait_ge(S("o_mix"), 4)
                dve.wait_ge(S("wo_hi"), 8 + k + 1)
                v.tensor_tensor(mlo[k], xnT[:, k, :], mhi[k].bitcast(F32), ALU.subtract).then_inc(S("o_mix"), 1)
            def split_up_dve(slot, n2):
                for w in range(2):
                    dve.wait_ge(S("u_hi"), n2 + (w + 1))
                    half = ring[:, slot, 2048 * w:2048 * (w + 1)]
                    v.tensor_tensor(ring_r[:, slot, 2048 * w:2048 * (w + 1)], half, whi[slot][:, 2048 * w:2048 * (w + 1)].bitcast(F32),
                                    ALU.subtract).then_inc(S("u_lo"), 1)

            for m in range(KD):
                if m == 6:
                    split_up_dve(0, 0)
                dve.wait_ge(S("h_mm"), m + 1)
                v.tensor_tensor(xT[:, m, 0:UA], xT[:, m, 0:UA], ps[m % 2][:, 0:UA], ALU.add)
                v.tensor_tensor(xT[:, m, UA:T], xT[:, m, UA:T], ps[2 + m % 2][:, 0:UB], ALU.add).then_inc(S("h_done"), 1)
            dve.wait_ge(S("h_done"), KD)
            dve.sem_inc(S("u_fc"), 1)
            dve.sem_inc(S("u_pad"), 2)
            norm_dve(dve, xT, V_GFFN)
            dve.wait_ge(S("xn_lo"), KD)
            v.memset(pad[:, :, :, 0:2], 0.0)
            v.memset(ssy[:], 1.0)
            dve.sem_inc(S("u_conv"), 2)
            UL = 4

            def up_dve(par, qn, split, before_conv=lambda: None):
                n = [0]

                def ulink(ins):
                    n[0] += 1
                    ins.then_inc(S("v_link"), 1)
                    dve.wait_ge(S("v_link"), qn * UL + (links[0] + n[0]))

                dve.wait_ge(S("u_ft"), qn + 1)
                v.tensor_copy(fcol[:, par, :, :], ps[6][:, 0:64].rearrange("p (w n) -> p w n", w=2)[:, :, 0:19]).then_inc(S("u_fc"), 1)
                dve.wait_ge(S("u_fc"), qn + 2)
                dve.wait_ge(S("u_conv"), qn + 1)
                for w in range(2):
                    pv = pad[:, par, w, 2 + SEQ:FPW].rearrange("p (b t) -> p b t", b=NB)
                    last = v.tensor_copy(pv[:, :, 0:2], fcol[:, par, w, 0:16].rearrange("p (b j) -> p b j", b=NB))
                last.then_inc(S("u_smp"), 1)
                dve.wait_ge(S("u_smp"), qn + 1)
                dve.wait_ge(S("u_pad"), qn + 3)
                dve.wait_ge(S("u_lT"), qn + 1)
                v.tensor_copy(l18[:, :, 0:2], pad[:, par, :, SEQ:SEQ + 2])
                for w in range(2):
                    pv = pad[:, par, w, 2 + SEQ:FPW].rearrange("p (b t) -> p b t", b=NB)
                    last = v.tensor_copy(l18[:, w, 2:18].rearrange("p (b j) -> p b j", b=NB), pv[:, :, TS:TS + 2])
                last.then_inc(S("u_l18"), 1)
                split()
                dve.wait_ge(S("u_act"), qn + 1)
                taps = [fcol[:, par, w, 16 + j:17 + j] for w in range(2) for j in range(3)]
                for w, c in ((1, cg), (0, ca)):
                    ulink(v.tensor_scalar(c, pad[:, par, w, 0:FVW], taps[3 * w], None, ALU.mult))
                    ulink(v.scalar_tensor_tensor(out=c, in0=pad[:, par, w, 1:1 + FVW], scalar=taps[3 * w + 1], in1=c,
                                                 op0=ALU.mult, op1=ALU.add))
                    v.scalar_tensor_tensor(out=c, in0=pad[:, par, w, 2:2 + FVW], scalar=taps[3 * w + 2], in1=c,
                                           op0=ALU.mult, op1=ALU.add).then_inc(S("u_cg" if w else "u_conv"), 1)
                dve.wait_ge(S("u_conv"), qn + 3)
                dve.wait_ge(S("u_silu"), qn + 1)
                v.tensor_tensor(actT[:, bass.ds(qn, 1), 0:SEQ], cg[:, 0:SEQ].unsqueeze(1), ca[:, 0:SEQ].unsqueeze(1), ALU.mult)
                v.tensor_tensor(actT[:, bass.ds(qn, 1), SEQ:T].rearrange("p k (b t) -> p (k b) t", b=NB), ffn_sample(cg),
                                ffn_sample(ca), ALU.mult).then_inc(S("u_act"), 1)
                dve.wait_ge(S("u_lT"), qn + 2)
                dve.wait_ge(S("u_fof"), qn + 1)
                v.tensor_copy(a7["fo"][0:18, :], ps[7][0:18, 0:256]).then_inc(S("u_fo"), 1)

            dve.sem_inc(S("u_lT"), 1)
            dve.sem_inc(S("u_act"), 1)
            dve.sem_inc(S("u_fo"), 1)
            with dve.Fori(0, 5) as it:
                for q in range(4):
                    if q % 2 == 0:
                        up_dve(0, it * 4 + q, lambda: split_up_dve(1 - q // 2, it * 4 + (q + 2)))
                    else:
                        up_dve(1, it * 4 + q, lambda: None)

            def split_down_dve(s, mn):
                dve.wait_ge(S("d_hi"), mn + 1)
                for k0, n, where in dhi_runs[s]:
                    last = v.tensor_tensor(dlo[s][:, k0:k0 + n, :].rearrange("p k n -> p (k n)"),
                                           draw[s][:, k0:k0 + n, :].rearrange("p k n -> p (k n)"), where.bitcast(F32),
                                           ALU.subtract)
                last.then_inc(S("d_lo"), 1)

            def act_lo(k):
                dve.wait_ge(S("a_hi"), k + 1)
                v.tensor_tensor(alo[k], actT[:, k, :], ahi[k].bitcast(F32), ALU.subtract).then_inc(S("a_lo"), 1)

            up_dve(0, 20, lambda: split_down_dve(0, 0))
            up_dve(1, 21, lambda: [act_lo(k) for k in range(12)])
            for k in range(12, NFF):
                act_lo(k)
            def down_dve(s, mn, split, turned):
                if split:
                    split_down_dve(1 - s, mn + 1)
                dve.wait_ge(S("d_mm"), mn + 1)
                dve.wait_ge(S("d_out"), mn + 1)
                x = xT[:, bass.ds(mn, 1), :]
                v.tensor_tensor(hst[:, s:s + 1, 0:UA], x[:, :, 0:UA], ps[s][:, 0:UA].unsqueeze(1), ALU.add)
                v.tensor_tensor(hst[:, s:s + 1, UA:T], x[:, :, UA:T], ps[2 + s][:, 0:UB].unsqueeze(1),
                                ALU.add).then_inc(S("d_add"), 1)
                if turned:
                    token_rows(1 - s, mn)

            def token_rows(s, mn):
                dve.wait_ge(S("d_sq"), mn + 1)
                dve.wait_ge(S("d_turned"), mn)
                g = gB[:, bass.ds((mn + (-1)) * P, P)]
                v.tensor_tensor(ytok[:, 0:4, bass.ds((mn + (-1)) * P, P)], ps[4 + s].rearrange("p (i n) -> p i n", i=4),
                                g.unsqueeze(1).to_broadcast([P, 4, P]), ALU.mult)
                v.tensor_tensor(ytok[0:NSMP, 4, bass.ds((mn + (-1)) * P, P)], ps[6 + s][0:NSMP, 0:P], g[0:NSMP, :],
                                ALU.mult).then_inc(S("d_out"), 1)

            dve.sem_inc(S("d_add"), 2)
            dve.sem_inc(S("d_out"), 2)
            down_dve(0, 0, True, False)
            dve.wait_ge(S("u_fof"), 1 + NFF)
            dve.wait_ge(S("vec_in"), 15 * 16)
            with dve.Fori(0, 3) as it:
                for x in range(2):
                    down_dve((1 + x) % 2, it * 2 + (1 + x), True, True)
            down_dve(1, 7, False, True)
            token_rows(1, 8)
            dve.wait_ge(S("d_out"), KD + 2)
            v.tensor_reduce(yrt, ssy[:, :, :], AX.X, ALU.add).then_inc(S("y_sum"), 1)
            dve.wait_ge(S("y_root"), 1)
            v.reciprocal(yrt, yrt).then_inc(S("y_sum"), 1)
            dve.wait_ge(S("y_sum"), 2)
            for i in range(1, NTILE, 2):
                v.tensor_scalar(ytok[:, i, :], ytok[:, i, :], yrt[:, i:i + 1], None, ALU.mult).then_inc(S("y_dve"), 1)

        @block.sync
        def _(sp):
            for i in range(4):
                sp.dma_start(xtok[:, i, :], A["x_prompt"][0, i * P:(i + 1) * P, :]).then_inc(S("x_in"), 16)
            sp.dma_start(xtok[0:NSMP, 4, :], A["x_sample"].rearrange("b t f -> (b t) f")).then_inc(S("x_in"), 16)
            sp.dma_start(vrows[V_GMIX:V_GMIX + 8, :], A["g_mix"][0].rearrange("(k p) -> k p", p=P)).then_inc(S("vec_in"), 16)
            sp.dma_start(vrows[V_GFFN:V_GFFN + 8, :], A["g_ffn"][0].rearrange("(k p) -> k p", p=P)).then_inc(S("vec_in"), 16)
            sp.dma_start(vrows[V_GNSA:V_GNSA + 4, :], A["g_nsa"][0].rearrange("(k p) -> k p", p=P)).then_inc(S("vec_in"), 16)
            sp.dma_start(vrows[V_SKIP:V_SKIP + 4, :], A["m_skip"][0].rearrange("(k p) -> k p", p=P)).then_inc(S("vec_in"), 16)
            sp.dma_start(vrows[V_GHEAD:V_GHEAD + 4, :], A["g_mhead"][0]).then_inc(S("vec_in"), 16)
            sp.dma_start(vrows[V_BCONV:V_BCONV + 4, :], A["b_mconv"][0].rearrange("(k p) -> k p", p=P)).then_inc(S("vec_in"), 16)
            sp.dma_start(vrows[V_WCONV:V_WCONV + 16, :], A["w_mconv"][0].rearrange("j (k p) -> (j k) p", p=P)).then_inc(S("vec_in"), 16)
            sp.dma_start(vrows[V_PE:V_PE + 32, :], A["pe_cmp"][0].rearrange("k (c two) d -> (k c) (two d)", two=2)).then_inc(S("vec_in"), 16)
            sp.dma_start(vrows[V_GFIN:V_GFIN + 8, :], A["g_final"].rearrange("(k p) -> k p", p=P)).then_inc(S("vec_in"), 16)
            sp.dma_start(mcs[0:24, :], A["state_mlstm_conv"][0].rearrange("b j f -> (b j) f")).then_inc(S("vec_in"), 16)
            sp.dma_start(nrows[0:32, :], A["state_mlstm_n"][0].rearrange("b h d -> (b h) d")).then_inc(S("vec_in"), 16)
            sp.dma_start(gb[:, 0:1], A["b_ig"].rearrange("a h -> h a"), allow_slow_non_contiguous=True).then_inc(S("vec_in"), 16)
            sp.dma_start(gb[:, 1:2], A["b_fg"].rearrange("a h -> h a"), allow_slow_non_contiguous=True).then_inc(S("vec_in"), 16)
            sp.dma_start(m0[:, :], A["state_mlstm_m"][0].rearrange("b h -> h b"), allow_slow_non_contiguous=True).then_inc(S("vec_in"), 16)

            def slab(n):
                c0, w = SLABS[n]
                if n == 0:
                    dq = ring[:, 0, :].rearrange("p (k g h d) -> p k g h d", k=KD, g=GRP, h=KVH)
                    for h in range(KVH):
                        for g in range(GRP):
                            at = (h * GRP + g) * HD
                            sp.dma_start(dq[:, :, g, h, :], w_in[:, :, at:at + HD]).then_inc(S("q_in"), 16)
                    return
                dst = ring[:, n % 2, :].rearrange("p (k n) -> p k n", k=KD)[:, :, 0:w]
                sp.dma_start(dst, w_in[:, :, c0:c0 + w]).then_inc(S(f"slab_in{n % 2}"), 16)

            slab(0)
            slab(1)
            sp.wait_ge(S("filled"), 1)
            sp.dma_start(wg[:, :, 0:MH], w_in[:, :, 2840:2844]).then_inc(S("wg_in"), 16)
            sp.dma_start(wg[:, :, 32:32 + MH], w_in[:, :, 2844:2848]).then_inc(S("wg_in"), 16)
            sp.wait_ge(S("setup_dve"), 2)
            for k in range(2):
                sp.dma_start(w1c[:, k, :, :], A["w_cmp1"][0, k].rearrange("(c p) n -> p c n", p=P)).then_inc(S("w1_in"), 16)
                sp.dma_start(w2c[:, k, :], A["w_cmp2"][0, k]).then_inc(S("w1_in"), 16)
            for n in range(2, 6):
                sp.wait_ge(S("job"), slab_last[n - 2] + 1)
                slab(n)
            for w, name in enumerate(("w_mq", "w_mk")):
                sp.dma_start(wqk[:, w, :, :], A[name][0].rearrange("h d e -> d h e")).then_inc(S("wqk_in"), 16)
            sp.wait_ge(S("c_kc"), 4 + 2 * 9)
            for b in range(NB):
                sp.dma_start(vnew[:, b, :, :],
                             kv[b * TS:(b + 1) * TS, 4, 256:768].rearrange("t (w k f) -> t w k f", w=2, k=2)[:, :, 1, :])\
                    .then_inc(S("m_cin"), 16)
            sp.dma_start(nbh.rearrange("b (h d) -> b h d", h=MH), A["state_mlstm_n"][0]).then_inc(S("wqk_in"), 16)
            for h in range(MH):
                if h:
                    sp.wait_ge(S("m_cout"), 16 * h)
                sp.dma_start(Cst[:, :, :], A["state_mlstm_C"][0, :, h].rearrange("b e d -> e b d")).then_inc(S("m_cin"), 16)
            sp.wait_ge(S("m_mix"), MH)

            def window(p):
                for b2 in range(2):
                    b = 2 * p + b2
                    sp.dma_start(wkv[:, 2 * (p % 2) + b2, :],
                                 A["state_win"][0, b].rearrange("(p j) k h d -> p (j k h d)", p=P)).then_inc(S(f"win_in{p % 2}"), 16)

            window(0)
            window(1)
            sp.wait_ge(S("kv_dve"), 1)
            for hd in range(HEADS):
                sp.dma_start(Vbd[hd * 16:hd * 16 + 16, hd * HD:(hd + 1) * HD],
                             vc_p[:, (hd // GRP) * HD:(hd // GRP + 1) * HD]).then_inc(S("vbd_in"), 16)
            sp.sem_inc(S("s_sto"), 16)
            for p in range(4):
                sp.wait_ge(S("s_out"), p + 2)
                sp.dma_start(osc[:, p * P:(p + 1) * P, :].rearrange("w r d -> r w d"), orow).then_inc(S("s_sto"), 16)
                if p < 2:
                    window(p + 2)
            sp.dma_start(ring[:, 0, :].rearrange("p (k n) -> p k n", k=KD),
                         A["w_out"][0].rearrange("(k p) n -> p k n", p=P)[:, :, 0:512]).then_inc(S("slab_in0"), 16)
            sp.dma_start(ring[:, 1, :].rearrange("p (k n) -> p k n", k=KD),
                         A["w_out"][0].rearrange("(k p) n -> p k n", p=P)[:, :, 512:D]).then_inc(S("slab_in1"), 16)
            sp.wait_ge(S("s_sto"), 5 * 16)
            for b in range(NB):
                for w in range(3):
                    sp.dma_start(osm[b * TS:(b + 1) * TS, w, :].rearrange("t (h d) -> t h d", h=HEADS),
                                 osc[w, b * 64:(b + 1) * 64, :].rearrange("(h t) d -> t h d", h=HEADS)).then_inc(S("s_sto"), 16)
            w_up = A["w_up"][0].rearrange("(k p) (w n) -> p w k n", p=P, w=2)
            w_dn = A["w_down"][0].rearrange("(k p) n -> p k n", p=P)
            f_st = A["state_ffn_conv"][0].rearrange("b j (w n) -> (b j) w n", w=2)
            f_wt = A["w_fconv"][0].rearrange("j (w n) -> j w n", w=2)

            def up_slab(n):
                s = n % 2
                dst = ring[:, s, :].rearrange("p (w k n) -> p w k n", w=2, k=KD)
                for w in range(2):
                    sp.dma_start(dst[:, w], w_up[:, w, :, n * 256:(n + 1) * 256]).then_inc(S(f"slab_in{s}"), 16)
                sp.dma_start(fin[0:16, s, :, :], f_st[:, :, n * 256:(n + 1) * 256]).then_inc(S(f"slab_in{s}"), 16)
                sp.dma_start(fin[16:19, s, :, :], f_wt[:, :, n * 256:(n + 1) * 256]).then_inc(S(f"slab_in{s}"), 16)

            sp.wait_ge(S("o_dve"), 1)
            for n in range(2):
                sp.wait_ge(S("h_mm"), 4 * (n + 1))
                up_slab(n)
            for n in range(2, 11):
                sp.wait_ge(S("u_mm"), 2 * (n - 1))
                up_slab(n)
            def down_tile(m):
                sp.dma_start(draw[m % 2], w_dn[:, :, m * P:(m + 1) * P]).then_inc(S(f"dn_in{m % 2}"), 16)

            sp.wait_ge(S("u_mm"), 20)
            down_tile(0)
            sp.dma_start(gB, bass.AP(A["g_final"].tensor, A["g_final"].offset, [[0, P], [1, D]])).then_inc(S("vec_in"), 16)
            sp.wait_ge(S("u_mm"), 22)
            down_tile(1)
            for m in range(2, KD):
                sp.wait_ge(S("d_mm"), m - 1)
                down_tile(m)
            for i in range(NTILE):
                sp.wait_ge(S("y_dve" if i % 2 else "y_act"), i // 2 + 1)
                dst = O["y_p"][0, i * P:(i + 1) * P, :] if i < 4 else O["y_s"].rearrange("b t f -> (b t) f")
                sp.dma_start(dst, ytok[0:TROWS[i], i, :]).then_inc(S("y_stored"), 16)
            sp.wait_ge(S("y_stored"), NTILE * 16)
            sp.wait_ge(S("stored"), outs[0])



_INS = ['x_prompt', 'x_sample', 'cache_cmp', 'cache_sel', 'state_win', 'state_mlstm_C', 'state_mlstm_n',
        'state_mlstm_m', 'state_mlstm_conv', 'state_ffn_conv', 'page_table',
        'g_mix', 'w_in', 'w_out', 'w_mconv', 'b_mconv', 'w_mq', 'w_mk', 'b_ig', 'b_fg', 'g_mhead', 'm_skip',
        'pe_cmp', 'w_cmp1', 'w_cmp2', 'g_nsa', 'g_ffn', 'w_up', 'w_fconv', 'w_down', 'g_final']
_OUTS = [('y_p', (1, 512, 1024)), ('y_s', (8, 8, 1024)),
         ('cmp_p', (1, 1, 512, 2, 2, 64)), ('cmp_s', (1, 8, 8, 2, 2, 64)),
         ('sel_p', (1, 1, 512, 2, 2, 64)), ('sel_s', (1, 8, 8, 2, 2, 64)),
         ('win_p', (1, 1, 512, 2, 2, 64)), ('win_s', (1, 8, 512, 2, 2, 64)),
         ('C_p', (1, 1, 4, 128, 128)), ('C_s', (1, 8, 4, 128, 128)),
         ('n_p', (1, 1, 4, 128)), ('n_s', (1, 8, 4, 128)),
         ('m_p', (1, 1, 4)), ('m_s', (1, 8, 4)),
         ('mconv_p', (1, 1, 3, 512)), ('mconv_s', (1, 8, 3, 512)),
         ('fconv_p', (1, 1, 2, 5632)), ('fconv_s', (1, 8, 2, 5632))]


def kernel(**inputs):
    import numpy as _np
    import concourse.bacc as _bacc
    from concourse import mybir as _mybir
    from concourse.bass_utils import run_bass_kernel_spmd as _run

    nc = _bacc.Bacc("TRN2", target_bir_lowering=False, num_devices=1)
    arrays, ins, outs = {}, {}, {}
    for name in _INS:
        a = _np.ascontiguousarray(inputs[name])
        arrays[f"in_{name}_dram"] = a
        ins[name] = nc.dram_tensor(f"in_{name}_dram", a.shape, _mybir.dt.from_np(a.dtype), kind="ExternalInput").ap()
    for name, shape in _OUTS:
        outs[name] = nc.dram_tensor(f"out_{name}_dram", shape, _mybir.dt.float32, kind="ExternalOutput").ap()
    hybrid_decoder_layer(nc, ins, outs)
    r = _run(nc, [arrays], core_ids=[0])
    return tuple(r.results[0][f"out_{name}_dram"] for name, _ in _OUTS)
```
